# Optimizing a Trainium2 kernel written in Bass

```python
import jax, jax.numpy as jnp
from jax import lax
import numpy as np

D_MODEL = 2048
BATCH = 1
SEQ = 256
DEPTH = 1

CHUNK = 64
GMLP_WIDTH = D_MODEL // 2
RWKV_WIDTH = D_MODEL - GMLP_WIDTH
GMLP_BLOCK = 128
GMLP_HEADS = 8
GMLP_HEAD_DIM = GMLP_WIDTH // GMLP_HEADS
RWKV_HEAD_DIM = 64
RWKV_HEADS = RWKV_WIDTH // RWKV_HEAD_DIM
DECAY_LORA = 64
AAA_LORA = 64
GATE_LORA = 160
RWKV_IN = 3 * RWKV_WIDTH + DECAY_LORA + AAA_LORA + GATE_LORA
IN_WIDTH = 2 * GMLP_WIDTH + RWKV_IN
PEER_KEYS = 128
PEER_EXPERTS = PEER_KEYS * PEER_KEYS
PEER_HEADS = 8
PEER_TOPK = 16
PEER_QK_HALF = 128
PEER_TOKEN_BLOCK = 128
N_MOD = 6
NORM_EPS = 1e-6
LN_EPS = 1e-5
GROUPNORM_EPS = 64e-5

kernel_name = "hybrid_gmlp_rwkv7_peer_adaln_block"

def rms_norm(x, g):
    xf = x.astype(jnp.float32)
    y = xf * lax.rsqrt(jnp.mean(xf * xf, axis=-1, keepdims=True) + NORM_EPS)
    return (y * g.astype(jnp.float32)).astype(x.dtype)

def layer_norm(x, g, b, eps):
    xf = x.astype(jnp.float32)
    mu = jnp.mean(xf, axis=-1, keepdims=True)
    var = jnp.mean(jnp.square(xf - mu), axis=-1, keepdims=True)
    y = (xf - mu) * lax.rsqrt(var + eps)
    return (y * g.astype(jnp.float32) + b.astype(jnp.float32)).astype(x.dtype)

def modulate(h, shift, scale):
    return h * (1 + scale[:, None, :]) + shift[:, None, :]

def gmlp_spatial_gate(u, v, v_g, v_b, w_s, b_s):
    bsz, seq, _ = u.shape
    vn = layer_norm(v, v_g, v_b, LN_EPS)
    chunk_id = jnp.arange(GMLP_BLOCK) // CHUNK
    mask = (chunk_id[None, :] <= chunk_id[:, None]).astype(w_s.dtype)
    vb = vn.reshape(bsz, seq // GMLP_BLOCK, GMLP_BLOCK, GMLP_HEADS, GMLP_HEAD_DIM)
    z = jnp.einsum("hij,bnjhd->bnihd", w_s * mask, vb) + b_s.T[None, None, :, :, None]
    return u * z.reshape(bsz, seq, GMLP_WIDTH)

def token_shift(p):
    return jnp.pad(p, ((0, 0), (1, 0), (0, 0)))[:, :-1]

def wkv7_scan(r, decay, k, v, a_vec, b_vec):
    bsz, _, nh, n = r.shape
    xs = tuple(jnp.moveaxis(t, 1, 0) for t in (r, decay, k, v, a_vec, b_vec))

    def step(state, inp):
        r_t, w_t, k_t, v_t, a_t, b_t = inp
        sa = jnp.einsum("bhvk,bhk->bhv", state, a_t)
        state = (state * w_t[:, :, None, :]
                 + sa[..., None] * b_t[:, :, None, :]
                 + v_t[..., None] * k_t[:, :, None, :])
        y_t = jnp.einsum("bhvk,bhk->bhv", state, r_t)
        return state, y_t

    s0 = jnp.zeros((bsz, nh, n, n), jnp.float32)
    _, ys = lax.scan(step, s0, xs)
    return jnp.moveaxis(ys, 0, 1)

def rwkv7_time_mix(p, mu, w0, w2, a0, a2, g2, k_k, k_a, r_k, ln_g, ln_b):
    bsz, seq, _ = p.shape
    f32 = jnp.float32
    p = p + (token_shift(p) - p) * mu
    cuts = [RWKV_WIDTH, 2 * RWKV_WIDTH, 3 * RWKV_WIDTH,
            3 * RWKV_WIDTH + DECAY_LORA, 3 * RWKV_WIDTH + DECAY_LORA + AAA_LORA]
    r, k, v, wl, al, gl = jnp.split(p, cuts, axis=-1)
    w = -jax.nn.softplus(-(w0 + jnp.tanh(wl) @ w2)) - 0.5
    a = jax.nn.sigmoid(a0 + al @ a2)
    g = jax.nn.sigmoid(gl) @ g2

    def heads(t):
        return t.reshape(bsz, seq, RWKV_HEADS, RWKV_HEAD_DIM).astype(f32)

    kk = heads(k * k_k)
    kk = kk / jnp.maximum(jnp.sqrt(jnp.sum(kk * kk, axis=-1, keepdims=True)), 1e-12)
    k = k * (1 + (a - 1) * k_a)
    rh, kh, vh, ah = heads(r), heads(k), heads(v), heads(a)
    decay = jnp.exp(-jnp.exp(heads(w)))
    y = wkv7_scan(rh, decay, kh, vh, -kk, kk * ah)
    y = layer_norm(y, ln_g.reshape(RWKV_HEADS, RWKV_HEAD_DIM),
                   ln_b.reshape(RWKV_HEADS, RWKV_HEAD_DIM), GROUPNORM_EPS)
    bonus = jnp.sum(rh * kh * r_k.astype(f32), axis=-1, keepdims=True) * vh
    return (y + bonus).reshape(bsz, seq, RWKV_WIDTH).astype(p.dtype) * g

def peer_ffn(h, w_q, sub_keys, expert_u, expert_v):
    bsz, seq, d = h.shape
    f32 = jnp.float32
    q = (h @ w_q).reshape(bsz, seq, PEER_HEADS, 2, PEER_QK_HALF).astype(f32)
    scores = jnp.einsum("bshpd,hpnd->bshpn", q, sub_keys.astype(f32))
    s_top, i_top = lax.top_k(scores, PEER_TOPK)
    cand = s_top[..., 0, :, None] + s_top[..., 1, None, :]
    cand_idx = i_top[..., 0, :, None] * PEER_KEYS + i_top[..., 1, None, :]
    cand = cand.reshape(bsz, seq, PEER_HEADS, PEER_TOPK * PEER_TOPK)
    cand_idx = cand_idx.reshape(bsz, seq, PEER_HEADS, PEER_TOPK * PEER_TOPK)
    s_fin, pos = lax.top_k(cand, PEER_TOPK)
    e_idx = jnp.take_along_axis(cand_idx, pos, axis=-1)
    gate = jax.nn.softmax(s_fin, axis=-1).astype(h.dtype)

    n_sel = PEER_HEADS * PEER_TOPK
    n_blocks = (bsz * seq) // PEER_TOKEN_BLOCK
    hb = h.reshape(n_blocks, PEER_TOKEN_BLOCK, d)
    eb = e_idx.reshape(n_blocks, PEER_TOKEN_BLOCK, n_sel)
    gb = gate.reshape(n_blocks, PEER_TOKEN_BLOCK, n_sel)

    def block(args):
        hx, ei, gi = args
        u_sel = expert_u[ei]
        act = jax.nn.gelu(jnp.einsum("tkd,td->tk", u_sel, hx), approximate=False) * gi
        return jnp.einsum("tk,tkd->td", act, expert_v[ei])

    out = lax.map(block, (hb, eb, gb))
    return out.reshape(bsz, seq, d)

def setup_inputs(seed: int = 0) -> dict:
    key = jax.random.key(seed)
    ks = jax.random.split(key, 32)
    f32 = jnp.float32
    L, D = DEPTH, D_MODEL

    def nrm(k, shape, std):
        return jax.random.normal(k, shape, f32) * std

    def gain(k, shape):
        return 1.0 + nrm(k, shape, 0.02)

    return {
        "x": nrm(ks[0], (BATCH, SEQ, D), 1.0),
        "c": nrm(ks[1], (BATCH, D), 1.0),
        "ada_w": nrm(ks[2], (L, D, N_MOD * D), 0.5 * D ** -0.5),
        "ada_b": nrm(ks[3], (L, N_MOD * D), 0.01),
        "norm1_g": gain(ks[4], (L, D)),
        "w_in": nrm(ks[5], (L, D, IN_WIDTH), D ** -0.5),
        "gmlp_v_g": gain(ks[6], (L, GMLP_WIDTH)),
        "gmlp_v_b": nrm(ks[7], (L, GMLP_WIDTH), 0.02),
        "gmlp_ws": nrm(ks[8], (L, GMLP_HEADS, GMLP_BLOCK, GMLP_BLOCK), GMLP_BLOCK ** -0.5),
        "gmlp_bs": gain(ks[9], (L, GMLP_HEADS, GMLP_BLOCK)),
        "gmlp_out_g": gain(ks[10], (L, GMLP_WIDTH)),
        "rwkv_mu": jax.random.uniform(ks[11], (L, RWKV_IN), f32),
        "rwkv_w0": jax.random.uniform(ks[12], (L, RWKV_WIDTH), f32, -6.5, -1.5),
        "rwkv_w2": nrm(ks[13], (L, DECAY_LORA, RWKV_WIDTH), 0.1 * DECAY_LORA ** -0.5),
        "rwkv_a0": nrm(ks[14], (L, RWKV_WIDTH), 0.1),
        "rwkv_a2": nrm(ks[15], (L, AAA_LORA, RWKV_WIDTH), 0.1 * AAA_LORA ** -0.5),
        "rwkv_g2": nrm(ks[16], (L, GATE_LORA, RWKV_WIDTH), GATE_LORA ** -0.5),
        "rwkv_kk": 0.85 + nrm(ks[17], (L, RWKV_WIDTH), 0.02),
        "rwkv_ka": gain(ks[18], (L, RWKV_WIDTH)),
        "rwkv_rk": nrm(ks[19], (L, RWKV_HEADS, RWKV_HEAD_DIM), 0.1),
        "rwkv_ln_g": gain(ks[20], (L, RWKV_WIDTH)),
        "rwkv_ln_b": nrm(ks[21], (L, RWKV_WIDTH), 0.02),
        "w_out": nrm(ks[22], (L, D, D), D ** -0.5),
        "norm2_g": gain(ks[23], (L, D)),
        "peer_wq": nrm(ks[24], (L, D, PEER_HEADS * 2 * PEER_QK_HALF), D ** -0.5),
        "peer_keys": nrm(ks[25], (L, PEER_HEADS, 2, PEER_KEYS, PEER_QK_HALF), PEER_QK_HALF ** -0.5),
        "peer_u": nrm(ks[26], (L, PEER_EXPERTS, D), D ** -0.5),
        "peer_v": nrm(ks[27], (L, PEER_EXPERTS, D), PEER_HEADS ** -0.5),
        "final_g": gain(ks[28], (D,)),
    }

def reference(x, c, ada_w, ada_b, norm1_g, w_in, gmlp_v_g, gmlp_v_b, gmlp_ws, gmlp_bs,
              gmlp_out_g, rwkv_mu, rwkv_w0, rwkv_w2, rwkv_a0, rwkv_a2, rwkv_g2, rwkv_kk,
              rwkv_ka, rwkv_rk, rwkv_ln_g, rwkv_ln_b, w_out, norm2_g, peer_wq, peer_keys,
              peer_u, peer_v, final_g):
    for l in range(DEPTH):
        mod = jax.nn.silu(c) @ ada_w[l] + ada_b[l]
        sh1, sc1, gt1, sh2, sc2, gt2 = jnp.split(mod, N_MOD, axis=-1)

        h = modulate(rms_norm(x, norm1_g[l]), sh1, sc1)
        p = h @ w_in[l]
        u, v, p_rwkv = jnp.split(p, [GMLP_WIDTH, 2 * GMLP_WIDTH], axis=-1)
        y_a = gmlp_spatial_gate(jax.nn.gelu(u, approximate=False), jax.nn.gelu(v, approximate=False),
                                gmlp_v_g[l], gmlp_v_b[l], gmlp_ws[l], gmlp_bs[l])
        y_a = rms_norm(y_a, gmlp_out_g[l])
        y_b = rwkv7_time_mix(p_rwkv, rwkv_mu[l], rwkv_w0[l], rwkv_w2[l], rwkv_a0[l], rwkv_a2[l],
                             rwkv_g2[l], rwkv_kk[l], rwkv_ka[l], rwkv_rk[l], rwkv_ln_g[l], rwkv_ln_b[l])
        y = jnp.concatenate([y_a, y_b], axis=-1) @ w_out[l]
        x = x + gt1[:, None, :] * y

        h = modulate(rms_norm(x, norm2_g[l]), sh2, sc2)
        x = x + gt2[:, None, :] * peer_ffn(h, peer_wq[l], peer_keys[l], peer_u[l], peer_v[l])
    return rms_norm(x, final_g)


_drawn_inputs = setup_inputs


def setup_inputs(seed=0):
    import zlib

    import numpy as np

    out = dict(_drawn_inputs(seed))
    spreads = {}
    factors = {'ada_b': 4.62,
     'norm1_g': 7.049,
     'gmlp_v_g': 64.0,
     'gmlp_v_b': 64.0,
     'gmlp_bs': 64.0,
     'gmlp_out_g': 64.0,
     'rwkv_w2': 64.0,
     'rwkv_a0': 8.0,
     'rwkv_a2': 8.0,
     'rwkv_kk': 64.0,
     'rwkv_ka': 8.0,
     'rwkv_ln_g': 64.0,
     'rwkv_ln_b': 64.0,
     'norm2_g': 51.92,
     'final_g': 7.286,
     'gmlp_ws': 4.558,
     'rwkv_w0': 8.0,
     'peer_wq': 5.341,
     'peer_keys': 5.297,
     'peer_u': 6.256,
     'peer_v': 5.277}
    for name, (base, spread) in spreads.items():
        noise = np.random.default_rng([zlib.crc32(name.encode()), seed]).standard_normal(out[name].shape)
        drawn = base * np.exp(spread * noise) if base else spread * noise
        out[name] = __import__('jax').numpy.asarray(drawn.astype(out[name].dtype))
    for name, factor in factors.items():
        out[name] = (out[name] * factor).astype(out[name].dtype)
    return out
```

```python
from contextlib import ExitStack
import numpy as np
import concourse.bass as bass
from concourse import mybir

P = 128
D = 2048
SEQ = 256
NT = SEQ // P
KT = D // P
GW = 1024
RT = GW // P
HD = 64
RW_IN = 3360
NRT = 27
LORA0 = 3 * RT
IN_W = 2 * GW + RW_IN
GH = 8
NH = 8
TOPK = 16
NK = 128
NSEL = NH * TOPK
SLOT = 2048
NW = 8
NA = 3
LEVELS = 7
QUAD = 4
DECAY = -0.6065306597126334
BIG = -3.0e38

COLS = {}
_o = 0
for _n, _w in (("c", 16), ("adab", 96), ("g1", 16), ("mu", 27), ("w0", 8), ("a0", 8), ("kk", 8), ("ka", 8),
               ("rk", 8), ("bs", 8), ("iota", 16)):
    COLS[_n] = (_o, _o + _w)
    _o += _w
NCOL = _o


class Steps:

    def __init__(self, eng, own):
        self.eng, self.own, self.n = eng, own, {}

    def __call__(self, ins, sem=None):
        sem = self.own if sem is None else sem
        ins.then_inc(sem, 1)
        self.n[sem.name] = self.n.get(sem.name, 0) + 1
        self.eng.wait_ge(sem, self.n[sem.name])


def build(nc, x, ada_w, w_in, ws_t, w2, a2, g2, w_out, wq, keys_t, peer_u, peer_v,
          cols, mats, masks, vg, vb, og, lng, lnb, n2g, fg, out):
    f32, u32, u8 = mybir.dt.float32, mybir.dt.uint32, mybir.dt.uint8
    ALU, ACT, AX = mybir.AluOpType, mybir.ActivationFunctionType, mybir.AxisListType
    ds = bass.ds
    ctx = ExitStack()
    with ctx:
        def sb(name, shape, dt=f32):
            return ctx.enter_context(nc.sbuf_tensor(name, shape, dt))

        def sem(name):
            return ctx.enter_context(nc.semaphore(name))

        XW = sb("XW", [P, 2 * D])
        H = sb("H", [P, 2 * D])
        HT = sb("HT", [P, KT * SEQ])
        RING = sb("RING", [P, (NW + NA) * SLOT])
        M = sb("M", [P, NRT * SEQ])
        PT = sb("PT", [P, NRT * (SEQ + 1)])
        ACC = sb("ACC", [P, 2 * SLOT])
        COL = sb("COL", [P, NCOL])
        MAT = sb("MAT", [P, 3, P])
        MASK = sb("MASK", [P, LEVELS + 2, P], u8)
        MODC = sb("MODC", [P, 32])
        MODR = sb("MODR", [P, 4 * KT])
        MODT = sb("MODT", [4 * KT, P])
        ST = sb("ST", [P, 64])
        MID = sb("MID", [P, RT, NT])
        FC = sb("FC", [P, RT])
        OMK = sb("OMK", [P, RT])
        SPR = sb("SPR", [P, QUAD, HD])
        BON = sb("BON", [P, NT, 2 * RT])
        GST = sb("GST", [P, 4, NT * 2 * RT])

        ident, ones, blk = MAT[:, 0, :], MAT[:, 1, :], MAT[:, 2, :]

        def col(name, a=0, b=None):
            lo, hi = COLS[name]
            return COL[:, lo + a:(hi if b is None else lo + b)]

        def slot(s, n=1):
            return RING[:, s * SLOT:(s + n) * SLOT]

        x3 = XW[:, :].rearrange("p (t d) -> p t d", t=NT)
        h3 = H[:, :].rearrange("p (t d) -> p t d", t=NT)
        ht3 = HT[:, :].rearrange("p (k s) -> p k s", k=KT)
        ptok = M[:, 0:NT * RW_IN].rearrange("p (t f) -> p t f", t=NT)
        m3 = M[:, :].rearrange("p (j s) -> p j s", j=NRT)
        pt3 = PT[:, :].rearrange("p (j s) -> p j s", j=NRT)
        acc = [ACC[:, i * SLOT:(i + 1) * SLOT] for i in range(2)]
        mask32 = PT[:, 0:(LEVELS + 2) * P].bitcast(u32).rearrange("p (m t) -> p m t", t=P)
        w2a2 = XW[:, 0:GW]
        g2a, g2b = XW[:, GW:2 * GW], XW[:, 2 * GW:3 * GW]
        wst = XW[:, 3 * GW:4 * GW].rearrange("p (h i) -> p h i", h=GH)
        def tiles(ap):
            return ap.rearrange("p (j s) -> p j s", j=RT)
        mr, mk, mv = m3[:, 0:RT, :], m3[:, RT:2 * RT, :], m3[:, 2 * RT:3 * RT, :]
        ar = PT[:, 0:4096].rearrange("p (j w s) -> p j w s", j=RT, w=2)
        bt = tiles(PT[:, 4096:6144])
        a_ft, kk_ft = tiles(acc[0]), tiles(acc[1])
        T1f, T2f, T3f = slot(8), slot(9), slot(10)
        T1, T2, T3 = tiles(T1f), tiles(T2f), tiles(T3f)
        vtok = T3f.rearrange("p (c f) -> p c f", c=NT)
        ytok = acc[1].rearrange("p (c f) -> p c f", c=NT)
        BAR = slot(0).rearrange("p (h w t) -> p h w t", h=8, w=2)
        KAR = slot(1).rearrange("p (h w t) -> p h w t", h=8, w=2)
        Xi = RING[:, 2 * SLOT:2 * SLOT + 1024].rearrange("p (h t) -> p h t", h=8)
        Yi = RING[:, 2 * SLOT + 1024:3 * SLOT].rearrange("p (h t) -> p h t", h=8)
        Q = RING[:, 3 * SLOT:3 * SLOT + LEVELS * 1024].rearrange("p (l h t) -> p l h t", l=LEVELS, h=8)
        o = 3 * SLOT + LEVELS * 1024
        SA, RH = RING[:, o:o + 512], RING[:, o + 512:o + 1024]
        BTok, KTok = RING[:, 7 * SLOT:7 * SLOT + 512], RING[:, 7 * SLOT + 512:7 * SLOT + 1024]
        ogr = RING[:, 7 * SLOT + 1024:8 * SLOT]
        vgr, vbr = T1f[:, 0:GW], T1f[:, GW:2 * GW]
        lngr, lnbr = T2f[:, 0:GW], T2f[:, GW:2 * GW]
        gt1b, sh2b, a2b = M[:, 0:D], M[:, D:2 * D], M[:, 2 * D:3 * D]
        n2gr = PT[:, 0:D]
        q3 = PT[:, D:3 * D].rearrange("p (t d) -> p t d", t=NT)
        keyst = acc[1].rearrange("p (g n) -> p g n", g=2 * NH)
        gt2b, fgr = PT[:, 0:D], PT[:, D:2 * D]
        cand = M[:, 0:2048].rearrange("p (h a b) -> p h a b", h=NH, a=TOPK)
        scr = M[:, 2048:2048 + 256]
        onehot = M[:, 2304:4352].rearrange("p (h a b) -> p h a b", h=NH, a=TOPK)
        tops = M[:, 4352:4608].rearrange("p (g k) -> p g k", g=2 * NH)
        topi = M[:, 4608:4864].bitcast(u32).rearrange("p (g k) -> p g k", g=2 * NH)
        topf = M[:, 4864:5120].rearrange("p (g k) -> p g k", g=2 * NH)
        sfin = M[:, 5120:5248].rearrange("p (h k) -> p h k", h=NH)
        pos = M[:, 5248:5376].bitcast(u32)
        posp = M[:, 5376:5504].bitcast(u32)
        posf = M[:, 5504:5632].rearrange("p (h k) -> p h k", h=NH)
        isel = M[:, 5632:5888].rearrange("p (w s) -> p w s", w=2)
        gate = M[:, 5888:6144].rearrange("p (t s) -> p t s", t=NT)
        eidx = M[:, 6144:6400].bitcast(u32).rearrange("p (t s) -> p t s", t=NT)
        dots = M[:, 6400:6656].rearrange("p (t s) -> p t s", t=NT)
        estage = M[:, 6656:6672].bitcast(u32).rearrange("p (w s) -> p w s", w=2)
        PS = ctx.enter_context(nc.psum_tensor("PS", [P, 8, 512], f32))
        mod_dram = nc.dram_tensor("mod_rows", (4 * KT, P), f32, kind="Internal").ap()
        mod_row = mod_dram.rearrange("(b k) p -> b (k p)", b=4)

        names = """ld_const ld_x ld_small ld_vrow ld_lnrow ld_x2 ld_rows ld_keys ld_fin
            act_own dve_own pool_own
            silu_c x_sumsq x_rstd x_norm xT_ps xT_sb ada_used ada_acc ada_cols mod_sb modT_ps modT_sb ada_stored pt_zero
            h1_ready w_used w_evac pT_ps pT_sb mix_lora lora_act mix_kk z_ps z_sb a_ps a_sb ss_ps ss_sb
            l_ready l_exp k2_done ar_free vt_ps vt_sb bon_in bon_ps bon_sb wkv_in uv_sb ln_var ln_std vn_ready zg_ps zg_sb
            ya_sumsq ya_std ya_done score_ps score_sb inv_p inv_q inv_xy inv_x inv_y tok_ps tok_sb
            rhs_ps rhs_sb sa_ps sa_sb y_ps y_sb st_ps st_sb gn_var gn_std gate_ps yb_done yT_ps yT_sb
            x2_done x2_sumsq x2_std h2_done h2T_ps h2T_sb q_done qT_ps qT_sb sc_ps sc_used sm_in sm_exp
            idx_ready dots_done act_ready used staged slot_open ring_open outs_sumsq outs_std out_ready stored""".split()
        S = {n: sem(n) for n in names}
        w_slot = [sem(f"w_slot{i}") for i in range(NW)]
        a_slot = [sem(f"a_slot{i}") for i in range(NA)]
        g_slot = [sem(f"g_slot{i}") for i in range(NW)]

        NB = 6
        w_in_v = w_in.rearrange("(q k p) n -> q p k n", q=4, p=P)
        w_out_v = w_out.rearrange("(q k p) n -> q p k n", q=4, p=P)
        wq_v = wq.rearrange("(q k p) n -> q p k n", q=4, p=P)
        RG = 6
        LASTW = RW_IN - RG * 512

        def row(ap, n):
            return ap.rearrange("(a n) -> a n", a=1).broadcast_to([P, n])

        block = ctx.enter_context(nc.Block())

        @block.sync
        def _(sp):
            sp.dma_start(COL[:, :], cols).then_inc(S["ld_const"], 16)
            sp.dma_start(MAT[:, :, :], mats).then_inc(S["ld_const"], 16)
            sp.dma_start(mask32, masks).then_inc(S["ld_const"], 16)
            sp.dma_start(x3, x.rearrange("(t p) d -> p t d", p=P)).then_inc(S["ld_x"], 16)

            def unit(view, kq, n0, width, s, wait):
                if wait is not None:
                    sp.wait_ge(S["w_used"], wait)
                sp.dma_start(slot(s)[:, 0:4 * width].rearrange("p (k n) -> p k n", k=4),
                             view[kq, :, :, ds(n0, width)]).then_inc(w_slot[s], 16)

            for g in range(RG):
                for kq in range(4):
                    u = 4 * g + kq
                    unit(w_in_v, kq, 2 * GW + 512 * g, 512, u % NW, u - 7 if u >= NW else None)
                if g == 2:
                    sp.wait_ge(S["x_norm"], NT)
                    sp.dma_start(w2a2[0:64, :], w2).then_inc(S["ld_small"], 16)
                    sp.dma_start(w2a2[64:128, :], a2).then_inc(S["ld_small"], 16)
                    sp.dma_start(g2a, g2[0:128, :]).then_inc(S["ld_small"], 16)
                    sp.dma_start(g2b[0:32, :], g2[128:160, :]).then_inc(S["ld_small"], 16)
                    sp.dma_start(wst, ws_t).then_inc(S["ld_small"], 16)
            for kq in range(4):
                unit(w_in_v, kq, 2 * GW + RG * 512, LASTW, kq, 4 * RG + kq - 7)
            with sp.Fori(0, 2) as b:
                for i in range(8):
                    unit(w_in_v, i % 4, b * 1024 + 512 * (i // 4), 512, (4 + i) % NW, b * 8 + (28 + i - 7))
            sp.wait_ge(S["bon_ps"], 1)
            sp.dma_start(vgr, row(vg, GW)).then_inc(S["ld_vrow"], 16)
            sp.dma_start(vbr, row(vb, GW)).then_inc(S["ld_vrow"], 16)
            sp.wait_ge(S["w_used"], 44)
            sp.dma_start(ogr, row(og, GW)).then_inc(S["ld_vrow"], 16)
            sp.wait_ge(S["wkv_in"], 1)
            sp.dma_start(lngr, row(lng, GW)).then_inc(S["ld_lnrow"], 16)
            sp.dma_start(lnbr, row(lnb, GW)).then_inc(S["ld_lnrow"], 16)
            sp.wait_ge(S["y_sb"], 8)
            sp.wait_ge(S["ya_done"], NT)
            for i in range(8):
                unit(w_out_v, i % 4, 512 * (i // 4), 512, (4 + i) % NW, 44)
            sp.wait_ge(S["gate_ps"], 1)
            sp.dma_start(x3, x.rearrange("(t p) d -> p t d", p=P)).then_inc(S["ld_x2"], 16)
            sp.wait_ge(S["ada_stored"], 16)
            sp.dma_start(gt1b, row(mod_row[0, :], D)).then_inc(S["ld_rows"], 16)
            sp.dma_start(sh2b, row(mod_row[1, :], D)).then_inc(S["ld_rows"], 16)
            sp.dma_start(a2b, row(mod_row[2, :], D)).then_inc(S["ld_rows"], 16)
            sp.wait_ge(S["y_ps"], 8)
            sp.dma_start(n2gr, row(n2g, D)).then_inc(S["ld_rows"], 16)
            sp.wait_ge(S["yb_done"], 1)
            sp.dma_start(keyst, keys_t).then_inc(S["ld_keys"], 16)
            for i in range(8):
                unit(w_out_v, i % 4, 1024 + 512 * (i // 4), 512, (4 + i) % NW, 52 + i - 7)
            with sp.Fori(0, 2) as b:
                for i in range(8):
                    unit(wq_v, i % 4, b * 1024 + 512 * (i // 4), 512, (4 + i) % NW, b * 8 + (60 + i - 7))
            sp.wait_ge(S["qT_ps"], 8)
            sp.dma_start(gt2b, row(mod_row[3, :], D)).then_inc(S["ld_fin"], 16)
            sp.dma_start(fgr, row(fg, D)).then_inc(S["ld_fin"], 16)
            for t in range(NT):
                sp.wait_ge(S["out_ready"], t + 1)
                sp.dma_start(out[t * P:(t + 1) * P, :], h3[:, t, :]).then_inc(S["stored"], 16)
            sp.wait_ge(S["stored"], 16 * NT)

        @block.gpsimd
        def _(pool):
            for n in range(NB * KT):
                b, k = n // KT, n % KT
                if n >= NA:
                    pool.wait_ge(S["ada_used"], n - NA + 1)
                pool.dma_start(slot(NW + n % NA), ada_w[k * P:(k + 1) * P, b * D:(b + 1) * D])\
                    .then_inc(a_slot[n % NA], 16)

            for ps in range(4):
                t, table = ps // 2, (peer_u, peer_v)[ps % 2]
                if ps % 2 == 0:
                    pool.wait_ge(S["idx_ready"], t + 1)
                with pool.Fori(0, 8) as i:
                    for half in range(2):
                        pool.wait_ge(S["used"], i * 16 + (128 * ps + 8 * half + 1))
                        nc.gpsimd.tensor_copy(estage[:, half, :], eidx[:, t, ds(i * 16 + 8 * half, 8)])\
                            .then_inc(S["staged"], 1)
                        pool.wait_ge(S["staged"], i * 2 + (16 * ps + half + 1))
                        for s in range(NW):
                            pool.wait_ge(S["used"], i * 16 + (128 * ps + 8 * half + s + 1))
                            pool.sem_inc(S["slot_open"], 1)
                            pool.indirect_dma_start(
                                slot(s), None, table,
                                bass.IndirectOffsetOnAxis(ap=estage[:, half, s:s + 1], axis=0),
                            ).then_inc(g_slot[s], 16)

        @block.tensor
        def _(pe):
            mm, tr = nc.tensor.matmul, nc.tensor.transpose

            def w_group(u0, use, slots, bank, width=512):
                for kq in range(4):
                    pe.wait_ge(w_slot[slots[kq]], use(kq))
                    w = slot(slots[kq])[:, 0:4 * width].rearrange("p (k n) -> p k n", k=4)
                    for k in range(4):
                        for t in range(NT):
                            kt = 4 * kq + k
                            last = mm(PS[:, bank + t, 0:width], ht3[:, kt, t * P:(t + 1) * P], w[:, k, :],
                                      start=(kt == 0), stop=(kt == KT - 1))
                    last.then_inc(S["w_used"], 1)

            pe.wait_ge(S["ld_const"], 48)
            pe.wait_ge(S["x_norm"], NT)
            for r in range(4):
                if r >= 2:
                    pe.wait_ge(S["xT_sb"], r - 1)
                for j in range(4):
                    for t in range(NT):
                        k = 4 * r + j
                        last = tr(PS[:, 2 * (r % 2) + j // 2, (j % 2) * 256 + t * P:(j % 2) * 256 + (t + 1) * P],
                                  h3[:, t, k * P:(k + 1) * P], ident)
                last.then_inc(S["xT_ps"], 1)
            def col_sum(b):
                pe.wait_ge(S["ada_acc"], b + 1)
                if b > 2:
                    pe.wait_ge(S["mod_sb"], b - 1)
                for j in range(KT):
                    c_ = (b % 2) * KT + j
                    last = mm(PS[:, 4, c_:c_ + 1], acc[b % 2][:, j * P:(j + 1) * P], ones[:, 0:1],
                              start=True, stop=True)
                last.then_inc(S["ada_cols"], 1)

            col_sum(0)
            col_sum(1)
            pe.wait_ge(S["h1_ready"], 1)

            for g in range(RG):
                if g >= 2:
                    pe.wait_ge(S["w_evac"], 2 * (g - 1))
                w_group(4 * g, lambda kq, g=g: 16 * ((4 * g + kq) // NW + 1), [(4 * g + kq) % NW for kq in range(4)],
                        2 * (g % 2))
                if g in (3, 5):
                    col_sum(2 + (g - 3) // 2)
            pe.wait_ge(S["w_evac"], 2 * (RG - 1))
            w_group(24, lambda kq: 16 * 4, [0, 1, 2, 3], 0, LASTW)
            col_sum(4)
            pe.wait_ge(S["w_evac"], 2 * (RG + 1))
            pe.wait_ge(S["mod_sb"], 4)
            for r in range(7):
                if r >= 2:
                    pe.wait_ge(S["pT_sb"], r - 1)
                for j in range(4 * r, min(4 * r + 4, NRT)):
                    w = min(P, RW_IN - j * P)
                    for t in range(NT):
                        jj = j % 4
                        last = tr(PS[0:w, 4 + 2 * (r % 2) + jj // 2, (jj % 2) * 256 + t * P:(jj % 2) * 256 + (t + 1) * P],
                                  ptok[:, t, j * P:j * P + w], ident)
                last.then_inc(S["pT_ps"], 1)

            def gmlp_body(b):
                for half in range(2):
                    pe.wait_ge(S["w_evac"], 16 + 2 * half if b else 14)
                    w_group(28 + 8 * b + 4 * half,
                            (lambda kq, half=half: 16 * ((28 + 8 * b + 4 * half + kq) // NW + 1)),
                            [(4 + 4 * half + kq) % NW for kq in range(4)], 2 * half)

            pe.wait_ge(S["pT_sb"], 7)
            col_sum(5)
            gmlp_body(0)
            pe.wait_ge(S["ld_small"], 80)
            pe.wait_ge(S["lora_act"], 3)
            pe.wait_ge(S["mod_sb"], 5)
            tr(PS[0:4 * KT, 5, 0:P], MODR[:, :], ident).then_inc(S["modT_ps"], 1)
            pe.wait_ge(S["modT_sb"], 1)
            for j in range(RT):
                last = mm(PS[:, 4 + j // 2, (j % 2) * 256:(j % 2 + 1) * 256], w2a2[0:64, j * P:(j + 1) * P],
                          m3[0:64, LORA0, :], start=True, stop=True)
            last.then_inc(S["z_ps"], 1)
            pe.wait_ge(S["z_sb"], RT)
            for j in range(RT):
                last = mm(PS[:, 4 + j // 2, (j % 2) * 256:(j % 2 + 1) * 256], w2a2[64:128, j * P:(j + 1) * P],
                          m3[64:128, LORA0, :], start=True, stop=True)
            last.then_inc(S["a_ps"], 1)
            pe.wait_ge(S["a_sb"], RT)
            pe.wait_ge(S["mix_kk"], 1)
            sq = PT[:, 4096:6144]
            for n in range(4):
                last = mm(PS[:, 4 + n, :], blk, sq[:, n * 512:(n + 1) * 512], start=True, stop=True)
            last.then_inc(S["ss_ps"], 1)
            gmlp_body(1)
            pe.wait_ge(S["ss_sb"], 1)
            for c in range(NT):
                for j in range(RT):
                    last = tr(PS[:, 4 + 2 * c + j // 4, (j % 4) * P:(j % 4 + 1) * P],
                              mv[:, j, c * P:(c + 1) * P], ident)
            last.then_inc(S["vt_ps"], 1)
            pe.wait_ge(S["bon_in"], 1)
            pe.wait_ge(S["vt_sb"], 1)
            for c in range(NT):
                for j in range(RT):
                    last = mm(PS[:, 4, (c * RT + j) * 2:(c * RT + j) * 2 + 2], T1[:, j, c * P:(c + 1) * P],
                              blk[:, 0:P:HD], start=True, stop=True)
            last.then_inc(S["bon_ps"], 1)
            pe.wait_ge(S["vn_ready"], NT)
            pe.wait_ge(S["w_evac"], 22)
            for t in range(NT):
                for h in range(GH):
                    last = mm(PS[:, 2 * t + h // 4, (h % 4) * P:(h % 4 + 1) * P], wst[:, h, :],
                              h3[:, t, GW + h * P:GW + (h + 1) * P], start=True, stop=True)
            last.then_inc(S["zg_ps"], 1)
            pe.wait_ge(S["bon_sb"], 1)
            pe.wait_ge(S["zg_sb"], NT)

            pe.wait_ge(S["wkv_in"], 1)
            for n in range(4):
                hf, c = n // 2, n % 2
                tok = slice(c * P, (c + 1) * P)

                def where(pos):
                    par, i = pos // 4, pos % 4
                    return QUAD * hf + i, slice(HD * par, HD * (par + 1))

                if n >= 1:
                    pe.wait_ge(S["y_sb"], 2 * n)
                    if c == 1:
                        pe.wait_ge(S["st_sb"], 2 * hf + 2)
                for w, (src, base) in enumerate(((bt, 0), (mk, 4))):
                    for pos in range(8):
                        j, pr = where(pos)
                        last = mm(PS[:, base + pos // 2, (pos % 2) * 256:(pos % 2 + 1) * 256],
                                  src[pr, j, tok], ar[pr, j, :, tok], start=True, stop=True)
                        if pos % 2:
                            last.then_inc(S["score_ps"], 1)
                pe.wait_ge(S["score_sb"], 8 * (n + 1))
                for l in range(LEVELS):
                    for g in range(2):
                        k = 14 * n + 2 * l + g
                        if l >= 1:
                            pe.wait_ge(S["inv_y"], k - 1)
                        if l >= 2:
                            pe.wait_ge(S["inv_x"], 10 * n + 2 * (l - 2) + g + 1)
                        for pos in range(4 * g, 4 * g + 4):
                            rhs = ident if l == 0 else (Q[:, 0, pos, :] if l == 1 else Xi[:, pos, :])
                            last = mm(PS[:, g, (pos % 4) * P:(pos % 4 + 1) * P], BAR[:, pos, 0, :], rhs,
                                      start=True, stop=True)
                        last.then_inc(S["inv_p"], 1)
                    for g in range(2):
                        pe.wait_ge(S["inv_q"], 14 * n + 2 * l + g + 1)
                        for pos in range(4 * g, 4 * g + 4):
                            if 1 <= l < LEVELS - 1:
                                mm(PS[:, 2 + g, (pos % 4) * P:(pos % 4 + 1) * P], Yi[:, pos, :], Q[:, l, pos, :],
                                   start=True, stop=True)
                        for pos in range(4 * g, 4 * g + 4):
                            last = mm(PS[:, 4 + g, (pos % 4) * P:(pos % 4 + 1) * P], Q[:, l, pos, :],
                                      ident if l == 0 else Yi[:, pos, :], start=True, stop=True)
                        last.then_inc(S["inv_xy"], 1)
                pe.wait_ge(S["inv_y"], 14 * (n + 1))
                if c == 0:
                    for w, src in enumerate((bt, mk)):
                        for i in range(QUAD):
                            last = tr(PS[:, 2 + w, i * P:(i + 1) * P], src[:, QUAD * hf + i, tok], ident)
                    last.then_inc(S["tok_ps"], 1)

                def head_v(pos):
                    j, pr = where(pos)
                    return vtok[:, c, j * P + pr.start:j * P + pr.stop]

                for pos in range(8):
                    j, pr = where(pos)
                    o_ = PS[:, 6 + pos // 4, (pos % 4) * HD:(pos % 4 + 1) * HD]
                    if c == 1:
                        mm(o_, ar[pr, j, 0, tok], SPR[pr, pos % 4, :], start=True, stop=False)
                    last = mm(o_, KAR[:, pos, 0, :], head_v(pos), start=(c == 0), stop=True)
                last.then_inc(S["rhs_ps"], 1)
                pe.wait_ge(S["rhs_sb"], n + 1)
                for pos in range(8):
                    last = mm(PS[:, 0, pos * HD:(pos + 1) * HD], Yi[:, pos, :], RH[:, pos * HD:(pos + 1) * HD],
                              start=True, stop=True)
                last.then_inc(S["sa_ps"], 1)
                pe.wait_ge(S["sa_sb"], n + 1)
                for pos in range(8):
                    j, pr = where(pos)
                    o_ = PS[:, 6 + pos // 4, (pos % 4) * HD:(pos % 4 + 1) * HD]
                    if c == 1:
                        mm(o_, ar[pr, j, 1, tok], SPR[pr, pos % 4, :], start=True, stop=False)
                    mm(o_, BAR[:, pos, 1, :], SA[:, pos * HD:(pos + 1) * HD], start=(c == 0), stop=False)
                    last = mm(o_, KAR[:, pos, 1, :], head_v(pos), start=False, stop=True)
                    if pos % 4 == 3:
                        last.then_inc(S["y_ps"], 1)
                if c == 0:
                    pe.wait_ge(S["tok_sb"], 2 * (hf + 1))
                    sa2 = SA.rearrange("p (r i d) -> p i r d", r=2, i=QUAD)
                    for i in range(QUAD):
                        j = QUAD * hf + i
                        o_ = PS[:, 1, i * P:(i + 1) * P]
                        mm(o_, BTok[:, i * P:(i + 1) * P], sa2[:, i, :, :], start=True, stop=False)
                        last = mm(o_, KTok[:, i * P:(i + 1) * P], vtok[:, c, j * P:(j + 1) * P], start=False, stop=True)
                    last.then_inc(S["st_ps"], 1)
            pe.wait_ge(S["y_sb"], 8)
            for t in range(NT):
                for n in range(2):
                    o_ = PS[:, 2 * t + n, :]
                    mm(o_, m3[:, LORA0 + 1, t * P:(t + 1) * P], g2a[:, n * 512:(n + 1) * 512], start=True, stop=False)
                    last = mm(o_, m3[0:32, LORA0 + 2, t * P:(t + 1) * P], g2b[0:32, n * 512:(n + 1) * 512],
                              start=False, stop=True)
            last.then_inc(S["gate_ps"], 1)

            def transposes(src, done_ps, done_sb, base):
                for r in range(8):
                    if r >= 2:
                        pe.wait_ge(S[done_sb], r - 1)
                    for j in range(2):
                        for t in range(NT):
                            k = 2 * r + j
                            last = tr(PS[:, base + r % 2, j * 256 + t * P:j * 256 + (t + 1) * P],
                                      src[:, t, k * P:(k + 1) * P], ident)
                    last.then_inc(S[done_ps], 1)
                pe.wait_ge(S[done_sb], 8)

            pe.wait_ge(S["ya_done"], NT)
            pe.wait_ge(S["yb_done"], 1)
            transposes(h3, "yT_ps", "yT_sb", 4)
            for g in range(4):
                if g >= 2:
                    pe.wait_ge(S["x2_done"], 2 * (g - 1))
                w_group(44 + 4 * g, lambda kq, g=g: 16 * ((44 + 4 * g + kq) // NW + 1),
                        [(4 + 4 * (g % 2) + kq) % NW for kq in range(4)], 2 * (g % 2))
            pe.wait_ge(S["h2_done"], NT)
            transposes(h3, "h2T_ps", "h2T_sb", 4)
            for g in range(4):
                if g < 2:
                    pe.wait_ge(S["x2_done"], 8)
                else:
                    pe.wait_ge(S["q_done"], 2 * (g - 1))
                w_group(60 + 4 * g, lambda kq, g=g: 16 * ((60 + 4 * g + kq) // NW + 1),
                        [(4 + 4 * (g % 2) + kq) % NW for kq in range(4)], 2 * (g % 2))
            pe.wait_ge(S["q_done"], 8)
            transposes(q3, "qT_ps", "qT_sb", 4)
            pe.wait_ge(S["ld_keys"], 16)
            for t in range(NT):
                if t == 1:
                    pe.wait_ge(S["sc_used"], 1)
                for g in range(2 * NH):
                    last = mm(PS[:, g // 4, (g % 4) * P:(g % 4 + 1) * P], ht3[:, g, t * P:(t + 1) * P],
                              keyst[:, g, :], start=True, stop=True)
                last.then_inc(S["sc_ps"], 1)

        @block.scalar
        def _(act):
            act_ = nc.scalar.activation
            act.wait_ge(S["ld_const"], 48)
            act_(col("c"), col("c"), ACT.Silu).then_inc(S["silu_c"], 1)
            act.wait_ge(S["ld_x"], 16)
            for t in range(NT):
                act_(h3[:, t, :], x3[:, t, :], ACT.Square, accum_out=ST[:, t:t + 1]).then_inc(S["x_sumsq"], 1)
            act.wait_ge(S["x_rstd"], 1)
            act_(ST[:, 2:4], ST[:, 2:4], ACT.Sqrt).then_inc(S["x_rstd"], 1)
            act.wait_ge(S["x_rstd"], 3)
            act.wait_ge(S["x_sumsq"], NT)
            for t in range(NT):
                act_(h3[:, t, :], x3[:, t, :], ACT.Copy, scale=ST[:, 4 + t:5 + t]).then_inc(S["x_norm"], 1)
            for r in range(4):
                act.wait_ge(S["xT_ps"], r + 1)
                b = 2 * (r % 2)
                act_(HT[:, r * 1024:(r + 1) * 1024].rearrange("p (b n) -> p b n", b=2), PS[:, b:b + 2, :], ACT.Copy)\
                    .then_inc(S["xT_sb"], 1)
            for g in range(RG + 1):
                act.wait_ge(S["w_used"], 4 * (g + 1))
                w = 512 if g < RG else LASTW
                for t in range(NT):
                    act_(ptok[:, t, g * 512:g * 512 + w], PS[:, 2 * (g % 2) + t, 0:w], ACT.Copy).then_inc(S["w_evac"], 1)
            for r in range(7):
                act.wait_ge(S["pT_ps"], r + 1)
                for j in range(4 * r, min(4 * r + 4, NRT), 2):
                    b = 4 + 2 * (r % 2) + (j % 4) // 2
                    if j + 1 < NRT:
                        last = act_(pt3[:, j:j + 2, 1:SEQ + 1], PS[:, b, :].rearrange("p (j s) -> p j s", j=2), ACT.Copy)
                    else:
                        last = act_(pt3[0:32, j, 1:SEQ + 1], PS[0:32, b, 0:SEQ], ACT.Copy)
                last.then_inc(S["pT_sb"], 1)
            act.wait_ge(S["mix_lora"], 1)
            act_(m3[0:64, LORA0, :], m3[0:64, LORA0, :], ACT.Tanh).then_inc(S["lora_act"], 1)
            act_(m3[:, LORA0 + 1, :], m3[:, LORA0 + 1, :], ACT.Sigmoid).then_inc(S["lora_act"], 1)
            act_(m3[0:32, LORA0 + 2, :], m3[0:32, LORA0 + 2, :], ACT.Sigmoid).then_inc(S["lora_act"], 1)

            def gelu_evac(b):
                for half in range(2):
                    act.wait_ge(S["w_used"], 28 + 8 * b + 4 * (half + 1))
                    for t in range(NT):
                        act_(h3[:, t, b * GW + half * 512:b * GW + (half + 1) * 512], PS[:, 2 * half + t, :], ACT.Gelu)\
                            .then_inc(S["w_evac"], 1)

            gelu_evac(0)
            act.wait_ge(S["modT_ps"], 1)
            act_(MODT[:, :], PS[0:4 * KT, 5, 0:P], ACT.Copy).then_inc(S["modT_sb"], 1)
            act.wait_ge(S["modT_sb"], 1)
            act.dma_start(mod_dram, MODT[:, :]).then_inc(S["ada_stored"], 16)
            act.wait_ge(S["z_ps"], 1)
            for j in range(RT):
                act_(T1[:, j, :], PS[:, 4 + j // 2, (j % 2) * 256:(j % 2 + 1) * 256], ACT.Sigmoid,
                     bias=col("w0", j, j + 1)).then_inc(S["z_sb"], 1)
            act.wait_ge(S["a_ps"], 1)
            for j in range(RT):
                act_(a_ft[:, j, :], PS[:, 4 + j // 2, (j % 2) * 256:(j % 2 + 1) * 256], ACT.Sigmoid,
                     bias=col("a0", j, j + 1)).then_inc(S["a_sb"], 1)
            act.wait_ge(S["ss_ps"], 1)
            act_(PT[:, 4096:6144].rearrange("p (b n) -> p b n", b=4), PS[:, 4:8, :], ACT.Sqrt).then_inc(S["ss_sb"], 1)
            act.wait_ge(S["l_ready"], 1)
            act_(T3f, T3f, ACT.Exp).then_inc(S["l_exp"], 1)
            act_(T1f, T2f, ACT.Exp).then_inc(S["l_exp"], 1)
            act_(FC[:, :], FC[:, :], ACT.Exp).then_inc(S["l_exp"], 1)
            act.wait_ge(S["l_exp"], 2)
            act_(T2f, T2f, ACT.Exp, scale=-1.0).then_inc(S["l_exp"], 1)
            gelu_evac(1)
            act.wait_ge(S["vt_ps"], 1)
            act.wait_ge(S["k2_done"], 1)
            act_(T3f.rearrange("p (b n) -> p b n", b=4), PS[:, 4:8, :], ACT.Copy).then_inc(S["vt_sb"], 1)
            act.wait_ge(S["bon_ps"], 1)
            act_(BON[:, :, :].rearrange("p c h -> p (c h)"), PS[:, 4, 0:32], ACT.Copy).then_inc(S["bon_sb"], 1)
            act.wait_ge(S["ln_var"], 1)
            act_(ST[:, 12:14], ST[:, 12:14], ACT.Sqrt).then_inc(S["ln_std"], 1)
            act.wait_ge(S["zg_sb"], NT)
            for t in range(NT):
                act_(h3[:, t, GW:2 * GW], h3[:, t, 0:GW], ACT.Square, accum_out=ST[:, 16 + t:17 + t]).then_inc(S["ya_sumsq"], 1)
            act.wait_ge(S["ya_std"], 1)
            act_(ST[:, 18:20], ST[:, 18:20], ACT.Sqrt).then_inc(S["ya_std"], 1)
            for n in range(4):
                c = n % 2
                for l in range(1, LEVELS - 1):
                    for g in range(2):
                        act.wait_ge(S["inv_xy"], 14 * n + 2 * l + g + 1)
                        act_(Xi[:, 4 * g:4 * g + 4, :].rearrange("p h t -> p (h t)"), PS[:, 2 + g, :], ACT.Copy)\
                            .then_inc(S["inv_x"], 1)
                if c == 0:
                    act.wait_ge(S["tok_ps"], n // 2 + 1)
                    act_(BTok, PS[:, 2, :], ACT.Copy).then_inc(S["tok_sb"], 1)
                    act_(KTok, PS[:, 3, :], ACT.Copy).then_inc(S["tok_sb"], 1)
                act.wait_ge(S["sa_ps"], n + 1)
                act_(SA, PS[:, 0, :], ACT.Copy).then_inc(S["sa_sb"], 1)
            act.wait_ge(S["gn_var"], 1)
            act_(GST[:, 1, :], GST[:, 1, :], ACT.Sqrt).then_inc(S["gn_std"], 1)

            def evac_t(done_ps, done_sb):
                for r in range(8):
                    act.wait_ge(S[done_ps], r + 1)
                    act_(HT[:, r * 512:(r + 1) * 512], PS[:, 4 + r % 2, :], ACT.Copy).then_inc(S[done_sb], 1)

            evac_t("yT_ps", "yT_sb")
            act.wait_ge(S["x2_done"], 8)
            act.wait_ge(S["yT_ps"], 8)
            for t in range(NT):
                act_(h3[:, t, :], x3[:, t, :], ACT.Square, accum_out=ST[:, 20 + t:21 + t]).then_inc(S["x2_sumsq"], 1)
            act.wait_ge(S["x2_std"], 1)
            act_(ST[:, 22:24], ST[:, 22:24], ACT.Sqrt).then_inc(S["x2_std"], 1)
            evac_t("h2T_ps", "h2T_sb")
            for g in range(4):
                act.wait_ge(S["w_used"], 60 + 4 * (g + 1))
                for t in range(NT):
                    act_(q3[:, t, g * 512:(g + 1) * 512], PS[:, 2 * (g % 2) + t, :], ACT.Copy).then_inc(S["q_done"], 1)
            evac_t("qT_ps", "qT_sb")
            for t in range(NT):
                act.wait_ge(S["sm_in"], t + 1)
                act_(gate[:, t, :], gate[:, t, :], ACT.Exp).then_inc(S["sm_exp"], 1)
            for t in range(NT):
                act.wait_ge(S["dots_done"], t + 1)
                act_(dots[:, t, :], dots[:, t, :], ACT.Gelu).then_inc(S["act_ready"], 1)
            act.wait_ge(S["outs_sumsq"], 2)
            for t in range(NT):
                act_(h3[:, t, :], x3[:, t, :], ACT.Square, accum_out=ST[:, 28 + t:29 + t]).then_inc(S["outs_sumsq"], 1)
            act.wait_ge(S["outs_std"], 1)
            act_(ST[:, 30:32], ST[:, 30:32], ACT.Sqrt).then_inc(S["outs_std"], 1)

        @block.vector
        def _(dve):
            v = nc.vector
            own = Steps(dve, S["dve_own"])

            def bc(ap, n):
                return ap.unsqueeze(2).broadcast_to([P, ap.shape[1], n])

            def mean_eps(out_, in_, width, eps, sem_=None):
                own(v.tensor_scalar(out_, in_, 1.0 / width, eps, ALU.mult, ALU.add), sem_)

            dve.wait_ge(S["x_sumsq"], NT)
            mean_eps(ST[:, 2:4], ST[:, 0:2], D, 1e-6, S["x_rstd"])
            dve.wait_ge(S["x_rstd"], 2)
            v.reciprocal(ST[:, 4:6], ST[:, 2:4]).then_inc(S["x_rstd"], 1)
            dve.wait_ge(S["ld_const"], 48)

            def ada(b):
                a = acc[b % 2]
                if b >= 2:
                    dve.wait_ge(S["ada_cols"], b - 1)
                for k in range(KT):
                    n = b * KT + k
                    dve.wait_ge(a_slot[n % NA], 16 * (n // NA + 1))
                    w, ck = slot(NW + n % NA), col("c", k, k + 1)
                    if k == 0:
                        v.tensor_scalar(a, w, ck, None, ALU.mult).then_inc(S["ada_used"], 1)
                    else:
                        v.scalar_tensor_tensor(a, w, ck, a, ALU.mult, ALU.add).then_inc(S["ada_used"], 1)
                    dve.wait_ge(S["ada_used"], n + 1)
                dve.sem_inc(S["ada_acc"], 1)

            def mod_cols(b):
                dve.wait_ge(S["ada_cols"], b + 1)
                own(v.tensor_tensor(MODR[:, (b - 2) * KT:(b - 1) * KT], PS[:, 4, (b % 2) * KT:(b % 2 + 1) * KT],
                                    col("adab", b * KT, (b + 1) * KT), ALU.add), S["mod_sb"])

            dve.wait_ge(S["silu_c"], 1)
            dve.wait_ge(S["ld_const"], 48)
            own(v.tensor_copy(MASK[:, :, :], mask32))
            v.memset(pt3[:, :, 0:1], 0.0).then_inc(S["pt_zero"], 1)
            ada(0)
            ada(1)
            dve.wait_ge(S["ada_cols"], 2)
            own(v.tensor_tensor(MODC[:, :], PS[:, 4, 0:32], col("adab", 0, 32), ALU.add), S["mod_sb"])
            own(v.scalar_tensor_tensor(MODC[:, 16:32], MODC[:, 16:32], 1.0, col("g1"), ALU.add, ALU.mult))
            dve.wait_ge(S["xT_sb"], 4)
            for k in range(KT):
                last = v.tensor_scalar(ht3[:, k, :], ht3[:, k, :], MODC[:, 16 + k:17 + k], MODC[:, k:k + 1], ALU.mult, ALU.add)
                if k < KT - 1:
                    own(last)
            last.then_inc(S["h1_ready"], 1)
            ada(2)
            ada(3)
            mod_cols(2)
            ada(4)
            mod_cols(3)
            ada(5)
            mod_cols(4)

            dve.wait_ge(S["pt_zero"], 1)
            dve.wait_ge(S["pT_sb"], 7)

            mod_cols(5)

            def mix(j0, j1, parts=P, sem_=None):
                m, cur, prev = m3[0:parts, j0:j1, :], pt3[0:parts, j0:j1, 1:SEQ + 1], pt3[0:parts, j0:j1, 0:SEQ]
                own(v.tensor_tensor(m, prev, cur, ALU.subtract))
                mu = COL[0:parts, COLS["mu"][0] + j0:COLS["mu"][0] + j1].unsqueeze(2).broadcast_to([parts, j1 - j0, SEQ])
                own(v.tensor_tensor(m, m, mu, ALU.mult))
                own(v.tensor_tensor(m, m, cur, ALU.add), sem_)

            mix(NRT - 1, NRT, 32)
            mix(LORA0, NRT - 1, P, S["mix_lora"])
            mix(RT, 2 * RT)
            own(v.tensor_tensor(kk_ft, mk, bc(col("kk"), SEQ), ALU.mult))
            mix(0, RT)
            mix(2 * RT, 3 * RT)
            own(v.tensor_tensor(bt, kk_ft, kk_ft, ALU.mult), S["mix_kk"])
            own(v.tensor_scalar(OMK[:, :], col("ka"), -1.0, 1.0, ALU.mult, ALU.add))
            dve.wait_ge(S["z_sb"], RT)
            own(v.tensor_scalar(T1f, T1f, DECAY, None, ALU.mult))
            for j in range(RT):
                for c in range(NT):
                    own(v.tensor_tensor_scan(T2[:, j, c * P:(c + 1) * P], ones, T1[:, j, c * P:(c + 1) * P], 0.0,
                                             ALU.mult, ALU.add))
            t2c = T2f.rearrange("p (m s) -> p m s", s=P)
            own(v.tensor_copy(MID[:, :, :].rearrange("p j c -> p (j c)"), t2c[:, :, P // 2 - 1]))
            own(v.tensor_tensor(t2c, t2c, bc(MID[:, :, :].rearrange("p j c -> p (j c)"), P), ALU.subtract))
            own(v.tensor_tensor(FC[:, :], T2[:, :, P - 1], MID[:, :, 1], ALU.add))
            own(v.tensor_tensor(T3f, T2f, T1f, ALU.subtract), S["l_ready"])
            dve.wait_ge(S["ss_sb"], 1)
            own(v.tensor_scalar(bt, bt, 1e-12, None, ALU.max))
            own(v.reciprocal(bt, bt))
            own(v.tensor_tensor(kk_ft, kk_ft, bt, ALU.mult))
            dve.wait_ge(S["l_exp"], 1)
            own(v.scalar_tensor_tensor(ar[:, :, 0, :], kk_ft, -1.0, T3, ALU.mult, ALU.mult))
            dve.wait_ge(S["a_sb"], RT)
            own(v.tensor_tensor(T3, a_ft, bc(col("ka"), SEQ), ALU.mult))
            own(v.tensor_tensor(T3, T3, bc(OMK[:, :], SEQ), ALU.add))
            own(v.tensor_tensor(mk, mk, T3, ALU.mult), S["k2_done"])
            dve.wait_ge(S["l_exp"], 2)
            own(v.tensor_tensor(ar[:, :, 1, :], mr, T1, ALU.mult))
            dve.wait_ge(S["l_exp"], 4)
            own(v.tensor_tensor(T1, mr, mk, ALU.mult))
            own(v.tensor_tensor(T1, T1, bc(col("rk"), SEQ), ALU.mult), S["bon_in"])
            own(v.tensor_tensor(a_ft, a_ft, kk_ft, ALU.mult))
            own(v.tensor_tensor(bt, a_ft, T2, ALU.mult))
            own(v.tensor_tensor(mk, mk, T2, ALU.mult))

            dve.wait_ge(S["ld_small"], 80)
            own(v.memset(wst[64:P, :, 0:64], 0.0))
            dve.wait_ge(S["w_evac"], 22)
            for t in range(NT):
                for i in range(2):
                    own(v.bn_stats(ST[:, 32 + 6 * i:38 + 6 * i], h3[:, t, GW + 512 * i:GW + 512 * (i + 1)]))
                own(v.bn_aggr(ST[:, 8 + 2 * t:10 + 2 * t], ST[:, 32:44]))
                own(v.tensor_scalar(ST[:, 12 + t:13 + t], ST[:, 9 + 2 * t:10 + 2 * t], 1e-5, None, ALU.add))
            dve.sem_inc(S["ln_var"], 1)
            dve.wait_ge(S["ln_std"], 1)
            own(v.reciprocal(ST[:, 14:16], ST[:, 12:14]))
            dve.wait_ge(S["ld_vrow"], 48)
            for t in range(NT):
                vv = h3[:, t, GW:2 * GW]
                own(v.tensor_scalar(vv, vv, ST[:, 8 + 2 * t:9 + 2 * t], ST[:, 14 + t:15 + t], ALU.subtract, ALU.mult))
                own(v.tensor_tensor(vv, vv, vgr, ALU.mult))
                own(v.tensor_tensor(vv, vv, vbr, ALU.add), S["vn_ready"])
            dve.wait_ge(S["w_used"], 44)
            own(v.memset(RING[:, 0:2 * SLOT], 0.0))
            own(v.tensor_copy(RING[:, 3 * SLOT:3 * SLOT + LEVELS * 1024].rearrange("p (m t) -> p m t", t=P),
                              ident.unsqueeze(1).broadcast_to([P, LEVELS * 8, P])), S["wkv_in"])
            dve.wait_ge(S["zg_ps"], 1)
            for t in range(NT):
                for h in range(GH):
                    u_ = h3[:, t, h * P:(h + 1) * P]
                    own(v.scalar_tensor_tensor(u_, PS[:, 2 * t + h // 4, (h % 4) * P:(h % 4 + 1) * P],
                                               col("bs", h, h + 1), u_, ALU.add, ALU.mult))
                dve.sem_inc(S["zg_sb"], 1)
            dve.wait_ge(S["ya_sumsq"], NT)
            mean_eps(ST[:, 18:20], ST[:, 16:18], GW, 1e-6, S["ya_std"])
            dve.wait_ge(S["ya_std"], 2)
            own(v.reciprocal(ST[:, 24:26], ST[:, 18:20]))
            for t in range(NT):
                ya = h3[:, t, 0:GW]
                own(v.scalar_tensor_tensor(ya, ya, ST[:, 24 + t:25 + t], ogr, ALU.mult, ALU.mult), S["ya_done"])

            strict_incl = MASK[:, LEVELS:LEVELS + 2, :].rearrange("p w t -> p (w t)")
            for n in range(4):
                hf, c = n // 2, n % 2
                for i in range(8):
                    dve.wait_ge(S["score_ps"], 8 * n + i + 1)
                    dst = (BAR, KAR)[i // 4][:, 2 * (i % 4):2 * (i % 4) + 2, :, :].rearrange("p h w t -> p h (w t)")
                    own(v.copy_predicated(dst, strict_incl.unsqueeze(1).broadcast_to([P, 2, 2 * P]),
                                          PS[:, i, :].rearrange("p (h t) -> p h t", h=2)), S["score_sb"])
                for l in range(LEVELS):
                    mask = MASK[:, l, :].unsqueeze(1).broadcast_to([P, 4, P])
                    for g in range(2):
                        dve.wait_ge(S["inv_p"], 14 * n + 2 * l + g + 1)
                        own(v.copy_predicated(Q[:, l, 4 * g:4 * g + 4, :], mask,
                                              PS[:, g, :].rearrange("p (h t) -> p h t", h=4)), S["inv_q"])
                    for g in range(2):
                        dve.wait_ge(S["inv_xy"], 14 * n + 2 * l + g + 1)
                        own(v.tensor_copy(Yi[:, 4 * g:4 * g + 4, :].rearrange("p h t -> p (h t)"), PS[:, 4 + g, :]), S["inv_y"])
                dve.wait_ge(S["rhs_ps"], n + 1)
                own(v.tensor_copy(RH.rearrange("p (b n) -> p b n", b=2), PS[:, 6:8, 0:256]), S["rhs_sb"])
                for par in range(2):
                    dve.wait_ge(S["y_ps"], 2 * n + par + 1)
                    dst = ytok[:, c, QUAD * hf * P:QUAD * (hf + 1) * P].rearrange("p (i d) -> p i d", i=QUAD)
                    own(v.tensor_copy(dst[:, :, HD * par:HD * (par + 1)],
                                      PS[:, 6 + par, 0:256].rearrange("p (i d) -> p i d", i=QUAD)), S["y_sb"])
                if c == 0:
                    dve.wait_ge(S["st_ps"], hf + 1)
                    for par in range(2):
                        pr = slice(HD * par, HD * (par + 1))
                        fc = FC[pr, QUAD * hf:QUAD * (hf + 1)].unsqueeze(2).broadcast_to([HD, QUAD, HD])
                        own(v.tensor_tensor(SPR[pr, :, :],
                                            PS[pr, 1, :].rearrange("p (i v) -> p i v", i=QUAD)[:, :, pr], fc, ALU.mult),
                            S["st_sb"])

            y4 = acc[1].rearrange("p (m d) -> p m d", d=HD)
            yf = acc[1].rearrange("p (t f) -> p t f", t=NT)
            sq4 = acc[0].rearrange("p (m d) -> p m d", d=HD)
            own(v.tensor_reduce(GST[:, 0, :], y4, AX.X, ALU.add))
            own(v.tensor_scalar(GST[:, 0, :], GST[:, 0, :], 1.0 / HD, None, ALU.mult))
            own(v.tensor_tensor(y4, y4, bc(GST[:, 0, :], HD), ALU.subtract))
            own(v.tensor_tensor(sq4, y4, y4, ALU.mult))
            own(v.tensor_reduce(GST[:, 1, :], sq4, AX.X, ALU.add))
            mean_eps(GST[:, 1, :], GST[:, 1, :], HD, 64e-5, S["gn_var"])
            dve.wait_ge(S["gn_std"], 1)
            own(v.reciprocal(GST[:, 2, :], GST[:, 1, :]))
            own(v.tensor_tensor(y4, y4, bc(GST[:, 2, :], HD), ALU.mult))
            dve.wait_ge(S["ld_lnrow"], 32)
            own(v.tensor_tensor(yf, yf, lngr.unsqueeze(1).broadcast_to([P, NT, GW]), ALU.mult))
            own(v.tensor_tensor(yf, yf, lnbr.unsqueeze(1).broadcast_to([P, NT, GW]), ALU.add))
            own(v.tensor_tensor(sq4, T3f.rearrange("p (m d) -> p m d", d=HD),
                                bc(BON[:, :, :].rearrange("p c h -> p (c h)"), HD), ALU.mult))
            own(v.tensor_tensor(acc[1], acc[1], acc[0], ALU.add))
            dve.wait_ge(S["gate_ps"], 1)
            for t in range(NT):
                own(v.tensor_tensor(h3[:, t, GW:2 * GW].rearrange("p (b n) -> p b n", b=2),
                                    yf[:, t, :].rearrange("p (b n) -> p b n", b=2), PS[:, 2 * t:2 * t + 2, :], ALU.mult))
            dve.sem_inc(S["yb_done"], 1)

            dve.wait_ge(S["ld_x2"], 16)
            dve.wait_ge(S["ld_rows"], 64)
            own(v.scalar_tensor_tensor(a2b, a2b, 1.0, n2gr, ALU.add, ALU.mult))
            tmp = T1f[:, 0:512]
            for g in range(4):
                cs = slice(g * 512, (g + 1) * 512)
                dve.wait_ge(S["w_used"], 44 + 4 * (g + 1))
                for t in range(NT):
                    own(v.tensor_tensor(tmp, PS[:, 2 * (g % 2) + t, :], gt1b[:, cs], ALU.mult))
                    own(v.tensor_tensor(x3[:, t, cs], x3[:, t, cs], tmp, ALU.add), S["x2_done"])
            dve.wait_ge(S["x2_sumsq"], NT)
            mean_eps(ST[:, 22:24], ST[:, 20:22], D, 1e-6, S["x2_std"])
            dve.wait_ge(S["x2_std"], 2)
            own(v.reciprocal(ST[:, 26:28], ST[:, 22:24]))
            for t in range(NT):
                own(v.scalar_tensor_tensor(h3[:, t, :], x3[:, t, :], ST[:, 26 + t:27 + t], a2b, ALU.mult, ALU.mult))
                own(v.tensor_tensor(h3[:, t, :], h3[:, t, :], sh2b, ALU.add), S["h2_done"])

            def top16(values, val, idx, work):
                own(v.max(val[:, 0:8], values))
                own(v.max_index(idx[:, 0:8], val[:, 0:8], values))
                own(v.match_replace(work, val[:, 0:8], values, BIG))
                own(v.max(val[:, 8:16], work))
                own(v.max_index(idx[:, 8:16], val[:, 8:16], work))

            iota = col("iota").unsqueeze(1).broadcast_to([P, NSEL, TOPK])
            for t in range(NT):
                dve.wait_ge(S["sc_ps"], t + 1)
                for g in range(2 * NH):
                    top16(PS[:, g // 4, (g % 4) * P:(g % 4 + 1) * P], tops[:, g, :], topi[:, g, :], scr[:, 0:P])
                dve.sem_inc(S["sc_used"], 1)
                own(v.tensor_copy(topf[:, :, :], topi[:, :, :]))
                for h in range(NH):
                    own(v.tensor_tensor(cand[:, h, :, :], bc(tops[:, 2 * h, :], TOPK),
                                        tops[:, 2 * h + 1, :].unsqueeze(1).broadcast_to([P, TOPK, TOPK]), ALU.add))
                    ch = cand[:, h, :, :].rearrange("p a b -> p (a b)")
                    top16(ch, sfin[:, h, :], pos[:, h * TOPK:(h + 1) * TOPK], scr)
                for w in range(2):
                    if w == 0:
                        own(v.tensor_scalar(posp, pos, 4, None, ALU.logical_shift_right))
                    else:
                        own(v.tensor_scalar(posp, pos, 15, None, ALU.bitwise_and))
                    own(v.tensor_copy(posf.rearrange("p h k -> p (h k)"), posp))
                    oh = onehot.rearrange("p h a b -> p (h a) b")
                    own(v.tensor_tensor(oh, iota, bc(posf.rearrange("p h k -> p (h k)"), TOPK), ALU.is_equal))
                    for h in range(NH):
                        own(v.tensor_tensor(onehot[:, h, :, :], onehot[:, h, :, :],
                                            topf[:, 2 * h + w, :].unsqueeze(1).broadcast_to([P, TOPK, TOPK]), ALU.mult))
                    own(v.tensor_reduce(isel[:, w, :], oh, AX.X, ALU.add))
                own(v.scalar_tensor_tensor(isel[:, 0, :], isel[:, 0, :], float(NK), isel[:, 1, :], ALU.mult, ALU.add))
                own(v.tensor_copy(eidx[:, t, :], isel[:, 0, :]))
                if t == 0:
                    dve.wait_ge(S["w_used"], 76)
                    dve.sem_inc(S["used"], NW)
                dve.sem_inc(S["idx_ready"], 1)
                gt = gate[:, t, :].rearrange("p (h k) -> p h k", h=NH)
                own(v.tensor_tensor(gt, sfin, bc(sfin[:, :, 0], TOPK), ALU.subtract), S["sm_in"])
                dve.wait_ge(S["sm_exp"], t + 1)
                own(v.tensor_reduce(ST[:, 44:52], gt, AX.X, ALU.add))
                own(v.reciprocal(ST[:, 52:60], ST[:, 44:52]))
                own(v.tensor_tensor(gt, gt, bc(ST[:, 52:60], TOPK), ALU.mult))

            for ps in range(4):
                t = ps // 2
                if ps % 2 == 1:
                    dve.sem_inc(S["dots_done"], 1)
                    dve.wait_ge(S["act_ready"], t + 1)
                    own(v.tensor_tensor(dots[:, t, :], dots[:, t, :], gate[:, t, :], ALU.mult))
                    own(v.memset(acc[t], 0.0))
                with dve.Fori(0, 8) as i:
                    for m in range(16):
                        s, half = m % NW, m // NW
                        dve.wait_ge(g_slot[s], i * 32 + 16 * (16 * ps + half + 1))
                        if ps % 2 == 0:
                            v.scalar_tensor_tensor(slot(s), slot(s), 1.0, h3[:, t, :], ALU.mult, ALU.mult,
                                                   accum_out=dots[:, t, ds(i * 16 + m, 1)]).then_inc(S["used"], 1)
                        else:
                            v.scalar_tensor_tensor(acc[t], slot(s), dots[:, t, ds(i * 16 + m, 1)], acc[t],
                                                   ALU.mult, ALU.add).then_inc(S["used"], 1)
                        dve.wait_ge(S["used"], i * 16 + (NW + 128 * ps + m + 1))
            dve.wait_ge(S["ld_fin"], 32)
            for t in range(NT):
                own(v.tensor_tensor(acc[t], acc[t], gt2b, ALU.mult))
                own(v.tensor_tensor(x3[:, t, :], x3[:, t, :], acc[t], ALU.add), S["outs_sumsq"])
            dve.wait_ge(S["outs_sumsq"], 4)
            mean_eps(ST[:, 30:32], ST[:, 28:30], D, 1e-6)
            dve.sem_inc(S["outs_std"], 1)
            dve.wait_ge(S["outs_std"], 2)
            own(v.reciprocal(ST[:, 60:62], ST[:, 30:32]))
            for t in range(NT):
                own(v.scalar_tensor_tensor(h3[:, t, :], x3[:, t, :], ST[:, 60 + t:61 + t], fgr, ALU.mult, ALU.mult),
                    S["out_ready"])


_COLS = [("c", 16), ("ada_b", 96), ("norm1_g", 16), ("rwkv_mu", 27), ("rwkv_w0", 8), ("rwkv_a0", 8),
         ("rwkv_kk", 8), ("rwkv_ka", 8), ("rwkv_rk", 8), ("gmlp_bs", 8)]


def kernel(**inputs):
    import concourse.bacc as _bacc
    from concourse.bass_utils import run_bass_kernel_spmd as _run

    a = {k: np.asarray(val) for k, val in inputs.items()}
    f = np.float32

    parts = []
    for name, w in _COLS:
        flat = a[name].reshape(-1)[:w * P]
        pad = np.zeros(w * P - flat.size, f)
        parts.append(np.concatenate([flat, pad]).reshape(w, P).T)
    parts.append(np.tile(np.arange(16, dtype=f), (P, 1)))
    i, l = np.arange(P)[:, None], np.arange(P)[None, :]
    mats = np.stack([(i == l), np.ones((P, P), bool), (i // HD == l // HD)], 1).astype(f)
    masks = [((i // (2 * m) == l // (2 * m)) & (i % (2 * m) >= m) & (l % (2 * m) < m)) for m in (1, 2, 4, 8, 16, 32, 64)]
    masks = np.stack(masks + [i < l, i <= l], 1).astype(np.uint32)

    data = {
        "x": a["x"][0], "ada_w": a["ada_w"][0],
        "w_in": a["w_in"][0], "ws_t": a["gmlp_ws"][0].transpose(2, 0, 1), "w2": a["rwkv_w2"][0],
        "a2": a["rwkv_a2"][0], "g2": a["rwkv_g2"][0], "w_out": a["w_out"][0], "wq": a["peer_wq"][0],
        "keys_t": a["peer_keys"][0].reshape(2 * NH, NK, P).transpose(2, 0, 1), "peer_u": a["peer_u"][0],
        "peer_v": a["peer_v"][0], "cols": np.concatenate(parts, 1), "mats": mats, "masks": masks,
        "vg": a["gmlp_v_g"][0], "vb": a["gmlp_v_b"][0], "og": a["gmlp_out_g"][0], "lng": a["rwkv_ln_g"][0],
        "lnb": a["rwkv_ln_b"][0], "n2g": a["norm2_g"][0], "fg": a["final_g"],
    }
    nc = _bacc.Bacc("TRN2", target_bir_lowering=False, num_devices=1, dynamic_dma_scratch_size=8192)
    arrays, args = {}, []
    for name, arr in data.items():
        arr = np.ascontiguousarray(arr)
        arrays[f"in_{name}"] = arr
        args.append(nc.dram_tensor(f"in_{name}", arr.shape, mybir.dt.from_np(arr.dtype), kind="ExternalInput").ap())
    args.append(nc.dram_tensor("out", (SEQ, D), mybir.dt.float32, kind="ExternalOutput").ap())
    build(nc, *args)
    r = _run(nc, [arrays], core_ids=[0])
    return r.results[0]["out"].reshape(1, SEQ, D)
```

```python
from contextlib import ExitStack
import numpy as np
import concourse.bass as bass
from concourse import mybir

P = 128
D = 2048
SEQ = 256
NT = SEQ // P
KT = D // P
GW = 1024
RT = GW // P
HD = 64
RW_IN = 3360
NRT = 27
LORA0 = 3 * RT
IN_W = 2 * GW + RW_IN
GH = 8
NH = 8
TOPK = 16
NK = 128
NSEL = NH * TOPK
SLOT = 2048
NW = 8
NA = 3
LEVELS = 7
QUAD = 4
DECAY = -0.6065306597126334
BIG = -3.0e38

COLS = {}
_o = 0
for _n, _w in (("c", 16), ("adab", 96), ("g1", 16), ("mu", 27), ("w0", 8), ("a0", 8), ("kk", 8), ("ka", 8),
               ("rk", 8), ("bs", 8), ("iota", 16)):
    COLS[_n] = (_o, _o + _w)
    _o += _w
NCOL = _o


class Steps:

    def __init__(self, eng, own):
        self.eng, self.own, self.n = eng, own, {}

    def __call__(self, ins, sem=None):
        sem = self.own if sem is None else sem
        ins.then_inc(sem, 1)
        self.n[sem.name] = self.n.get(sem.name, 0) + 1
        self.eng.wait_ge(sem, self.n[sem.name])


def build(nc, x, ada_w, w_in, ws_t, w2, a2, g2, w_out, wq, keys_t, peer_u, peer_v,
          cols, mats, masks, vg, vb, og, lng, lnb, n2g, fg, out):
    f32, u32, u8 = mybir.dt.float32, mybir.dt.uint32, mybir.dt.uint8
    ALU, ACT, AX = mybir.AluOpType, mybir.ActivationFunctionType, mybir.AxisListType
    ds = bass.ds
    ctx = ExitStack()
    with ctx:
        def sb(name, shape, dt=f32):
            return ctx.enter_context(nc.sbuf_tensor(name, shape, dt))

        def sem(name):
            return ctx.enter_context(nc.semaphore(name))

        XW = sb("XW", [P, 2 * D])
        H = sb("H", [P, 2 * D])
        HT = sb("HT", [P, KT * SEQ])
        RING = sb("RING", [P, (NW + NA) * SLOT])
        M = sb("M", [P, NRT * SEQ])
        PT = sb("PT", [P, NRT * (SEQ + 1)])
        ACC = sb("ACC", [P, 2 * SLOT])
        COL = sb("COL", [P, NCOL])
        MAT = sb("MAT", [P, 3, P])
        MASK = sb("MASK", [P, LEVELS + 2, P], u8)
        MODC = sb("MODC", [P, 32])
        MODR = sb("MODR", [P, 4 * KT])
        MODT = sb("MODT", [3 * KT, P])
        SSQ = sb("SSQ", [P, NT, 4])
        ST = sb("ST", [P, 64])
        MID = sb("MID", [P, RT, NT])
        FC = sb("FC", [P, RT])
        OMK = sb("OMK", [P, RT])
        SPR = sb("SPR", [P, QUAD, HD])
        BON = sb("BON", [P, NT, 2 * RT])
        GST = sb("GST", [P, 4, NT * 2 * RT])

        ident, ones, blk = MAT[:, 0, :], MAT[:, 1, :], MAT[:, 2, :]

        def col(name, a=0, b=None):
            lo, hi = COLS[name]
            return COL[:, lo + a:(hi if b is None else lo + b)]

        def slot(s, n=1):
            return RING[:, s * SLOT:(s + n) * SLOT]

        x3 = XW[:, :].rearrange("p (t d) -> p t d", t=NT)
        h3 = H[:, :].rearrange("p (t d) -> p t d", t=NT)
        ht3 = HT[:, :].rearrange("p (k s) -> p k s", k=KT)
        ptok = M[:, 0:NT * RW_IN].rearrange("p (t f) -> p t f", t=NT)
        m3 = M[:, :].rearrange("p (j s) -> p j s", j=NRT)
        pt3 = PT[:, :].rearrange("p (j s) -> p j s", j=NRT)
        acc = [ACC[:, i * SLOT:(i + 1) * SLOT] for i in range(2)]
        mask32 = PT[:, 0:(LEVELS + 2) * P].bitcast(u32).rearrange("p (m t) -> p m t", t=P)
        w2a2 = XW[:, 0:GW]
        g2a, g2b = XW[:, GW:2 * GW], XW[:, 2 * GW:3 * GW]
        wst = XW[:, 3 * GW:4 * GW].rearrange("p (h i) -> p h i", h=GH)
        def tiles(ap):
            return ap.rearrange("p (j s) -> p j s", j=RT)
        mr, mk, mv = m3[:, 0:RT, :], m3[:, RT:2 * RT, :], m3[:, 2 * RT:3 * RT, :]
        ar = PT[:, 0:4096].rearrange("p (j w s) -> p j w s", j=RT, w=2)
        bt = tiles(PT[:, 4096:6144])
        a_ft, kk_ft = tiles(acc[0]), tiles(acc[1])
        T1f, T2f, T3f = slot(8), slot(9), slot(10)
        T1, T2, T3 = tiles(T1f), tiles(T2f), tiles(T3f)
        vtok = T3f.rearrange("p (c f) -> p c f", c=NT)
        ytok = acc[1].rearrange("p (c f) -> p c f", c=NT)
        def heads2(ap):
            return ap.rearrange("p (h w t) -> p h w t", h=8, w=2)

        def heads1(ap):
            return ap.rearrange("p (h t) -> p h t", h=8)

        BAR = [heads2(slot(0)), heads2(slot(1))]
        KAR = [heads2(HT[:, 0:SLOT]), heads2(HT[:, SLOT:2 * SLOT])]
        Xi = heads1(RING[:, 2 * SLOT:2 * SLOT + 1024])
        Yi = [heads1(RING[:, 2 * SLOT + 1024:3 * SLOT]), heads1(M[:, 0:1024])]
        Q = RING[:, 3 * SLOT:3 * SLOT + LEVELS * 1024].rearrange("p (l h t) -> p l h t", l=LEVELS, h=8)
        o = 3 * SLOT + LEVELS * 1024
        SA, RH = RING[:, o:o + 512], RING[:, o + 512:o + 1024]
        BTok, KTok = RING[:, 7 * SLOT:7 * SLOT + 512], RING[:, 7 * SLOT + 512:7 * SLOT + 1024]
        ogr = RING[:, 7 * SLOT + 1024:8 * SLOT]
        vgr, vbr = T1f[:, 0:GW], T1f[:, GW:2 * GW]
        lngr, lnbr = T2f[:, 0:GW], T2f[:, GW:2 * GW]
        gt1b, sh2b, a2b = M[:, 0:D], M[:, D:2 * D], M[:, 2 * D:3 * D]
        n2gr = PT[:, 0:D]
        qt = [PT[:, i * 1024:(i + 1) * 1024].rearrange("p (g s) -> p g s", g=4) for i in range(2)]
        xtmp = M[:, 3 * D:3 * D + 512]
        q3 = PT[:, D:3 * D].rearrange("p (t d) -> p t d", t=NT)
        keyst = acc[1].rearrange("p (g n) -> p g n", g=2 * NH)
        gt2b, fgr = PT[:, 0:D], PT[:, D:2 * D]
        cand = M[:, 0:512].rearrange("p (h a b) -> p h a b", h=2, a=TOPK)
        onehot = M[:, 512:1024].rearrange("p (h a b) -> p h a b", h=2, a=TOPK)
        scr = M[:, 1024:1280]
        GS = 2 * TOPK
        tops = M[:, 1280:1344].rearrange("p (g k) -> p g k", g=4)
        topi = M[:, 1344:1408].bitcast(u32).rearrange("p (g k) -> p g k", g=4)
        topf = M[:, 1536:1600]
        pos = M[:, 1600:1632].bitcast(u32)
        posp = M[:, 1632:1664].bitcast(u32)
        posf = M[:, 1664:1696]
        isel = M[:, 1696:1760].rearrange("p (w s) -> p w s", w=2)
        sc1 = M[:, 2048:4096]
        sfin = M[:, 1792:2048].rearrange("p (t s) -> p t s", t=NT)
        gate = M[:, 5888:6144].rearrange("p (t s) -> p t s", t=NT)
        eidx = M[:, 6144:6400].bitcast(u32).rearrange("p (t s) -> p t s", t=NT)
        dots = M[:, 6400:6656].rearrange("p (t s) -> p t s", t=NT)
        estage = M[:, 6656:6672].bitcast(u32).rearrange("p (w s) -> p w s", w=2)
        PS = ctx.enter_context(nc.psum_tensor("PS", [P, 8, 512], f32))
        mod_dram = nc.dram_tensor("mod_rows", (4 * KT, P), f32, kind="Internal").ap()
        mod_row = mod_dram.rearrange("(b k) p -> b (k p)", b=4)

        names = """ld_const ld_x ld_small ld_vrow ld_lnrow ld_x2 ld_rows ld_keys ld_fin
            act_own dve_own pool_own
            silu_c x_sumsq x_rstd x_norm xT_ps xT_sb ada_used ada_acc ada_cols mod_sb modT_ps modT_sb ada_stored pt_zero
            h1_ready w_used w_evac pT_ps pT_sb mix_lora lora_act mix_kk z_ps z_sb a_ps a_sb ss_ps ss_sb
            l_ready l_exp k2_done ar_free vt_ps vt_sb bon_in bon_ps bon_sb wkv_in wkv_init gate_used uv_sb ln_var ln_std vn_ready zg_ps zg_sb
            ya_sumsq ya_std ya_done score_ps score_sb inv_p inv_q inv_xy inv_x inv_y tok_ps tok_sb
            rhs_ps rhs_sb sa_ps sa_sb y_ps y_sb st_ps st_sb gn_var gn_std gate_ps yb_done yT_ps yT_sb
            x2_done x2_sumsq x2_std h2_done h2T_ps h2T_sb q_done qT_ps qT_sb sc_ps sc_used sc1_sb sm_in sm_exp
            idx0_ready idx1_ready dots_done act_ready used staged slot_open ring_open outs_sumsq outs_std out_ready stored""".split()
        S = {n: sem(n) for n in names}
        w_slot = [sem(f"w_slot{i}") for i in range(NW)]
        a_slot = [sem(f"a_slot{i}") for i in range(NA)]
        g_slot = [sem(f"g_slot{i}") for i in range(NW)]

        gslot = [slot(s) for s in (8, 9, 10, 4, 5, 6, 7, 0)]
        NB = 6
        w_in_v = w_in.rearrange("(q k p) n -> q p k n", q=4, p=P)
        w_out_v = w_out.rearrange("(q k p) n -> q p k n", q=4, p=P)
        wq_v = wq.rearrange("(q k p) n -> q p k n", q=4, p=P)
        RG = 6
        LASTW = RW_IN - RG * 512

        def row(ap, n):
            return ap.rearrange("(a n) -> a n", a=1).broadcast_to([P, n])

        block = ctx.enter_context(nc.Block())

        @block.sync
        def _(sp):
            sp.dma_start(COL[:, :], cols).then_inc(S["ld_const"], 16)
            sp.dma_start(MAT[:, :, :], mats).then_inc(S["ld_const"], 16)
            sp.dma_start(mask32, masks).then_inc(S["ld_const"], 16)
            sp.dma_start(x3, x.rearrange("(t p) d -> p t d", p=P)).then_inc(S["ld_x"], 16)

            def unit(view, kq, n0, width, s, wait):
                if wait is not None:
                    sp.wait_ge(S["w_used"], wait)
                sp.dma_start(slot(s)[:, 0:4 * width].rearrange("p (k n) -> p k n", k=4),
                             view[kq, :, :, ds(n0, width)]).then_inc(w_slot[s], 16)

            sp.wait_ge(S["ada_used"], 29)
            for g in range(RG):
                for kq in range(4):
                    u = 4 * g + kq
                    unit(w_in_v, kq, 2 * GW + 512 * g, 512, u % NW, u - 7 if u >= NW else None)
                if g == 2:
                    sp.wait_ge(S["x_norm"], NT)
                    sp.dma_start(w2a2[0:64, :], w2).then_inc(S["ld_small"], 16)
                    sp.dma_start(w2a2[64:128, :], a2).then_inc(S["ld_small"], 16)
                    sp.dma_start(g2a, g2[0:128, :]).then_inc(S["ld_small"], 16)
                    sp.dma_start(g2b[0:32, :], g2[128:160, :]).then_inc(S["ld_small"], 16)
                    sp.dma_start(wst, ws_t).then_inc(S["ld_small"], 16)
            for kq in range(4):
                unit(w_in_v, kq, 2 * GW + RG * 512, LASTW, kq, 4 * RG + kq - 7)
            with sp.Fori(0, 2) as b:
                for i in range(8):
                    unit(w_in_v, i % 4, b * 1024 + 512 * (i // 4), 512, (4 + i) % NW, b * 8 + (28 + i - 7))
            sp.wait_ge(S["bon_ps"], 1)
            sp.dma_start(vgr, row(vg, GW)).then_inc(S["ld_vrow"], 16)
            sp.dma_start(vbr, row(vb, GW)).then_inc(S["ld_vrow"], 16)
            sp.wait_ge(S["w_used"], 44)
            sp.dma_start(ogr, row(og, GW)).then_inc(S["ld_vrow"], 16)
            sp.wait_ge(S["wkv_in"], 1)
            sp.dma_start(lngr, row(lng, GW)).then_inc(S["ld_lnrow"], 16)
            sp.dma_start(lnbr, row(lnb, GW)).then_inc(S["ld_lnrow"], 16)
            sp.wait_ge(S["y_sb"], 8)
            sp.wait_ge(S["ya_done"], NT)
            for i in range(8):
                unit(w_out_v, i % 4, 512 * (i // 4), 512, (4 + i) % NW, 44)
            sp.wait_ge(S["gate_ps"], 2)
            sp.dma_start(x3, x.rearrange("(t p) d -> p t d", p=P)).then_inc(S["ld_x2"], 16)
            sp.wait_ge(S["ada_stored"], 16)
            sp.dma_start(gt1b, row(mod_row[0, :], D)).then_inc(S["ld_rows"], 16)
            sp.dma_start(sh2b, row(mod_row[1, :], D)).then_inc(S["ld_rows"], 16)
            sp.dma_start(a2b, row(mod_row[2, :], D)).then_inc(S["ld_rows"], 16)
            sp.dma_start(n2gr, row(n2g, D)).then_inc(S["ld_rows"], 16)
            sp.wait_ge(S["yb_done"], 2)
            sp.dma_start(keyst, keys_t).then_inc(S["ld_keys"], 16)
            for i in range(8):
                unit(w_out_v, i % 4, 1024 + 512 * (i // 4), 512, (4 + i) % NW, 52 + i - 7)
            with sp.Fori(0, 2) as b:
                for i in range(8):
                    unit(wq_v, i % 4, b * 1024 + 512 * (i // 4), 512, (4 + i) % NW, b * 8 + (60 + i - 7))
            sp.wait_ge(S["sc_ps"], 4)
            sp.wait_ge(S["ada_stored"], 32)
            sp.dma_start(gt2b, row(mod_row[3, :], D)).then_inc(S["ld_fin"], 16)
            sp.dma_start(fgr, row(fg, D)).then_inc(S["ld_fin"], 16)
            for t in range(NT):
                sp.wait_ge(S["out_ready"], t + 1)
                sp.dma_start(out[t * P:(t + 1) * P, :], h3[:, t, :]).then_inc(S["stored"], 16)
            sp.wait_ge(S["stored"], 16 * NT)

        @block.gpsimd
        def _(pool):
            for n in range(NB * KT):
                b, k = n // KT, n % KT
                if n == 5 * KT:
                    pool.wait_ge(S["w_used"], 44)
                    nc.gpsimd.memset(HT[:, :], 0.0).then_inc(S["wkv_init"], 1)
                    pool.wait_ge(S["yb_done"], 2)
                if n >= NA:
                    pool.wait_ge(S["ada_used"], n - NA + 1)
                pool.dma_start(slot(NW + n % NA), ada_w[k * P:(k + 1) * P, b * D:(b + 1) * D])\
                    .then_inc(a_slot[n % NA], 16)

            for ps in range(4):
                t, table = ps // 2, (peer_u, peer_v)[ps % 2]
                with pool.Fori(0, 8) as i:
                    pool.wait_ge(S[f"idx{t}_ready"], i + 1)
                    for half in range(2):
                        pool.wait_ge(S["used"], i * 16 + (128 * ps + 8 * half + 1))
                        nc.gpsimd.tensor_copy(estage[:, half, :], eidx[:, t, ds(i * 16 + 8 * half, 8)])\
                            .then_inc(S["staged"], 1)
                        pool.wait_ge(S["staged"], i * 2 + (16 * ps + half + 1))
                        for s in range(NW):
                            pool.wait_ge(S["used"], i * 16 + (128 * ps + 8 * half + s + 1))
                            pool.sem_inc(S["slot_open"], 1)
                            pool.indirect_dma_start(
                                gslot[s], None, table,
                                bass.IndirectOffsetOnAxis(ap=estage[:, half, s:s + 1], axis=0),
                            ).then_inc(g_slot[s], 16)

        @block.tensor
        def _(pe):
            mm, tr = nc.tensor.matmul, nc.tensor.transpose

            def w_group(u0, use, slots, bank, width=512, between=()):
                for kq in range(4):
                    pe.wait_ge(w_slot[slots[kq]], use(kq))
                    w = slot(slots[kq])[:, 0:4 * width].rearrange("p (k n) -> p k n", k=4)
                    for k in range(4):
                        for t in range(NT):
                            kt = 4 * kq + k
                            last = mm(PS[:, bank + t, 0:width], ht3[:, kt, t * P:(t + 1) * P], w[:, k, :],
                                      start=(kt == 0), stop=(kt == KT - 1))
                    last.then_inc(S["w_used"], 1)
                    if kq < len(between):
                        between[kq]()

            pe.wait_ge(S["ld_const"], 48)
            pe.wait_ge(S["x_norm"], NT)
            for r in range(4):
                if r >= 2:
                    pe.wait_ge(S["xT_sb"], r - 1)
                for j in range(4):
                    for t in range(NT):
                        k = 4 * r + j
                        last = tr(PS[:, 2 * (r % 2) + j // 2, (j % 2) * 256 + t * P:(j % 2) * 256 + (t + 1) * P],
                                  h3[:, t, k * P:(k + 1) * P], ident)
                last.then_inc(S["xT_ps"], 1)
            def col_sum(b):
                pe.wait_ge(S["ada_acc"], b + 1)
                if b > 2:
                    pe.wait_ge(S["mod_sb"], b - 1)
                for j in range(KT):
                    c_ = (b % 2) * KT + j
                    last = mm(PS[:, 4, c_:c_ + 1], acc[b % 2][:, j * P:(j + 1) * P], ones[:, 0:1],
                              start=True, stop=True)
                last.then_inc(S["ada_cols"], 1)

            col_sum(0)
            col_sum(1)
            pe.wait_ge(S["h1_ready"], 1)

            for g in range(RG):
                if g >= 2:
                    pe.wait_ge(S["w_evac"], 2 * (g - 1))
                w_group(4 * g, lambda kq, g=g: 16 * ((4 * g + kq) // NW + 1), [(4 * g + kq) % NW for kq in range(4)],
                        2 * (g % 2))
                if g == 3:
                    col_sum(2)
            pe.wait_ge(S["w_evac"], 2 * (RG - 1))
            w_group(24, lambda kq: 16 * 4, [0, 1, 2, 3], 0, LASTW)
            col_sum(3)
            pe.wait_ge(S["w_evac"], 2 * (RG + 1))
            pe.wait_ge(S["mod_sb"], 3)
            for r in range(7):
                if r >= 2:
                    pe.wait_ge(S["pT_sb"], r - 1)
                for j in range(4 * r, min(4 * r + 4, NRT)):
                    w = min(P, RW_IN - j * P)
                    for t in range(NT):
                        jj = j % 4
                        last = tr(PS[0:w, 4 + 2 * (r % 2) + jj // 2, (jj % 2) * 256 + t * P:(jj % 2) * 256 + (t + 1) * P],
                                  ptok[:, t, j * P:j * P + w], ident)
                last.then_inc(S["pT_ps"], 1)

            def gmlp_body(b):
                for half in range(2):
                    pe.wait_ge(S["w_evac"], 16 + 2 * half if b else 14)
                    w_group(28 + 8 * b + 4 * half,
                            (lambda kq, half=half: 16 * ((28 + 8 * b + 4 * half + kq) // NW + 1)),
                            [(4 + 4 * half + kq) % NW for kq in range(4)], 2 * half)

            gmlp_body(0)
            pe.wait_ge(S["ld_small"], 80)
            pe.wait_ge(S["lora_act"], 3)
            col_sum(4)
            pe.wait_ge(S["mod_sb"], 4)
            tr(PS[0:3 * KT, 5, 0:P], MODR[:, 0:3 * KT], ident).then_inc(S["modT_ps"], 1)
            pe.wait_ge(S["modT_sb"], 1)
            for j in range(RT):
                last = mm(PS[:, 4 + j // 2, (j % 2) * 256:(j % 2 + 1) * 256], w2a2[0:64, j * P:(j + 1) * P],
                          m3[0:64, LORA0, :], start=True, stop=True)
            last.then_inc(S["z_ps"], 1)
            pe.wait_ge(S["z_sb"], RT)
            for j in range(RT):
                last = mm(PS[:, 4 + j // 2, (j % 2) * 256:(j % 2 + 1) * 256], w2a2[64:128, j * P:(j + 1) * P],
                          m3[64:128, LORA0, :], start=True, stop=True)
            last.then_inc(S["a_ps"], 1)
            pe.wait_ge(S["a_sb"], RT)
            pe.wait_ge(S["mix_kk"], 1)
            sq = PT[:, 4096:6144]
            for n in range(4):
                last = mm(PS[:, 4 + n, :], blk, sq[:, n * 512:(n + 1) * 512], start=True, stop=True)
            last.then_inc(S["ss_ps"], 1)
            gmlp_body(1)
            pe.wait_ge(S["ss_sb"], 1)
            for c in range(NT):
                for j in range(RT):
                    last = tr(PS[:, 4 + 2 * c + j // 4, (j % 4) * P:(j % 4 + 1) * P],
                              mv[:, j, c * P:(c + 1) * P], ident)
            last.then_inc(S["vt_ps"], 1)
            pe.wait_ge(S["bon_in"], 1)
            pe.wait_ge(S["vt_sb"], 1)
            for c in range(NT):
                for j in range(RT):
                    last = mm(PS[:, 4, (c * RT + j) * 2:(c * RT + j) * 2 + 2], T1[:, j, c * P:(c + 1) * P],
                              blk[:, 0:P:HD], start=True, stop=True)
            last.then_inc(S["bon_ps"], 1)
            pe.wait_ge(S["bon_sb"], 1)
            pe.wait_ge(S["w_evac"], 22)
            pe.wait_ge(S["wkv_in"], 1)
            pe.wait_ge(S["wkv_init"], 3)

            def where(n, pos):
                par, i = pos // 4, pos % 4
                return QUAD * (n // 2) + i, slice(HD * par, HD * (par + 1))

            def head_v(n, pos):
                j, pr = where(n, pos)
                return vtok[:, n % 2, j * P + pr.start:j * P + pr.stop]

            def scores(n):
                tok = slice((n % 2) * P, (n % 2 + 1) * P)
                if n:
                    pe.wait_ge(S["inv_y"], 14 * n)
                for i in range(8):
                    if i >= 6:
                        pe.wait_ge(S["score_sb"], 8 * n + i - 5)
                    for pos in range(2 * (i % 4), 2 * (i % 4) + 2):
                        j, pr = where(n, pos)
                        last = mm(PS[:, i % 6, (pos % 2) * 256:(pos % 2 + 1) * 256],
                                  (bt, mk)[i // 4][pr, j, tok], ar[pr, j, :, tok], start=True, stop=True)
                    last.then_inc(S["score_ps"], 1)
                pe.wait_ge(S["score_sb"], 8 * (n + 1))

            def chain(n, step):
                hf, c = n // 2, n % 2
                tok = slice(c * P, (c + 1) * P)
                if step == 0:
                    pe.wait_ge(S["inv_y"], 14 * (n + 1))
                    pe.wait_ge(S["zg_sb"], 2 * NT)
                    if c == 0:
                        if n:
                            pe.wait_ge(S["y_sb"], 2 * n)
                        for w, src in enumerate((bt, mk)):
                            for i in range(QUAD):
                                last = tr(PS[:, 6 + w, i * P:(i + 1) * P], src[:, QUAD * hf + i, tok], ident)
                        last.then_inc(S["tok_ps"], 1)
                if step == 1:
                    if c == 0:
                        pe.wait_ge(S["tok_sb"], 2 * (hf + 1))
                    else:
                        pe.wait_ge(S["st_sb"], 2 * (hf + 1))
                    for pos in range(8):
                        j, pr = where(n, pos)
                        o_ = PS[:, 6 + pos // 4, (pos % 4) * HD:(pos % 4 + 1) * HD]
                        if c == 1:
                            mm(o_, ar[pr, j, 0, tok], SPR[pr, pos % 4, :], start=True, stop=False)
                        last = mm(o_, KAR[n % 2][:, pos, 0, :], head_v(n, pos), start=(c == 0), stop=True)
                    last.then_inc(S["rhs_ps"], 1)
                if step == 2:
                    pe.wait_ge(S["rhs_sb"], n + 1)
                    for pos in range(8):
                        last = mm(PS[:, 6, pos * HD:(pos + 1) * HD], Yi[n % 2][:, pos, :],
                                  RH[:, pos * HD:(pos + 1) * HD], start=True, stop=True)
                    last.then_inc(S["sa_ps"], 1)
                if step == 3:
                    pe.wait_ge(S["sa_sb"], n + 1)
                    for pos in range(8):
                        j, pr = where(n, pos)
                        o_ = PS[:, 6 + pos // 4, (pos % 4) * HD:(pos % 4 + 1) * HD]
                        if c == 1:
                            mm(o_, ar[pr, j, 1, tok], SPR[pr, pos % 4, :], start=True, stop=False)
                        mm(o_, BAR[n % 2][:, pos, 1, :], SA[:, pos * HD:(pos + 1) * HD], start=(c == 0), stop=False)
                        last = mm(o_, KAR[n % 2][:, pos, 1, :], head_v(n, pos), start=False, stop=True)
                        if pos % 4 == 3:
                            last.then_inc(S["y_ps"], 1)
                if step == 4 and c == 0:
                    pe.wait_ge(S["y_sb"], 2 * n + 2)
                    sa2 = SA.rearrange("p (r i d) -> p i r d", r=2, i=QUAD)
                    for i in range(QUAD):
                        j = QUAD * hf + i
                        o_ = PS[:, 6, i * P:(i + 1) * P]
                        mm(o_, BTok[:, i * P:(i + 1) * P], sa2[:, i, :, :], start=True, stop=False)
                        last = mm(o_, KTok[:, i * P:(i + 1) * P], vtok[:, c, j * P:(j + 1) * P], start=False, stop=True)
                    last.then_inc(S["st_ps"], 1)

            def out_gate(hf):
                pe.wait_ge(S["y_sb"], 4 * hf + 4 if hf else 6)
                if hf == 0:
                    pe.wait_ge(S["st_sb"], 4)
                for t in range(NT):
                    o_ = PS[:, 6 + t, :]
                    mm(o_, m3[:, LORA0 + 1, t * P:(t + 1) * P], g2a[:, hf * 512:(hf + 1) * 512], start=True, stop=False)
                    last = mm(o_, m3[0:32, LORA0 + 2, t * P:(t + 1) * P], g2b[0:32, hf * 512:(hf + 1) * 512],
                              start=False, stop=True)
                last.then_inc(S["gate_ps"], 1)

            def spatial(i):
                t, hh = i // 2, i % 2
                pe.wait_ge(S["vn_ready"], t + 1)
                if i >= 2:
                    pe.wait_ge(S["zg_sb"], i - 1)
                for h in range(4 * hh, 4 * hh + 4):
                    last = mm(PS[:, 6 + i % 2, (h % 4) * P:(h % 4 + 1) * P], wst[:, h, :],
                              h3[:, t, GW + h * P:GW + (h + 1) * P], start=True, stop=True)
                last.then_inc(S["zg_ps"], 1)

            for n in range(4):
                scores(n)
                for l in range(LEVELS):
                    for g in range(2):
                        k = 14 * n + 2 * l + g
                        if l >= 1:
                            pe.wait_ge(S["inv_y"], k - 1)
                        if l >= 2:
                            pe.wait_ge(S["inv_x"], 10 * n + 2 * (l - 2) + g + 1)
                        for pos in range(4 * g, 4 * g + 4):
                            o_ = PS[:, g, (pos % 4) * P:(pos % 4 + 1) * P]
                            if l == 0:
                                last = tr(o_, BAR[n % 2][:, pos, 0, :], ident)
                            else:
                                last = mm(o_, BAR[n % 2][:, pos, 0, :], Q[:, 0, pos, :] if l == 1 else Xi[:, pos, :],
                                          start=True, stop=True)
                        last.then_inc(S["inv_p"], 1)
                    if n == 0 and l >= 3:
                        spatial(l - 3)
                    if n >= 1 and l < 5:
                        chain(n - 1, l)
                    if n == 3 and l == 6:
                        out_gate(0)
                    for g in range(2):
                        pe.wait_ge(S["inv_q"], 14 * n + 2 * l + g + 1)
                        for pos in range(4 * g, 4 * g + 4):
                            if 1 <= l < LEVELS - 1:
                                mm(PS[:, 2 + g, (pos % 4) * P:(pos % 4 + 1) * P], Yi[n % 2][:, pos, :], Q[:, l, pos, :],
                                   start=True, stop=True)
                        for pos in range(4 * g, 4 * g + 4):
                            o_ = PS[:, 4 + g, (pos % 4) * P:(pos % 4 + 1) * P]
                            if l == 0:
                                last = tr(o_, Q[:, 0, pos, :], ident)
                            else:
                                last = mm(o_, Q[:, l, pos, :], Yi[n % 2][:, pos, :], start=True, stop=True)
                        last.then_inc(S["inv_xy"], 1)
            pe.wait_ge(S["gate_used"], 1)
            for step in range(4):
                chain(3, step)
            out_gate(1)

            def transposes(done_ps, done_sb, tile_done=None):
                for r in range(8):
                    if r >= 2:
                        pe.wait_ge(S[done_sb], r - 1)
                    if tile_done and r % 4 == 0:
                        pe.wait_ge(S[tile_done], r // 4 + 1)
                    for j in range(4):
                        k = 4 * (r % 4) + j
                        last = tr(PS[:, 4 + r % 2, j * P:(j + 1) * P], h3[:, r // 4, k * P:(k + 1) * P], ident)
                    last.then_inc(S[done_ps], 1)
                pe.wait_ge(S[done_sb], 8)

            pe.wait_ge(S["ya_done"], NT)
            pe.wait_ge(S["yb_done"], 2)
            transposes("yT_ps", "yT_sb")
            for g in range(4):
                if g >= 2:
                    pe.wait_ge(S["x2_done"], 2 * (g - 1))
                w_group(44 + 4 * g, lambda kq, g=g: 16 * ((44 + 4 * g + kq) // NW + 1),
                        [(4 + 4 * (g % 2) + kq) % NW for kq in range(4)], 2 * (g % 2))
            transposes("h2T_ps", "h2T_sb", "h2_done")
            pe.wait_ge(S["ada_acc"], NB)
            for j in range(KT):
                last = mm(PS[:, 7, j:j + 1], acc[0][:, j * P:(j + 1) * P], ones[:, 0:1], start=True, stop=True)
            last.then_inc(S["ada_cols"], 1)

            def query_t(g):
                pe.wait_ge(S["q_done"], 2 * (g + 1))
                for j in range(4):
                    for t in range(NT):
                        last = tr(PS[:, 4 + j // 2, (j % 2) * 256 + t * P:(j % 2) * 256 + (t + 1) * P],
                                  q3[:, t, g * 512 + j * P:g * 512 + (j + 1) * P], ident)
                last.then_inc(S["qT_ps"], 1)

            def query_scores(g):
                pe.wait_ge(S["qT_sb"], g + 1)
                if g == 0:
                    pe.wait_ge(S["ld_keys"], 16)
                    pe.wait_ge(S["modT_sb"], 2)
                else:
                    pe.wait_ge(S["sc_used"], g)
                    pe.wait_ge(S["sc1_sb"], g)
                for t in range(NT):
                    for j in range(4):
                        last = mm(PS[:, 6 + t, j * P:(j + 1) * P], qt[g % 2][:, j, t * P:(t + 1) * P],
                                  keyst[:, 4 * g + j, :], start=True, stop=True)
                last.then_inc(S["sc_ps"], 1)

            for g in range(4):
                if g < 2:
                    pe.wait_ge(S["x2_done"], 8)
                else:
                    pe.wait_ge(S["q_done"], 2 * (g - 1))
                w_group(60 + 4 * g, lambda kq, g=g: 16 * ((60 + 4 * g + kq) // NW + 1),
                        [(4 + 4 * (g % 2) + kq) % NW for kq in range(4)], 2 * (g % 2),
                        between=[lambda: query_t(g - 1), lambda: query_scores(g - 1)] if g else ())
                if g == 0:
                    pe.wait_ge(S["mod_sb"], 5)
                    tr(PS[0:KT, 7, P:2 * P], MODR[:, 3 * KT:4 * KT], ident).then_inc(S["modT_ps"], 1)
            query_t(3)
            query_scores(3)

        @block.scalar
        def _(act):
            act_ = nc.scalar.activation
            act.wait_ge(S["ld_const"], 48)
            act_(col("c"), col("c"), ACT.Silu).then_inc(S["silu_c"], 1)
            act.wait_ge(S["ld_x"], 16)
            for t in range(NT):
                act_(h3[:, t, :], x3[:, t, :], ACT.Square, accum_out=ST[:, t:t + 1]).then_inc(S["x_sumsq"], 1)
            act.wait_ge(S["x_rstd"], 1)
            act_(ST[:, 2:4], ST[:, 2:4], ACT.Sqrt).then_inc(S["x_rstd"], 1)
            act.wait_ge(S["x_rstd"], 3)
            act.wait_ge(S["x_sumsq"], NT)
            for t in range(NT):
                act_(h3[:, t, :], x3[:, t, :], ACT.Copy, scale=ST[:, 4 + t:5 + t]).then_inc(S["x_norm"], 1)
            for r in range(4):
                act.wait_ge(S["xT_ps"], r + 1)
                b = 2 * (r % 2)
                act_(HT[:, r * 1024:(r + 1) * 1024].rearrange("p (b n) -> p b n", b=2), PS[:, b:b + 2, :], ACT.Copy)\
                    .then_inc(S["xT_sb"], 1)
            for g in range(RG + 1):
                act.wait_ge(S["w_used"], 4 * (g + 1))
                w = 512 if g < RG else LASTW
                for t in range(NT):
                    act_(ptok[:, t, g * 512:g * 512 + w], PS[:, 2 * (g % 2) + t, 0:w], ACT.Copy).then_inc(S["w_evac"], 1)
            for r in range(7):
                act.wait_ge(S["pT_ps"], r + 1)
                for j in range(4 * r, min(4 * r + 4, NRT), 2):
                    b = 4 + 2 * (r % 2) + (j % 4) // 2
                    if j + 1 < NRT:
                        last = act_(pt3[:, j:j + 2, 1:SEQ + 1], PS[:, b, :].rearrange("p (j s) -> p j s", j=2), ACT.Copy)
                    else:
                        last = act_(pt3[0:32, j, 1:SEQ + 1], PS[0:32, b, 0:SEQ], ACT.Copy)
                last.then_inc(S["pT_sb"], 1)
            act.wait_ge(S["mix_lora"], 1)
            act_(m3[0:64, LORA0, :], m3[0:64, LORA0, :], ACT.Tanh).then_inc(S["lora_act"], 1)
            act_(m3[:, LORA0 + 1, :], m3[:, LORA0 + 1, :], ACT.Sigmoid).then_inc(S["lora_act"], 1)
            act_(m3[0:32, LORA0 + 2, :], m3[0:32, LORA0 + 2, :], ACT.Sigmoid).then_inc(S["lora_act"], 1)

            def gelu_evac(b):
                for half in range(2):
                    act.wait_ge(S["w_used"], 28 + 8 * b + 4 * (half + 1))
                    for t in range(NT):
                        act_(h3[:, t, b * GW + half * 512:b * GW + (half + 1) * 512], PS[:, 2 * half + t, :], ACT.Gelu)\
                            .then_inc(S["w_evac"], 1)

            gelu_evac(0)
            act.wait_ge(S["modT_ps"], 1)
            act_(MODT[:, :], PS[0:3 * KT, 5, 0:P], ACT.Copy).then_inc(S["modT_sb"], 1)
            act.wait_ge(S["modT_sb"], 1)
            act.dma_start(mod_dram[0:3 * KT, :], MODT[:, :]).then_inc(S["ada_stored"], 16)
            act.wait_ge(S["z_ps"], 1)
            for j in range(RT):
                act_(T1[:, j, :], PS[:, 4 + j // 2, (j % 2) * 256:(j % 2 + 1) * 256], ACT.Sigmoid,
                     bias=col("w0", j, j + 1)).then_inc(S["z_sb"], 1)
            act.wait_ge(S["a_ps"], 1)
            for j in range(RT):
                act_(a_ft[:, j, :], PS[:, 4 + j // 2, (j % 2) * 256:(j % 2 + 1) * 256], ACT.Sigmoid,
                     bias=col("a0", j, j + 1)).then_inc(S["a_sb"], 1)
            act.wait_ge(S["ss_ps"], 1)
            act_(PT[:, 4096:6144].rearrange("p (b n) -> p b n", b=4), PS[:, 4:8, :], ACT.Sqrt).then_inc(S["ss_sb"], 1)
            act.wait_ge(S["l_ready"], 1)
            act_(T3f, T3f, ACT.Exp).then_inc(S["l_exp"], 1)
            act_(T1f, T2f, ACT.Exp).then_inc(S["l_exp"], 1)
            act_(FC[:, :], FC[:, :], ACT.Exp).then_inc(S["l_exp"], 1)
            act.wait_ge(S["l_exp"], 2)
            act_(T2f, T2f, ACT.Exp, scale=-1.0).then_inc(S["l_exp"], 1)
            gelu_evac(1)
            act_(RING[:, 3 * SLOT:3 * SLOT + LEVELS * 1024].rearrange("p (m t) -> p m t", t=P),
                 ident.unsqueeze(1).broadcast_to([P, LEVELS * 8, P]), ACT.Copy).then_inc(S["wkv_init"], 1)
            act.wait_ge(S["vt_ps"], 1)
            act.wait_ge(S["k2_done"], 1)
            act_(T3f.rearrange("p (b n) -> p b n", b=4), PS[:, 4:8, :], ACT.Copy).then_inc(S["vt_sb"], 1)
            act.wait_ge(S["bon_ps"], 1)
            act_(BON[:, :, :].rearrange("p c h -> p (c h)"), PS[:, 4, 0:32], ACT.Copy).then_inc(S["bon_sb"], 1)

            def chain(n, step):
                hf, c = n // 2, n % 2
                if step == 0 and c == 0:
                    act.wait_ge(S["tok_ps"], hf + 1)
                    act_(BTok, PS[:, 6, :], ACT.Copy).then_inc(S["tok_sb"], 1)
                    act_(KTok, PS[:, 7, :], ACT.Copy).then_inc(S["tok_sb"], 1)
                if step == 1:
                    act.wait_ge(S["rhs_ps"], n + 1)
                    act_(RH.rearrange("p (b n) -> p b n", b=2), PS[:, 6:8, 0:256], ACT.Copy).then_inc(S["rhs_sb"], 1)
                if step == 2:
                    act.wait_ge(S["sa_ps"], n + 1)
                    act_(SA, PS[:, 6, :], ACT.Copy).then_inc(S["sa_sb"], 1)
                if step == 3:
                    for par in range(2):
                        act.wait_ge(S["y_ps"], 2 * n + par + 1)
                        dst = ytok[:, c, QUAD * hf * P:QUAD * (hf + 1) * P].rearrange("p (i d) -> p i d", i=QUAD)
                        act_(dst[:, :, HD * par:HD * (par + 1)],
                             PS[:, 6 + par, 0:256].rearrange("p (i d) -> p i d", i=QUAD), ACT.Copy).then_inc(S["y_sb"], 1)

            for n in range(4):
                for l in range(LEVELS):
                    if n == 0 and l == 0:
                        act.wait_ge(S["ln_var"], 1)
                        act_(ST[:, 12:14], ST[:, 12:14], ACT.Sqrt).then_inc(S["ln_std"], 1)
                    if n == 1 and l == 5:
                        act.wait_ge(S["zg_sb"], 2 * NT)
                        for t in range(NT):
                            act_(h3[:, t, GW:2 * GW], h3[:, t, 0:GW], ACT.Square, accum_out=ST[:, 16 + t:17 + t])\
                                .then_inc(S["ya_sumsq"], 1)
                    if n == 2 and l == 0:
                        act.wait_ge(S["ya_std"], 1)
                        act_(ST[:, 18:20], ST[:, 18:20], ACT.Sqrt).then_inc(S["ya_std"], 1)
                    if n == 3 and l == 3:
                        act.wait_ge(S["gn_var"], 1)
                        act_(GST[:, 1, 0:16], GST[:, 1, 0:16], ACT.Sqrt).then_inc(S["gn_std"], 1)
                    if n >= 1 and l < 4:
                        chain(n - 1, l)
                    if 1 <= l < LEVELS - 1:
                        for g in range(2):
                            act.wait_ge(S["inv_xy"], 14 * n + 2 * l + g + 1)
                            act_(Xi[:, 4 * g:4 * g + 4, :].rearrange("p h t -> p (h t)"), PS[:, 2 + g, :], ACT.Copy)\
                                .then_inc(S["inv_x"], 1)
            for step in range(4):
                chain(3, step)
            act.wait_ge(S["gn_var"], 2)
            act_(GST[:, 1, 16:32], GST[:, 1, 16:32], ACT.Sqrt).then_inc(S["gn_std"], 1)

            def evac_t(done_ps, done_sb):
                for r in range(8):
                    act.wait_ge(S[done_ps], r + 1)
                    act_(ht3[:, 4 * (r % 4):4 * (r % 4) + 4, (r // 4) * P:(r // 4 + 1) * P],
                         PS[:, 4 + r % 2, :].rearrange("p (j s) -> p j s", j=4), ACT.Copy).then_inc(S[done_sb], 1)

            evac_t("yT_ps", "yT_sb")
            for g in range(4):
                act.wait_ge(S["x2_done"], 2 * (g + 1))
                for t in range(NT):
                    cs = slice(g * 512, (g + 1) * 512)
                    act_(h3[:, t, cs], x3[:, t, cs], ACT.Square, accum_out=SSQ[:, t, g:g + 1]).then_inc(S["x2_sumsq"], 1)
            act.wait_ge(S["x2_std"], 1)
            act_(ST[:, 22:24], ST[:, 22:24], ACT.Sqrt).then_inc(S["x2_std"], 1)
            evac_t("h2T_ps", "h2T_sb")
            def query_out(g):
                act.wait_ge(S["qT_ps"], g + 1)
                if g >= 2:
                    act.wait_ge(S["sc_ps"], g - 1)
                act_(qt[g % 2].rearrange("p (b j) s -> p b (j s)", b=2), PS[:, 4:6, :], ACT.Copy).then_inc(S["qT_sb"], 1)
                act.wait_ge(S["sc_ps"], g + 1)
                act_(sc1[:, g * 512:(g + 1) * 512], PS[:, 7, :], ACT.Copy).then_inc(S["sc1_sb"], 1)

            for g in range(4):
                act.wait_ge(S["w_used"], 60 + 4 * (g + 1))
                for t in range(NT):
                    act_(q3[:, t, g * 512:(g + 1) * 512], PS[:, 2 * (g % 2) + t, :], ACT.Copy).then_inc(S["q_done"], 1)
                if g == 0:
                    act.wait_ge(S["modT_ps"], 2)
                    act.wait_ge(S["ada_stored"], 16)
                    act_(MODT[0:KT, :], PS[0:KT, 7, P:2 * P], ACT.Copy).then_inc(S["modT_sb"], 1)
                    act.wait_ge(S["modT_sb"], 2)
                    act.dma_start(mod_dram[3 * KT:4 * KT, :], MODT[0:KT, :]).then_inc(S["ada_stored"], 16)
                query_out(g)
            for t in range(NT):
                act.wait_ge(S["sm_in"], t + 1)
                act_(gate[:, t, :], gate[:, t, :], ACT.Exp).then_inc(S["sm_exp"], 1)
                act.wait_ge(S["dots_done"], t + 1)
                act_(dots[:, t, :], dots[:, t, :], ACT.Gelu).then_inc(S["act_ready"], 1)
            act.wait_ge(S["outs_sumsq"], 2)
            for t in range(NT):
                act_(h3[:, t, :], x3[:, t, :], ACT.Square, accum_out=ST[:, 28 + t:29 + t]).then_inc(S["outs_sumsq"], 1)
            act.wait_ge(S["outs_std"], 1)
            act_(ST[:, 30:32], ST[:, 30:32], ACT.Sqrt).then_inc(S["outs_std"], 1)

        @block.vector
        def _(dve):
            v = nc.vector
            own = Steps(dve, S["dve_own"])

            def bc(ap, n):
                return ap.unsqueeze(2).broadcast_to([P, ap.shape[1], n])

            def mean_eps(out_, in_, width, eps, sem_=None):
                own(v.tensor_scalar(out_, in_, 1.0 / width, eps, ALU.mult, ALU.add), sem_)

            dve.wait_ge(S["x_sumsq"], NT)
            mean_eps(ST[:, 2:4], ST[:, 0:2], D, 1e-6, S["x_rstd"])
            dve.wait_ge(S["x_rstd"], 2)
            v.reciprocal(ST[:, 4:6], ST[:, 2:4]).then_inc(S["x_rstd"], 1)
            dve.wait_ge(S["ld_const"], 48)

            def ada_units(b, a, k0, k1):
                for k in range(k0, k1):
                    n = b * KT + k
                    dve.wait_ge(a_slot[n % NA], 16 * (n // NA + 1))
                    w, ck = slot(NW + n % NA), col("c", k, k + 1)
                    if k == 0:
                        v.tensor_scalar(a, w, ck, None, ALU.mult).then_inc(S["ada_used"], 1)
                    else:
                        v.scalar_tensor_tensor(a, w, ck, a, ALU.mult, ALU.add).then_inc(S["ada_used"], 1)
                    dve.wait_ge(S["ada_used"], n + 1)

            def ada(b):
                if b >= 2:
                    dve.wait_ge(S["ada_cols"], b - 1)
                ada_units(b, acc[b % 2], 0, KT)
                dve.sem_inc(S["ada_acc"], 1)

            def mod_cols(b):
                dve.wait_ge(S["ada_cols"], b + 1)
                own(v.tensor_tensor(MODR[:, (b - 2) * KT:(b - 1) * KT], PS[:, 4, (b % 2) * KT:(b % 2 + 1) * KT],
                                    col("adab", b * KT, (b + 1) * KT), ALU.add), S["mod_sb"])

            dve.wait_ge(S["silu_c"], 1)
            dve.wait_ge(S["ld_const"], 48)
            own(v.tensor_copy(MASK[:, :, :], mask32))
            v.memset(pt3[:, :, 0:1], 0.0).then_inc(S["pt_zero"], 1)
            ada(0)
            ada(1)
            dve.wait_ge(S["ada_cols"], 2)
            own(v.tensor_tensor(MODC[:, :], PS[:, 4, 0:32], col("adab", 0, 32), ALU.add), S["mod_sb"])
            own(v.scalar_tensor_tensor(MODC[:, 16:32], MODC[:, 16:32], 1.0, col("g1"), ALU.add, ALU.mult))
            dve.wait_ge(S["xT_sb"], 4)
            for k in range(KT):
                last = v.tensor_scalar(ht3[:, k, :], ht3[:, k, :], MODC[:, 16 + k:17 + k], MODC[:, k:k + 1], ALU.mult, ALU.add)
                if k < KT - 1:
                    own(last)
            last.then_inc(S["h1_ready"], 1)
            ada(2)
            ada(3)
            mod_cols(2)
            ada_units(4, acc[0], 0, KT // 2)
            mod_cols(3)
            ada_units(4, acc[0], KT // 2, KT)
            dve.sem_inc(S["ada_acc"], 1)

            dve.wait_ge(S["pt_zero"], 1)
            dve.wait_ge(S["pT_sb"], 7)

            def mix(j0, j1, parts=P, sem_=None):
                m, cur, prev = m3[0:parts, j0:j1, :], pt3[0:parts, j0:j1, 1:SEQ + 1], pt3[0:parts, j0:j1, 0:SEQ]
                own(v.tensor_tensor(m, prev, cur, ALU.subtract))
                mu = COL[0:parts, COLS["mu"][0] + j0:COLS["mu"][0] + j1].unsqueeze(2).broadcast_to([parts, j1 - j0, SEQ])
                own(v.tensor_tensor(m, m, mu, ALU.mult))
                own(v.tensor_tensor(m, m, cur, ALU.add), sem_)

            mix(NRT - 1, NRT, 32)
            mix(LORA0, NRT - 1, P, S["mix_lora"])
            mix(RT, 2 * RT)
            own(v.tensor_tensor(kk_ft, mk, bc(col("kk"), SEQ), ALU.mult))
            mix(0, RT)
            mix(2 * RT, 3 * RT)
            own(v.tensor_tensor(bt, kk_ft, kk_ft, ALU.mult), S["mix_kk"])
            mod_cols(4)
            own(v.tensor_scalar(OMK[:, :], col("ka"), -1.0, 1.0, ALU.mult, ALU.add))
            dve.wait_ge(S["z_sb"], RT)
            own(v.tensor_scalar(T1f, T1f, DECAY, None, ALU.mult))
            for j in range(RT):
                for c in range(NT):
                    own(v.tensor_tensor_scan(T2[:, j, c * P:(c + 1) * P], ones, T1[:, j, c * P:(c + 1) * P], 0.0,
                                             ALU.mult, ALU.add))
            t2c = T2f.rearrange("p (m s) -> p m s", s=P)
            own(v.tensor_copy(MID[:, :, :].rearrange("p j c -> p (j c)"), t2c[:, :, P // 2 - 1]))
            own(v.tensor_tensor(t2c, t2c, bc(MID[:, :, :].rearrange("p j c -> p (j c)"), P), ALU.subtract))
            own(v.tensor_tensor(FC[:, :], T2[:, :, P - 1], MID[:, :, 1], ALU.add))
            own(v.tensor_tensor(T3f, T2f, T1f, ALU.subtract), S["l_ready"])
            dve.wait_ge(S["ss_sb"], 1)
            own(v.tensor_scalar(bt, bt, 1e-12, None, ALU.max))
            own(v.reciprocal(bt, bt))
            own(v.tensor_tensor(kk_ft, kk_ft, bt, ALU.mult))
            dve.wait_ge(S["l_exp"], 1)
            own(v.scalar_tensor_tensor(ar[:, :, 0, :], kk_ft, -1.0, T3, ALU.mult, ALU.mult))
            dve.wait_ge(S["a_sb"], RT)
            own(v.tensor_tensor(T3, a_ft, bc(col("ka"), SEQ), ALU.mult))
            own(v.tensor_tensor(T3, T3, bc(OMK[:, :], SEQ), ALU.add))
            own(v.tensor_tensor(mk, mk, T3, ALU.mult), S["k2_done"])
            dve.wait_ge(S["l_exp"], 2)
            own(v.tensor_tensor(ar[:, :, 1, :], mr, T1, ALU.mult))
            dve.wait_ge(S["l_exp"], 4)
            own(v.tensor_tensor(T1, mr, mk, ALU.mult))
            own(v.tensor_tensor(T1, T1, bc(col("rk"), SEQ), ALU.mult), S["bon_in"])
            own(v.tensor_tensor(a_ft, a_ft, kk_ft, ALU.mult))
            own(v.tensor_tensor(bt, a_ft, T2, ALU.mult))
            own(v.tensor_tensor(mk, mk, T2, ALU.mult), S["wkv_in"])

            def gmlp_stats():
                dve.wait_ge(S["ld_small"], 80)
                own(v.memset(wst[64:P, :, 0:64], 0.0))
                dve.wait_ge(S["w_evac"], 22)
                for t in range(NT):
                    for i in range(2):
                        own(v.bn_stats(ST[:, 32 + 6 * i:38 + 6 * i], h3[:, t, GW + 512 * i:GW + 512 * (i + 1)]))
                    own(v.bn_aggr(ST[:, 8 + 2 * t:10 + 2 * t], ST[:, 32:44]))
                    own(v.tensor_scalar(ST[:, 12 + t:13 + t], ST[:, 9 + 2 * t:10 + 2 * t], 1e-5, None, ALU.add))
                dve.sem_inc(S["ln_var"], 1)

            def gmlp_norm(t):
                if t == 0:
                    dve.wait_ge(S["ln_std"], 1)
                    own(v.reciprocal(ST[:, 14:16], ST[:, 12:14]))
                    dve.wait_ge(S["ld_vrow"], 48)
                vv = h3[:, t, GW:2 * GW]
                own(v.tensor_scalar(vv, vv, ST[:, 8 + 2 * t:9 + 2 * t], ST[:, 14 + t:15 + t], ALU.subtract, ALU.mult))
                own(v.tensor_tensor(vv, vv, vgr, ALU.mult))
                own(v.tensor_tensor(vv, vv, vbr, ALU.add), S["vn_ready"])

            def gmlp_gate(i):
                t, hh = i // 2, i % 2
                dve.wait_ge(S["zg_ps"], i + 1)
                for h in range(4 * hh, 4 * hh + 4):
                    u_ = h3[:, t, h * P:(h + 1) * P]
                    last = v.scalar_tensor_tensor(u_, PS[:, 6 + i % 2, (h % 4) * P:(h % 4 + 1) * P],
                                                  col("bs", h, h + 1), u_, ALU.add, ALU.mult)
                    own(last, S["zg_sb"] if h % 4 == 3 else None)

            def gmlp_out(part):
                if part == 0:
                    dve.wait_ge(S["ya_sumsq"], NT)
                    mean_eps(ST[:, 18:20], ST[:, 16:18], GW, 1e-6, S["ya_std"])
                else:
                    dve.wait_ge(S["ya_std"], 2)
                    own(v.reciprocal(ST[:, 24:26], ST[:, 18:20]))
                    for t in range(NT):
                        ya = h3[:, t, 0:GW]
                        own(v.scalar_tensor_tensor(ya, ya, ST[:, 24 + t:25 + t], ogr, ALU.mult, ALU.mult), S["ya_done"])

            def group_norm(hf, part):
                fs = slice(hf * 512, (hf + 1) * 512)
                y3, s3 = ytok[:, :, fs], acc[0].rearrange("p (t f) -> p t f", t=NT)[:, :, fs]

                def per_head(ap):
                    return ap.rearrange("p t (h d) -> p t h d", d=HD)

                def stat(i):
                    return GST[:, i, hf * 16:(hf + 1) * 16].rearrange("p (t h) -> p t h", t=NT)

                def over_d(ap):
                    return ap.unsqueeze(3).broadcast_to([P, NT, 8, HD])

                if part == 0:
                    dve.wait_ge(S["y_sb"], 4 * (hf + 1))
                    own(v.tensor_reduce(stat(0), per_head(y3), AX.X, ALU.add))
                    own(v.tensor_scalar(stat(0), stat(0), 1.0 / HD, None, ALU.mult))
                    own(v.tensor_tensor(per_head(y3), per_head(y3), over_d(stat(0)), ALU.subtract))
                if part == 1:
                    own(v.tensor_tensor(s3, y3, y3, ALU.mult))
                    own(v.tensor_reduce(stat(1), per_head(s3), AX.X, ALU.add))
                    mean_eps(stat(1), stat(1), HD, 64e-5, S["gn_var"])
                if part == 2:
                    own(v.tensor_tensor(per_head(s3), per_head(vtok[:, :, fs]),
                                        over_d(BON[:, :, 8 * hf:8 * hf + 8]), ALU.mult))
                    dve.wait_ge(S["gn_std"], hf + 1)
                    own(v.reciprocal(stat(2), stat(1)))
                if part == 3:
                    own(v.tensor_tensor(per_head(y3), per_head(y3), over_d(stat(2)), ALU.mult))
                    dve.wait_ge(S["ld_lnrow"], 32)
                    own(v.tensor_tensor(y3, y3, lngr[:, fs].unsqueeze(1).broadcast_to([P, NT, 512]), ALU.mult))
                if part == 4:
                    own(v.tensor_tensor(y3, y3, lnbr[:, fs].unsqueeze(1).broadcast_to([P, NT, 512]), ALU.add))
                    own(v.tensor_tensor(y3, y3, s3, ALU.add))
                if part == 5:
                    dve.wait_ge(S["gate_ps"], hf + 1)
                    for t in range(NT):
                        own(v.tensor_tensor(h3[:, t, GW + hf * 512:GW + (hf + 1) * 512], y3[:, t, :], PS[:, 6 + t, :],
                                            ALU.mult))
                    dve.sem_inc(S["gate_used"], 1)
                    dve.sem_inc(S["yb_done"], 1)

            fill = {(0, 0): [lambda: gmlp_norm(0)], (0, 1): [lambda: gmlp_norm(1)],
                    (2, 0): [lambda: gmlp_out(1)],
                    (3, 0): [lambda: group_norm(0, 0)], (3, 1): [lambda: group_norm(0, 1)],
                    (3, 3): [lambda: group_norm(0, 2)], (3, 4): [lambda: group_norm(0, 3)],
                    (3, 5): [lambda: group_norm(0, 4)], (3, 6): [lambda: group_norm(0, 5)]}
            dve.wait_ge(S["w_used"], 44)
            v.memset(RING[:, 0:2 * SLOT], 0.0).then_inc(S["wkv_init"], 1)
            strict_incl = MASK[:, LEVELS:LEVELS + 2, :].rearrange("p w t -> p (w t)")
            gmlp_stats()
            dve.wait_ge(S["wkv_init"], 3)
            for n in range(4):
                hf, c = n // 2, n % 2
                for i in range(8):
                    dve.wait_ge(S["score_ps"], 8 * n + i + 1)
                    dst = (BAR, KAR)[i // 4][n % 2][:, 2 * (i % 4):2 * (i % 4) + 2, :, :].rearrange("p h w t -> p h (w t)")
                    own(v.copy_predicated(dst, strict_incl.unsqueeze(1).broadcast_to([P, 2, 2 * P]),
                                          PS[:, i % 6, :].rearrange("p (h t) -> p h t", h=2)), S["score_sb"])
                for l in range(LEVELS):
                    mask = MASK[:, l, :].unsqueeze(1).broadcast_to([P, 4, P])
                    for g in range(2):
                        dve.wait_ge(S["inv_p"], 14 * n + 2 * l + g + 1)
                        own(v.copy_predicated(Q[:, l, 4 * g:4 * g + 4, :], mask,
                                              PS[:, g, :].rearrange("p (h t) -> p h t", h=4)), S["inv_q"])
                    if n == 0 and l >= 3:
                        gmlp_gate(l - 3)
                    if n == 1 and l == 6:
                        gmlp_out(0)
                    if n in (1, 3) and l == 4:
                        dve.wait_ge(S["st_ps"], hf + 1)
                        for par in range(2):
                            pr = slice(HD * par, HD * (par + 1))
                            fc = FC[pr, QUAD * hf:QUAD * (hf + 1)].unsqueeze(2).broadcast_to([HD, QUAD, HD])
                            own(v.tensor_tensor(SPR[pr, :, :],
                                                PS[pr, 6, :].rearrange("p (i v) -> p i v", i=QUAD)[:, :, pr], fc, ALU.mult),
                                S["st_sb"])
                    for g in range(2):
                        dve.wait_ge(S["inv_xy"], 14 * n + 2 * l + g + 1)
                        own(v.tensor_copy(Yi[n % 2][:, 4 * g:4 * g + 4, :].rearrange("p h t -> p (h t)"), PS[:, 4 + g, :]),
                            S["inv_y"])
                    for piece in fill.get((n, l), ()):
                        piece()
            for part in range(6):
                group_norm(1, part)

            dve.wait_ge(S["ld_x2"], 16)
            dve.wait_ge(S["ld_rows"], 64)
            own(v.scalar_tensor_tensor(a2b, a2b, 1.0, n2gr, ALU.add, ALU.mult))
            for g in range(4):
                ada_units(5, acc[0], 4 * g, 4 * g + 4)
                cs = slice(g * 512, (g + 1) * 512)
                dve.wait_ge(S["w_used"], 44 + 4 * (g + 1))
                for t in range(NT):
                    own(v.tensor_tensor(xtmp, PS[:, 2 * (g % 2) + t, :], gt1b[:, cs], ALU.mult))
                    own(v.tensor_tensor(x3[:, t, cs], x3[:, t, cs], xtmp, ALU.add), S["x2_done"])
            dve.sem_inc(S["ada_acc"], 1)
            dve.wait_ge(S["x2_sumsq"], 8)
            own(v.tensor_reduce(ST[:, 20:22], SSQ[:, :, :], AX.X, ALU.add))
            mean_eps(ST[:, 22:24], ST[:, 20:22], D, 1e-6, S["x2_std"])
            dve.wait_ge(S["x2_std"], 2)
            own(v.reciprocal(ST[:, 26:28], ST[:, 22:24]))
            for t in range(NT):
                own(v.scalar_tensor_tensor(h3[:, t, :], x3[:, t, :], ST[:, 26 + t:27 + t], a2b, ALU.mult, ALU.mult))
                own(v.tensor_tensor(h3[:, t, :], h3[:, t, :], sh2b, ALU.add), S["h2_done"])
            dve.wait_ge(S["ada_cols"], 6)
            own(v.tensor_tensor(MODR[:, 3 * KT:4 * KT], PS[:, 7, 0:KT], col("adab", 5 * KT, 6 * KT), ALU.add), S["mod_sb"])

            def top16(values, val, idx, work):
                own(v.max(val[:, 0:8], values))
                own(v.max_index(idx[:, 0:8], val[:, 0:8], values))
                own(v.match_replace(work, val[:, 0:8], values, BIG))
                own(v.max(val[:, 8:16], work))
                own(v.max_index(idx[:, 8:16], val[:, 8:16], work))

            iota = col("iota").unsqueeze(1).broadcast_to([P, GS, TOPK])

            def select(g, t):
                src = PS[:, 6, :] if t == 0 else sc1[:, g * 512:(g + 1) * 512]
                for j in range(4):
                    top16(src[:, j * P:(j + 1) * P], tops[:, j, :], topi[:, j, :], scr[:, 0:P])
                if t == 0:
                    dve.sem_inc(S["sc_used"], 1)
                tp = tops.rearrange("p (h w) k -> p h w k", w=2)
                own(v.tensor_copy(topf, topi.rearrange("p g k -> p (g k)")))
                tf = topf.rearrange("p (h w k) -> p h w k", h=2, w=2)
                own(v.tensor_tensor(cand, tp[:, :, 0, :].unsqueeze(3).broadcast_to([P, 2, TOPK, TOPK]),
                                    tp[:, :, 1, :].unsqueeze(2).broadcast_to([P, 2, TOPK, TOPK]), ALU.add))
                for h in range(2):
                    top16(cand[:, h, :, :].rearrange("p a b -> p (a b)"),
                          sfin[:, t, g * GS + h * TOPK:g * GS + (h + 1) * TOPK], pos[:, h * TOPK:(h + 1) * TOPK], scr)
                for w in range(2):
                    if w == 0:
                        own(v.tensor_scalar(posp, pos, 4, None, ALU.logical_shift_right))
                    else:
                        own(v.tensor_scalar(posp, pos, 15, None, ALU.bitwise_and))
                    own(v.tensor_copy(posf, posp))
                    oh = onehot.rearrange("p h a b -> p (h a) b")
                    own(v.tensor_tensor(oh, iota, bc(posf, TOPK), ALU.is_equal))
                    own(v.tensor_tensor(onehot, onehot, tf[:, :, w, :].unsqueeze(2).broadcast_to([P, 2, TOPK, TOPK]),
                                        ALU.mult))
                    own(v.tensor_reduce(isel[:, w, :], oh, AX.X, ALU.add))
                own(v.scalar_tensor_tensor(isel[:, 0, :], isel[:, 0, :], float(NK), isel[:, 1, :], ALU.mult, ALU.add))
                own(v.tensor_copy(eidx[:, t, g * GS:(g + 1) * GS], isel[:, 0, :]))
                dve.sem_inc(S[f"idx{t}_ready"], 2)

            def softmax_in(t):
                sh = sfin[:, t, :].rearrange("p (h k) -> p h k", h=NH)
                gt = gate[:, t, :].rearrange("p (h k) -> p h k", h=NH)
                own(v.tensor_tensor(gt, sh, bc(sh[:, :, 0], TOPK), ALU.subtract), S["sm_in"])

            def softmax_out(t):
                gt = gate[:, t, :].rearrange("p (h k) -> p h k", h=NH)
                dve.wait_ge(S["sm_exp"], t + 1)
                own(v.tensor_reduce(ST[:, 44:52], gt, AX.X, ALU.add))
                own(v.reciprocal(ST[:, 52:60], ST[:, 44:52]))
                own(v.tensor_tensor(gt, gt, bc(ST[:, 52:60], TOPK), ALU.mult))

            dve.sem_inc(S["used"], 3)
            for g in range(4):
                dve.wait_ge(S["sc_ps"], g + 1)
                if g == 2:
                    dve.sem_inc(S["used"], 4)
                if g == 3:
                    dve.sem_inc(S["used"], 1)
                select(g, 0)
                if g in (0, 1):
                    dve.wait_ge(S["sc1_sb"], g + 1)
                    select(g, 1)
            softmax_in(0)

            def experts(ps, i0, i1):
                t = ps // 2
                with dve.Fori(i0, i1) as i:
                    for m in range(16):
                        s, half = m % NW, m // NW
                        dve.wait_ge(g_slot[s], i * 32 + 16 * (16 * ps + half + 1))
                        if ps % 2 == 0:
                            v.scalar_tensor_tensor(gslot[s], gslot[s], 1.0, h3[:, t, :], ALU.mult, ALU.mult,
                                                   accum_out=dots[:, t, ds(i * 16 + m, 1)]).then_inc(S["used"], 1)
                        else:
                            v.scalar_tensor_tensor(acc[t], gslot[s], dots[:, t, ds(i * 16 + m, 1)], acc[t],
                                                   ALU.mult, ALU.add).then_inc(S["used"], 1)
                        dve.wait_ge(S["used"], i * 16 + (NW + 128 * ps + m + 1))

            def weights(t):
                dve.sem_inc(S["dots_done"], 1)
                dve.wait_ge(S["act_ready"], t + 1)
                own(v.tensor_tensor(dots[:, t, :], dots[:, t, :], gate[:, t, :], ALU.mult))
                own(v.memset(acc[t], 0.0))

            experts(0, 0, 4)
            dve.wait_ge(S["sc1_sb"], 4)
            select(2, 1)
            softmax_out(0)
            experts(0, 4, 8)
            weights(0)
            experts(1, 0, 4)
            select(3, 1)
            softmax_in(1)
            experts(1, 4, 8)
            experts(2, 0, 8)
            softmax_out(1)
            weights(1)
            experts(3, 0, 8)
            dve.wait_ge(S["ld_fin"], 32)
            for t in range(NT):
                own(v.tensor_tensor(acc[t], acc[t], gt2b, ALU.mult))
                own(v.tensor_tensor(x3[:, t, :], x3[:, t, :], acc[t], ALU.add), S["outs_sumsq"])
            dve.wait_ge(S["outs_sumsq"], 4)
            mean_eps(ST[:, 30:32], ST[:, 28:30], D, 1e-6)
            dve.sem_inc(S["outs_std"], 1)
            dve.wait_ge(S["outs_std"], 2)
            own(v.reciprocal(ST[:, 60:62], ST[:, 30:32]))
            for t in range(NT):
                own(v.scalar_tensor_tensor(h3[:, t, :], x3[:, t, :], ST[:, 60 + t:61 + t], fgr, ALU.mult, ALU.mult),
                    S["out_ready"])


_COLS = [("c", 16), ("ada_b", 96), ("norm1_g", 16), ("rwkv_mu", 27), ("rwkv_w0", 8), ("rwkv_a0", 8),
         ("rwkv_kk", 8), ("rwkv_ka", 8), ("rwkv_rk", 8), ("gmlp_bs", 8)]


def kernel(**inputs):
    import concourse.bacc as _bacc
    from concourse.bass_utils import run_bass_kernel_spmd as _run

    a = {k: np.asarray(val) for k, val in inputs.items()}
    f = np.float32

    parts = []
    for name, w in _COLS:
        flat = a[name].reshape(-1)[:w * P]
        pad = np.zeros(w * P - flat.size, f)
        parts.append(np.concatenate([flat, pad]).reshape(w, P).T)
    parts.append(np.tile(np.arange(16, dtype=f), (P, 1)))
    i, l = np.arange(P)[:, None], np.arange(P)[None, :]
    mats = np.stack([(i == l), np.ones((P, P), bool), (i // HD == l // HD)], 1).astype(f)
    masks = [((i // (2 * m) == l // (2 * m)) & (i % (2 * m) >= m) & (l % (2 * m) < m)) for m in (1, 2, 4, 8, 16, 32, 64)]
    masks = np.stack(masks + [i < l, i <= l], 1).astype(np.uint32)

    data = {
        "x": a["x"][0], "ada_w": a["ada_w"][0],
        "w_in": a["w_in"][0], "ws_t": a["gmlp_ws"][0].transpose(2, 0, 1), "w2": a["rwkv_w2"][0],
        "a2": a["rwkv_a2"][0], "g2": a["rwkv_g2"][0], "w_out": a["w_out"][0], "wq": a["peer_wq"][0],
        "keys_t": a["peer_keys"][0].reshape(2 * NH, NK, P).transpose(2, 0, 1), "peer_u": a["peer_u"][0],
        "peer_v": a["peer_v"][0], "cols": np.concatenate(parts, 1), "mats": mats, "masks": masks,
        "vg": a["gmlp_v_g"][0], "vb": a["gmlp_v_b"][0], "og": a["gmlp_out_g"][0], "lng": a["rwkv_ln_g"][0],
        "lnb": a["rwkv_ln_b"][0], "n2g": a["norm2_g"][0], "fg": a["final_g"],
    }
    nc = _bacc.Bacc("TRN2", target_bir_lowering=False, num_devices=1, dynamic_dma_scratch_size=8192)
    arrays, args = {}, []
    for name, arr in data.items():
        arr = np.ascontiguousarray(arr)
        arrays[f"in_{name}"] = arr
        args.append(nc.dram_tensor(f"in_{name}", arr.shape, mybir.dt.from_np(arr.dtype), kind="ExternalInput").ap())
    args.append(nc.dram_tensor("out", (SEQ, D), mybir.dt.float32, kind="ExternalOutput").ap())
    build(nc, *args)
    r = _run(nc, [arrays], core_ids=[0])
    return r.results[0]["out"].reshape(1, SEQ, D)
```

```python
from contextlib import ExitStack
import numpy as np
import concourse.bass as bass
from concourse import mybir

P = 128
D = 2048
SEQ = 256
NT = SEQ // P
KT = D // P
GW = 1024
RT = GW // P
HD = 64
RW_IN = 3360
NRT = 27
LORA0 = 3 * RT
GH = 8
NH = 8
TOPK = 16
NK = 128
NSEL = NH * TOPK
SLOT = 2048
NW = 8
NA = 3
LEVELS = 7
QUAD = 4
DECAY = -0.6065306597126334
BIG = -3.0e38

COLS = {}
_o = 0
for _n, _w in (("c", 16), ("adab", 96), ("g1", 16), ("mu", 27), ("w0", 8), ("a0", 8), ("kk", 8), ("ka", 8),
               ("rk", 8), ("bs", 8), ("iota", 16)):
    COLS[_n] = (_o, _o + _w)
    _o += _w
NCOL = _o


class Steps:

    def __init__(self, eng, own):
        self.eng, self.own, self.n = eng, own, {}

    def __call__(self, ins, sem=None):
        self.post(ins, sem)
        self.wait(sem)

    def post(self, ins, sem=None):
        sem = self.own if sem is None else sem
        ins.then_inc(sem, 1)
        self.n[sem.name] = self.n.get(sem.name, 0) + 1

    def wait(self, sem=None):
        sem = self.own if sem is None else sem
        self.eng.wait_ge(sem, self.n[sem.name])


def build(nc, x, ada_w, w_in, ws_t, w2, a2, g2, w_out, wq, keys_t, peer_u, peer_v,
          cols, mats, masks, vg, vb, og, lng, lnb, n2g, fg, out):
    f32, u32, u8 = mybir.dt.float32, mybir.dt.uint32, mybir.dt.uint8
    ALU, ACT, AX = mybir.AluOpType, mybir.ActivationFunctionType, mybir.AxisListType
    ds = bass.ds
    ctx = ExitStack()
    with ctx:
        def sb(name, shape, dt=f32):
            return ctx.enter_context(nc.sbuf_tensor(name, shape, dt))

        def sem(name):
            return ctx.enter_context(nc.semaphore(name))

        XW = sb("XW", [P, 2 * D])
        H = sb("H", [P, 2 * D])
        HT = sb("HT", [P, KT * SEQ])
        RING = sb("RING", [P, (NW + NA) * SLOT])
        M = sb("M", [P, NRT * SEQ])
        PT = sb("PT", [P, NRT * (SEQ + 1)])
        ACC = sb("ACC", [P, 2 * SLOT])
        COL = sb("COL", [P, NCOL])
        MAT = sb("MAT", [P, 3, P])
        MASK = sb("MASK", [P, LEVELS + 2, P], u8)
        MODC = sb("MODC", [P, 32])
        MODR = sb("MODR", [P, 4 * KT])
        MODT = sb("MODT", [3 * KT, P])
        SSQ = sb("SSQ", [P, NT, 4])
        ST = sb("ST", [P, 64])
        MID = sb("MID", [P, RT, NT])
        FC = sb("FC", [P, RT])
        OMK = sb("OMK", [P, RT])
        SPR = sb("SPR", [P, QUAD, HD])
        BON = sb("BON", [P, NT, 2 * RT])
        GST = sb("GST", [P, 4, NT * 2 * RT])

        ident, ones, blk = MAT[:, 0, :], MAT[:, 1, :], MAT[:, 2, :]

        def col(name, a=0, b=None):
            lo, hi = COLS[name]
            return COL[:, lo + a:(hi if b is None else lo + b)]

        def slot(s, n=1):
            return RING[:, s * SLOT:(s + n) * SLOT]

        x3 = XW[:, :].rearrange("p (t d) -> p t d", t=NT)
        h3 = H[:, :].rearrange("p (t d) -> p t d", t=NT)
        ht3 = HT[:, :].rearrange("p (k s) -> p k s", k=KT)
        gt2acc = M[:, 2 * D:3 * D]
        ptok = M[:, 0:NT * RW_IN].rearrange("p (t f) -> p t f", t=NT)
        m3 = M[:, :].rearrange("p (j s) -> p j s", j=NRT)
        pt3 = PT[:, :].rearrange("p (j s) -> p j s", j=NRT)
        acc = [ACC[:, i * SLOT:(i + 1) * SLOT] for i in range(2)]
        mask32 = PT[:, 0:(LEVELS + 2) * P].bitcast(u32).rearrange("p (m t) -> p m t", t=P)
        w2a2 = XW[:, 0:GW]
        g2a, g2b = XW[:, GW:2 * GW], XW[:, 2 * GW:3 * GW]
        wst = XW[:, 3 * GW:4 * GW].rearrange("p (h i) -> p h i", h=GH)
        def tiles(ap):
            return ap.rearrange("p (j s) -> p j s", j=RT)
        mr, mk, mv = m3[:, 0:RT, :], m3[:, RT:2 * RT, :], m3[:, 2 * RT:3 * RT, :]
        ar = PT[:, 0:4096].rearrange("p (j w s) -> p j w s", j=RT, w=2)
        bt = tiles(PT[:, 4096:6144])
        a_ft, kk_ft = tiles(acc[0]), tiles(acc[1])
        T1f, T2f, T3f = slot(8), slot(9), slot(10)
        T1, T2, T3 = tiles(T1f), tiles(T2f), tiles(T3f)
        vtok = T3f.rearrange("p (c f) -> p c f", c=NT)
        ytok = acc[1].rearrange("p (c f) -> p c f", c=NT)
        def heads2(ap):
            return ap.rearrange("p (h w t) -> p h w t", h=8, w=2)

        def heads1(ap):
            return ap.rearrange("p (h t) -> p h t", h=8)

        BAR = [heads2(slot(0)), heads2(slot(3))]
        KAR = [heads2(HT[:, 0:SLOT]), heads2(HT[:, SLOT:2 * SLOT])]
        Xi = heads1(slot(1)[:, 0:1024])
        Yi = [heads1(slot(1)[:, 1024:2048]), heads1(M[:, 0:1024])]
        SA, RH = M[:, 1024:1536], M[:, 1536:2048]
        ogr = slot(2)[:, 0:1024]
        Qf = RING[:, 4 * SLOT:4 * SLOT + LEVELS * 1024]
        Q = Qf.rearrange("p (l h t) -> p l h t", l=LEVELS, h=8)
        BTok, KTok = slot(7)[:, 1024:1536], slot(7)[:, 1536:2048]
        vgr, vbr = T1f[:, 0:GW], T1f[:, GW:2 * GW]
        lngr, lnbr = T2f[:, 0:GW], T2f[:, GW:2 * GW]
        gt1b, sh2b, a2b = M[:, 0:D], M[:, D:2 * D], M[:, 2 * D:3 * D]
        n2gr = PT[:, 0:D]
        qt = PT[:, 0:2048].rearrange("p (b t j s) -> p b t j s", b=2, t=NT, j=4)
        junk = PT[:, 3 * D:3 * D + 512]
        xtmp = M[:, 3 * D:3 * D + 512]
        q3 = PT[:, D:3 * D].rearrange("p (t d) -> p t d", t=NT)
        keyst = acc[1].rearrange("p (g n) -> p g n", g=2 * NH)
        gt2b, fgr = PT[:, 0:D], PT[:, D:2 * D]
        cand = M[:, 0:512].rearrange("p (h a b) -> p h a b", h=2, a=TOPK)
        onehot = [M[:, 512:1024], M[:, 0:512]]
        GS = 2 * TOPK
        tops = M[:, 1280:1344].rearrange("p (g k) -> p g k", g=4)
        topi = M[:, 1344:1408].bitcast(u32).rearrange("p (g k) -> p g k", g=4)
        topf = M[:, 1536:1600]
        pos = M[:, 1600:1632].bitcast(u32)
        posp = M[:, 1024:1088].bitcast(u32).rearrange("p (w s) -> p w s", w=2)
        posf = M[:, 1088:1152].rearrange("p (w s) -> p w s", w=2)
        isel = M[:, 1696:1760].rearrange("p (w s) -> p w s", w=2)
        sc1 = M[:, 2048:4096]
        sfin = M[:, 1792:2048].rearrange("p (t s) -> p t s", t=NT)
        gate = PT[:, 6656:6912].rearrange("p (t s) -> p t s", t=NT)
        eidx = M[:, 6144:6400].bitcast(u32).rearrange("p (t s) -> p t s", t=NT)
        dots = M[:, 6400:6656].rearrange("p (t s) -> p t s", t=NT)
        estage = M[:, 6656:6672].bitcast(u32).rearrange("p (w s) -> p w s", w=2)
        PS = ctx.enter_context(nc.psum_tensor("PS", [P, 8, 512], f32))
        mod_dram = nc.dram_tensor("mod_rows", (4 * KT, P), f32, kind="Internal").ap()
        mod_row = mod_dram.rearrange("(b k) p -> b (k p)", b=4)

        names = """ld_const ld_x ld_small ld_vrow ld_lnrow ld_x2 ld_rows ld_keys ld_fin ld_gt2_0 ld_gt2_1 dve_own
            silu_c x_sumsq x_rstd x_norm xT_ps xT_sb ada_used ada_acc ada_cols mod_sb modT_ps modT_sb ada_stored
            pt_zero h1_ready w_used w_evac pT_ps pT_sb mix_lora lora_act mix_kk z_ps z_sb a_ps a_sb ss_ps ss_sb
            l_ready l_exp at_done k_scale k2_done vt_ps vt_sb bon_in bon_ps bon_sb wkv_in kar_zero q_init
            gate_used ln_var ln_std vn_ready zg_ps zg_sb ya_sumsq ya_std ya_done score_ps score_sb inv_p inv_q
            inv_xy inv_x inv_y0 inv_y1 tok_ps tok_sb rhs_ps rhs_sb sa_ps sa_sb y_ps y_sb st_ps st_sb gn_var
            gn_std gate_ps yb_done yT_ps yT_sb x2_done x2_sumsq x2_std h2_done h2T_ps h2T_sb q00_ps q_done0
            q_done1 qT_ps0 qT_ps1 qT_sb0 qT_sb1 sc_ps0 sc_ps1 sc_used sc1_sb sm_in sm_exp idx0_ready idx1_ready
            dots_done act_ready used staged slot_open x_out out_sumsq out_var out_std out_ready stored""".split()
        S = {n: sem(n) for n in names}
        w_slot = [sem(f"w_slot{i}") for i in range(NW)]
        a_slot = [sem(f"a_slot{i}") for i in range(NA)]
        g_slot = [sem(f"g_slot{i}") for i in range(NW)]

        gslot = [slot(8), slot(9), slot(10), M[:, 2 * D:3 * D], slot(4), slot(5), slot(6), slot(7)]
        NB = 6
        w_in_v = w_in.rearrange("(q k p) n -> q p k n", q=4, p=P)
        w_out_v = w_out.rearrange("(q k p) n -> q p k n", q=4, p=P)
        wq_v = wq.rearrange("(q k p) n -> q p k n", q=4, p=P)
        RG = 6
        LASTW = RW_IN - RG * 512

        GT2_SLOT = [0, 1] * 7 + [0, 0]

        def gt2_before(k):
            return max(i for i in range(k) if GT2_SLOT[i] == GT2_SLOT[k])

        OUT_UNITS = [(0, 0), (0, 1), (1, 0), (1, 1), (2, 0), (2, 1), (0, 2), (0, 3), (1, 2), (1, 3), (2, 2), (2, 3),
                     (3, 0), (3, 1), (3, 2), (3, 3)]
        OUT_DONE = [44 + OUT_UNITS.index((g, 3)) + 1 for g in range(4)]

        def y_round(r):
            return (r // 2) % 2, 8 * (r // 4) + 4 * (r % 2)

        def h_round(r):
            return r // 4, 4 * (r % 4)

        def row(ap, n):
            return ap.rearrange("(a n) -> a n", a=1).broadcast_to([P, n])

        block = ctx.enter_context(nc.Block())

        @block.sync
        def _(sp):
            sp.dma_start(COL[:, :], cols).then_inc(S["ld_const"], 16)
            sp.dma_start(MAT[:, :, :], mats).then_inc(S["ld_const"], 16)
            sp.dma_start(mask32, masks).then_inc(S["ld_const"], 16)
            sp.dma_start(x3, x.rearrange("(t p) d -> p t d", p=P)).then_inc(S["ld_x"], 16)

            def unit(view, kq, n0, width, s, wait):
                if wait is not None:
                    sp.wait_ge(S["w_used"], wait)
                sp.dma_start(slot(s)[:, 0:4 * width].rearrange("p (k n) -> p k n", k=4),
                             view[kq, :, :, ds(n0, width)]).then_inc(w_slot[s], 16)

            sp.wait_ge(S["ada_used"], 31)
            for g in range(RG):
                for kq in range(4):
                    u = 4 * g + kq
                    unit(w_in_v, kq, 2 * GW + 512 * g, 512, u % NW, u - 7 if u >= NW else None)
                if g == 2:
                    sp.wait_ge(S["x_norm"], NT)
                    sp.dma_start(w2a2[0:64, :], w2).then_inc(S["ld_small"], 16)
                    sp.dma_start(w2a2[64:128, :], a2).then_inc(S["ld_small"], 16)
                    sp.dma_start(g2a, g2[0:128, :]).then_inc(S["ld_small"], 16)
                    sp.dma_start(g2b[0:32, :], g2[128:160, :]).then_inc(S["ld_small"], 16)
                    sp.dma_start(wst, ws_t).then_inc(S["ld_small"], 16)
            for kq in range(4):
                unit(w_in_v, kq, 2 * GW + RG * 512, LASTW, kq, 4 * RG + kq - 7)
            with sp.Fori(0, 2) as b:
                for i in range(8):
                    unit(w_in_v, i % 4, b * 1024 + 512 * (i // 4), 512, (4 + i) % NW, b * 8 + (28 + i - 7))
            sp.wait_ge(S["bon_ps"], 1)
            sp.dma_start(vgr, row(vg, GW)).then_inc(S["ld_vrow"], 16)
            sp.dma_start(vbr, row(vb, GW)).then_inc(S["ld_vrow"], 16)
            sp.wait_ge(S["w_used"], 44)
            sp.dma_start(ogr, row(og, GW)).then_inc(S["ld_vrow"], 16)
            sp.wait_ge(S["ada_used"], (NB - 1) * KT + 14)
            sp.dma_start(lngr, row(lng, GW)).then_inc(S["ld_lnrow"], 16)
            sp.dma_start(lnbr, row(lnb, GW)).then_inc(S["ld_lnrow"], 16)
            sp.wait_ge(S["inv_y0"], 28)
            sp.wait_ge(S["inv_y1"], 28)
            sp.wait_ge(S["ya_done"], NT)
            for i, (g, kq) in enumerate(OUT_UNITS[:8]):
                if i == 7:
                    sp.wait_ge(S["y_sb"], 8)
                unit(w_out_v, kq, 512 * g, 512, (4 + i) % NW, 44)
            sp.wait_ge(S["gate_ps"], 2)
            sp.dma_start(x3, x.rearrange("(t p) d -> p t d", p=P)).then_inc(S["ld_x2"], 16)
            sp.wait_ge(S["ada_stored"], 16)
            sp.dma_start(gt1b, row(mod_row[0, :], D)).then_inc(S["ld_rows"], 16)
            sp.dma_start(sh2b, row(mod_row[1, :], D)).then_inc(S["ld_rows"], 16)
            sp.wait_ge(S["ada_cols"], NB)
            sp.dma_start(a2b, row(mod_row[2, :], D)).then_inc(S["ld_rows"], 16)
            sp.dma_start(n2gr, row(n2g, D)).then_inc(S["ld_rows"], 16)
            sp.wait_ge(S["yb_done"], 2)
            sp.dma_start(keyst, keys_t).then_inc(S["ld_keys"], 16)
            for i, (g, kq) in enumerate(OUT_UNITS[8:]):
                unit(w_out_v, kq, 512 * g, 512, (4 + i) % NW, 52 + i - 7)
            for i in range(4):
                unit(wq_v, i, 0, 512, 4 + i, 60 + i - 7)
            for i in range(4):
                unit(wq_v, i, 512, 512, i, 64 + i - 7)
            with sp.Fori(0, 2) as g:
                for i in range(4):
                    unit(wq_v, i, g * 512 + 1024, 512, i, g * 4 + (68 + i - 3))
            sp.wait_ge(S["sc_ps0"], 4)
            sp.wait_ge(S["sc_ps1"], 4)
            sp.wait_ge(S["ada_stored"], 32)
            sp.dma_start(gt2b, row(mod_row[3, :], D)).then_inc(S["ld_fin"], 16)
            sp.dma_start(fgr, row(fg, D)).then_inc(S["ld_fin"], 16)
            for t in range(NT):
                for i in range(2):
                    sp.wait_ge(S["out_ready"], 2 * t + i + 1)
                    sp.dma_start(out[t * P:(t + 1) * P, i * GW:(i + 1) * GW], h3[:, t, i * GW:(i + 1) * GW])\
                        .then_inc(S["stored"], 16)
            sp.wait_ge(S["stored"], 16 * 2 * NT)

        @block.gpsimd
        def _(pool):
            for n in range((NB - 1) * KT):
                b, k = n // KT, n % KT
                if n >= NA:
                    pool.wait_ge(S["ada_used"], n - NA + 1)
                pool.dma_start(slot(NW + n % NA), ada_w[k * P:(k + 1) * P, b * D:(b + 1) * D])\
                    .then_inc(a_slot[n % NA], 16)
            pool.wait_ge(S["w_used"], 44)
            for i in range(2):
                nc.gpsimd.memset(HT[:, i * SLOT:(i + 1) * SLOT], 0.0).then_inc(S["kar_zero"], 1)
            pool.wait_ge(S["wkv_in"], 1)
            pool.wait_ge(S["vn_ready"], NT)
            for k in range(KT):
                if k >= 2:
                    pool.wait_ge(S["ada_used"], (NB - 1) * KT + gt2_before(k) + 1)
                pool.dma_start(slot(8 + GT2_SLOT[k]), ada_w[k * P:(k + 1) * P, (NB - 1) * D:NB * D])\
                    .then_inc(S[f"ld_gt2_{GT2_SLOT[k]}"], 16)

            for ps in range(4):
                t, table = ps // 2, (peer_u, peer_v)[ps % 2]
                with pool.Fori(0, 8) as i:
                    pool.wait_ge(S[f"idx{t}_ready"], i + 1)
                    for half in range(2):
                        pool.wait_ge(S["used"], i * 16 + (128 * ps + 8 * half + 1))
                        nc.gpsimd.tensor_copy(estage[:, half, :], eidx[:, t, ds(i * 16 + 8 * half, 8)])\
                            .then_inc(S["staged"], 1)
                        pool.wait_ge(S["staged"], i * 2 + (16 * ps + half + 1))
                        for s in range(NW):
                            pool.wait_ge(S["used"], i * 16 + (128 * ps + 8 * half + s + 1))
                            pool.sem_inc(S["slot_open"], 1)
                            pool.indirect_dma_start(
                                gslot[s], None, table,
                                bass.IndirectOffsetOnAxis(ap=estage[:, half, s:s + 1], axis=0),
                            ).then_inc(g_slot[s], 16)

        @block.tensor
        def _(pe):
            mm, tr = nc.tensor.matmul, nc.tensor.transpose

            def w_group(u0, use, slots, bank, width=512, between=(), first=False):
                for kq in range(4):
                    pe.wait_ge(w_slot[slots[kq]], use(kq))
                    if first:
                        pe.wait_ge(S["h1_ready"], 4 * (kq + 1))
                    w = slot(slots[kq])[:, 0:4 * width].rearrange("p (k n) -> p k n", k=4)
                    for k in range(4):
                        for t in range(NT):
                            kt = 4 * kq + k
                            last = mm(PS[:, bank + t, 0:width], ht3[:, kt, t * P:(t + 1) * P], w[:, k, :],
                                      start=(kt == 0), stop=(kt == KT - 1))
                    last.then_inc(S["w_used"], 1)
                    if kq < len(between):
                        between[kq]()

            pe.wait_ge(S["ld_const"], 48)
            pe.wait_ge(S["x_norm"], NT)
            for r in range(4):
                if r >= 2:
                    pe.wait_ge(S["xT_sb"], r - 1)
                for j in range(4):
                    for t in range(NT):
                        k = 4 * r + j
                        last = tr(PS[:, 2 * (r % 2) + j // 2, (j % 2) * 256 + t * P:(j % 2) * 256 + (t + 1) * P],
                                  h3[:, t, k * P:(k + 1) * P], ident)
                last.then_inc(S["xT_ps"], 1)
            def col_sum(b, bank=4):
                pe.wait_ge(S["ada_acc"], b + 1)
                if b == 3:
                    pe.wait_ge(S["mod_sb"], 2)
                for j in range(KT):
                    c_ = (b % 2) * KT + j
                    last = mm(PS[:, bank, c_:c_ + 1], acc[b % 2][:, j * P:(j + 1) * P], ones[:, 0:1],
                              start=True, stop=True)
                last.then_inc(S["ada_cols"], 1)

            col_sum(0)
            col_sum(1)

            for g in range(RG):
                if g >= 2:
                    pe.wait_ge(S["w_evac"], 2 * (g - 1))
                w_group(4 * g, lambda kq, g=g: 16 * ((4 * g + kq) // NW + 1), [(4 * g + kq) % NW for kq in range(4)],
                        2 * (g % 2), first=(g == 0))
                if g == 3:
                    col_sum(2)
            pe.wait_ge(S["w_evac"], 2 * (RG - 1))
            w_group(24, lambda kq: 16 * 4, [0, 1, 2, 3], 0, LASTW)
            pe.wait_ge(S["w_evac"], 2 * (RG + 1))
            pe.wait_ge(S["mod_sb"], 2)
            for r in range(7):
                if r >= 2:
                    pe.wait_ge(S["pT_sb"], r - 1)
                for j in range(4 * r, min(4 * r + 4, NRT)):
                    w = min(P, RW_IN - j * P)
                    for t in range(NT):
                        jj = j % 4
                        last = tr(PS[0:w, 4 + 2 * (r % 2) + jj // 2, (jj % 2) * 256 + t * P:(jj % 2) * 256 + (t + 1) * P],
                                  ptok[:, t, j * P:j * P + w], ident)
                last.then_inc(S["pT_ps"], 1)

            def gmlp_body(b, between):
                for half in range(2):
                    pe.wait_ge(S["w_evac"], 16 + 2 * half if b else 14)
                    w_group(28 + 8 * b + 4 * half,
                            (lambda kq, half=half: 16 * ((28 + 8 * b + 4 * half + kq) // NW + 1)),
                            [(4 + 4 * half + kq) % NW for kq in range(4)], 2 * half, between=between[4 * half:4 * half + 4])

            def nothing():
                pass

            def ada_sum_3():
                pe.wait_ge(S["pT_sb"], 7)
                col_sum(3)

            def lora(rows, done):
                for j in range(RT):
                    last = mm(PS[:, 4 + j // 2, (j % 2) * 256:(j % 2 + 1) * 256], w2a2[rows, j * P:(j + 1) * P],
                              m3[rows, LORA0, :], start=True, stop=True)
                last.then_inc(S[done], 1)

            def lora_z():
                pe.wait_ge(S["ld_small"], 80)
                pe.wait_ge(S["lora_act"], 3)
                pe.wait_ge(S["mod_sb"], 3)
                lora(slice(0, 64), "z_ps")

            def ada_sum_4_lora_a():
                pe.wait_ge(S["w_evac"], 18)
                col_sum(4, 2)
                pe.wait_ge(S["z_sb"], RT)
                lora(slice(64, 128), "a_ps")

            def mod_rows():
                pe.wait_ge(S["mod_sb"], 4)
                tr(PS[0:3 * KT, 3, 0:P], MODR[:, 0:3 * KT], ident).then_inc(S["modT_ps"], 1)
                pe.wait_ge(S["modT_sb"], 1)

            def v_tok():
                pe.wait_ge(S["ss_sb"], 1)
                for c in range(NT):
                    for j in range(RT):
                        last = tr(PS[:, 4 + 2 * c + j // 4, (j % 4) * P:(j % 4 + 1) * P],
                                  mv[:, j, c * P:(c + 1) * P], ident)
                last.then_inc(S["vt_ps"], 1)

            def head_squares():
                pe.wait_ge(S["a_sb"], RT)
                pe.wait_ge(S["mix_kk"], 1)
                for n in range(4):
                    last = mm(PS[:, 4 + n, :], blk, PT[:, 4096 + n * 512:4096 + (n + 1) * 512], start=True, stop=True)
                last.then_inc(S["ss_ps"], 1)

            gmlp_body(0, [nothing, ada_sum_3, nothing, nothing, nothing, nothing, nothing, lora_z])
            gmlp_body(1, [ada_sum_4_lora_a, head_squares, mod_rows, nothing, nothing, v_tok])
            pe.wait_ge(S["bon_in"], 1)
            pe.wait_ge(S["vt_sb"], 1)
            for c in range(NT):
                for j in range(RT):
                    last = mm(PS[:, 4, (c * RT + j) * 2:(c * RT + j) * 2 + 2], T1[:, j, c * P:(c + 1) * P],
                              blk[:, 0:P:HD], start=True, stop=True)
            last.then_inc(S["bon_ps"], 1)
            pe.wait_ge(S["bon_sb"], 1)
            pe.wait_ge(S["w_evac"], 22)
            pe.wait_ge(S["wkv_in"], 1)

            def where(n, pos):
                par, i = pos // 4, pos % 4
                return QUAD * (n // 2) + i, slice(HD * par, HD * (par + 1))

            def head_v(n, pos):
                j, pr = where(n, pos)
                return vtok[:, n % 2, j * P + pr.start:j * P + pr.stop]

            def scores(n):
                tok = slice((n % 2) * P, (n % 2 + 1) * P)
                if n:
                    pe.wait_ge(S["inv_y0"], 7 * n)
                    pe.wait_ge(S["inv_y1"], 7 * n)
                for i in range(8):
                    if i >= 6:
                        pe.wait_ge(S["score_sb"], 8 * n + i - 5)
                    for pos in range(2 * (i % 4), 2 * (i % 4) + 2):
                        j, pr = where(n, pos)
                        last = mm(PS[:, i % 6, (pos % 2) * 256:(pos % 2 + 1) * 256],
                                  (bt, mk)[i // 4][pr, j, tok], ar[pr, j, :, tok], start=True, stop=True)
                    last.then_inc(S["score_ps"], 1)
                pe.wait_ge(S["score_sb"], 8 * (n + 1))

            def chain(n, step):
                hf, c = n // 2, n % 2
                tok = slice(c * P, (c + 1) * P)
                if step == 0:
                    pe.wait_ge(S["inv_y0"], 7 * (n + 1))
                    pe.wait_ge(S["inv_y1"], 7 * (n + 1))
                    pe.wait_ge(S["zg_sb"], 2 * NT)
                    if c == 0:
                        if n:
                            pe.wait_ge(S["y_sb"], 2 * n)
                        for w, src in enumerate((bt, mk)):
                            for i in range(QUAD):
                                last = tr(PS[:, 6 + w, i * P:(i + 1) * P], src[:, QUAD * hf + i, tok], ident)
                        last.then_inc(S["tok_ps"], 1)
                if step == 1:
                    if c == 0:
                        pe.wait_ge(S["tok_sb"], 2 * (hf + 1))
                    else:
                        pe.wait_ge(S["st_sb"], 2 * (hf + 1))
                    for pos in range(8):
                        j, pr = where(n, pos)
                        o_ = PS[:, 6 + pos // 4, (pos % 4) * HD:(pos % 4 + 1) * HD]
                        if c == 1:
                            mm(o_, ar[pr, j, 0, tok], SPR[pr, pos % 4, :], start=True, stop=False)
                        last = mm(o_, KAR[n % 2][:, pos, 0, :], head_v(n, pos), start=(c == 0), stop=True)
                    last.then_inc(S["rhs_ps"], 1)
                if step == 2:
                    pe.wait_ge(S["rhs_sb"], n + 1)
                    for pos in range(8):
                        last = mm(PS[:, 6, pos * HD:(pos + 1) * HD], Yi[n % 2][:, pos, :],
                                  RH[:, pos * HD:(pos + 1) * HD], start=True, stop=True)
                    last.then_inc(S["sa_ps"], 1)
                if step == 3:
                    pe.wait_ge(S["sa_sb"], n + 1)
                    for pos in range(8):
                        j, pr = where(n, pos)
                        o_ = PS[:, 6 + pos // 4, (pos % 4) * HD:(pos % 4 + 1) * HD]
                        if c == 1:
                            mm(o_, ar[pr, j, 1, tok], SPR[pr, pos % 4, :], start=True, stop=False)
                        mm(o_, BAR[n % 2][:, pos, 1, :], SA[:, pos * HD:(pos + 1) * HD], start=(c == 0), stop=False)
                        last = mm(o_, KAR[n % 2][:, pos, 1, :], head_v(n, pos), start=False, stop=True)
                        if pos % 4 == 3:
                            last.then_inc(S["y_ps"], 1)
                if step == 4 and c == 0:
                    pe.wait_ge(S["y_sb"], 2 * n + 2)
                    sa2 = SA.rearrange("p (r i d) -> p i r d", r=2, i=QUAD)
                    for i in range(QUAD):
                        j = QUAD * hf + i
                        o_ = PS[:, 6, i * P:(i + 1) * P]
                        mm(o_, BTok[:, i * P:(i + 1) * P], sa2[:, i, :, :], start=True, stop=False)
                        last = mm(o_, KTok[:, i * P:(i + 1) * P], vtok[:, c, j * P:(j + 1) * P], start=False, stop=True)
                    last.then_inc(S["st_ps"], 1)

            def out_gate(hf):
                pe.wait_ge(S["y_sb"], 4 * hf + 4 if hf else 6)
                if hf == 0:
                    pe.wait_ge(S["st_sb"], 4)
                for t in range(NT):
                    o_ = PS[:, 6 + t, :]
                    mm(o_, m3[:, LORA0 + 1, t * P:(t + 1) * P], g2a[:, hf * 512:(hf + 1) * 512], start=True, stop=False)
                    last = mm(o_, m3[0:32, LORA0 + 2, t * P:(t + 1) * P], g2b[0:32, hf * 512:(hf + 1) * 512],
                              start=False, stop=True)
                last.then_inc(S["gate_ps"], 1)

            def spatial(i):
                t, hh = i // 2, i % 2
                pe.wait_ge(S["vn_ready"], t + 1)
                if i >= 2:
                    pe.wait_ge(S["zg_sb"], i - 1)
                for h in range(4 * hh, 4 * hh + 4):
                    last = mm(PS[:, 6 + i % 2, (h % 4) * P:(h % 4 + 1) * P], wst[:, h, :],
                              h3[:, t, GW + h * P:GW + (h + 1) * P], start=True, stop=True)
                last.then_inc(S["zg_ps"], 1)

            for n in range(4):
                scores(n)
                for l in range(LEVELS):
                    for g in range(2):
                        if l >= 2:
                            pe.wait_ge(S["inv_x"], 10 * n + 2 * (l - 2) + g + 1)
                        for pos in range(4 * g, 4 * g + 4):
                            o_ = PS[:, g, (pos % 4) * P:(pos % 4 + 1) * P]
                            if l == 0:
                                last = tr(o_, BAR[n % 2][:, pos, 0, :], ident)
                            else:
                                last = mm(o_, BAR[n % 2][:, pos, 0, :], Q[:, 0, pos, :] if l == 1 else Xi[:, pos, :],
                                          start=True, stop=True)
                        last.then_inc(S["inv_p"], 1)
                    if n == 0 and l >= 3:
                        spatial(l - 3)
                    if n >= 1 and l < 5:
                        chain(n - 1, l)
                    if n == 3 and l == 5:
                        pe.wait_ge(S["ada_acc"], NB)
                        for j in range(KT):
                            last = mm(PS[:, 7, 256 + j:257 + j], gt2acc[:, j * P:(j + 1) * P], ones[:, 0:1],
                                      start=True, stop=True)
                        last.then_inc(S["ada_cols"], 1)
                    if n == 3 and l == 6:
                        pe.wait_ge(S["mod_sb"], 5)
                        out_gate(0)
                    for g in range(2):
                        pe.wait_ge(S["inv_q"], 14 * n + 2 * l + g + 1)
                        if l >= 1:
                            pe.wait_ge(S[f"inv_y{g}"], 7 * n + l)
                        for pos in range(4 * g, 4 * g + 4):
                            if 1 <= l < LEVELS - 1:
                                mm(PS[:, 2 + g, (pos % 4) * P:(pos % 4 + 1) * P], Yi[n % 2][:, pos, :], Q[:, l, pos, :],
                                   start=True, stop=True)
                        for pos in range(4 * g, 4 * g + 4):
                            o_ = PS[:, 4 + g, (pos % 4) * P:(pos % 4 + 1) * P]
                            if l == 0:
                                last = tr(o_, Q[:, 0, pos, :], ident)
                            else:
                                last = mm(o_, Q[:, l, pos, :], Yi[n % 2][:, pos, :], start=True, stop=True)
                        last.then_inc(S["inv_xy"], 1)

            def transpose_round(r, at, bank, done_ps):
                t, k0 = at(r)
                for j in range(4):
                    last = tr(PS[:, bank, j * P:(j + 1) * P], h3[:, t, (k0 + j) * P:(k0 + j + 1) * P], ident)
                last.then_inc(S[done_ps], 1)

            def out_units(a, b):
                for i in range(a, b):
                    g, kq = OUT_UNITS[i]
                    s = (4 + i) % NW
                    pe.wait_ge(w_slot[s], 16 * ((44 + i) // NW + 1))
                    w = slot(s).rearrange("p (k n) -> p k n", k=4)
                    for k in range(4):
                        for t in range(NT):
                            kt = 4 * kq + k
                            last = mm(PS[:, 2 * g + t, :], ht3[:, kt, t * P:(t + 1) * P], w[:, k, :],
                                      start=(kt == 0), stop=(kt == KT - 1))
                    last.then_inc(S["w_used"], 1)

            pe.wait_ge(S["inv_y0"], 28)
            pe.wait_ge(S["inv_y1"], 28)
            pe.wait_ge(S["ya_done"], NT)
            transpose_round(0, y_round, 4, "yT_ps")
            transpose_round(1, y_round, 5, "yT_ps")
            pe.wait_ge(S["gate_used"], 1)
            chain(3, 0)
            chain(3, 1)
            for r in (2, 3):
                pe.wait_ge(S["yT_sb"], r - 1)
                transpose_round(r, y_round, 4 + r % 2, "yT_ps")
            chain(3, 2)
            pe.wait_ge(S["yT_sb"], 4)
            out_units(0, 1)
            chain(3, 3)
            out_units(1, 2)
            out_gate(1)
            out_units(2, 6)
            pe.wait_ge(S["yb_done"], 2)
            for r in range(4, 8):
                if r >= 6:
                    pe.wait_ge(S["yT_sb"], r - 1)
                transpose_round(r, y_round, 6 + r % 2, "yT_ps")
            pe.wait_ge(S["yT_sb"], 8)
            out_units(6, 16)
            pe.wait_ge(S["x2_done"], 2)
            pe.wait_ge(S["mod_sb"], 5)
            tr(PS[0:KT, 0, 0:P], MODR[:, 3 * KT:4 * KT], ident).then_inc(S["modT_ps"], 1)
            for r in range(8):
                if r >= 2:
                    pe.wait_ge(S["h2T_sb"], r - 1)
                if r % 2 == 0:
                    pe.wait_ge(S["h2_done"], r // 2 + 1)
                transpose_round(r, h_round, 4 + r % 2, "h2T_ps")
            pe.wait_ge(S["h2T_sb"], 8)

            def query_t(g, t):
                pe.wait_ge(S[f"q_done{t}"], g + 1)
                for j in range(4):
                    last = tr(PS[:, 4 + t, j * P:(j + 1) * P], q3[:, t, g * 512 + j * P:g * 512 + (j + 1) * P], ident)
                last.then_inc(S[f"qT_ps{t}"], 1)

            def query_scores(g, t):
                pe.wait_ge(S[f"qT_sb{t}"], g + 1)
                if g == 0:
                    pe.wait_ge(S["ld_keys"], 16)
                else:
                    pe.wait_ge(S[("sc_used", "sc1_sb")[t]], g)
                for j in range(4):
                    last = mm(PS[:, 6 + t, j * P:(j + 1) * P], qt[:, g % 2, t, j, :], keyst[:, 4 * g + j, :],
                              start=True, stop=True)
                last.then_inc(S[f"sc_ps{t}"], 1)

            pe.wait_ge(S["x2_done"], 8)
            pe.wait_ge(S["modT_sb"], 2)
            for t in range(NT):
                for kq in range(4):
                    pe.wait_ge(w_slot[4 + kq], 16 * 8)
                    w = slot(4 + kq).rearrange("p (k n) -> p k n", k=4)
                    for k in range(4):
                        kt = 4 * kq + k
                        last = mm(PS[:, t, :], ht3[:, kt, t * P:(t + 1) * P], w[:, k, :], start=(kt == 0),
                                  stop=(kt == KT - 1))
                    if t == 1:
                        last.then_inc(S["w_used"], 1)
                        if kq == 0:
                            query_t(0, 0)
                        if kq == 1:
                            query_scores(0, 0)
                    elif kq == 3:
                        last.then_inc(S["q00_ps"], 1)
            w_group(64, lambda kq: 16 * 9, [0, 1, 2, 3], 2, between=[lambda: query_t(0, 1), lambda: query_scores(0, 1)])
            for g in (2, 3):
                pe.wait_ge(S["q_done0"], g - 1)
                pe.wait_ge(S["q_done1"], g - 1)
                w_group(60 + 4 * g, lambda kq, g=g: 16 * (8 + g), [0, 1, 2, 3], 2 * (g % 2),
                        between=[lambda: [query_t(g - 1, t) for t in range(NT)],
                                 lambda: [query_scores(g - 1, t) for t in range(NT)]])
            for t in range(NT):
                query_t(3, t)
            for t in range(NT):
                query_scores(3, t)

        @block.scalar
        def _(act):
            act_ = nc.scalar.activation
            act.wait_ge(S["ld_const"], 48)
            act_(col("c"), col("c"), ACT.Silu).then_inc(S["silu_c"], 1)
            act.wait_ge(S["ld_x"], 16)
            for t in range(NT):
                act_(h3[:, t, :], x3[:, t, :], ACT.Square, accum_out=ST[:, t:t + 1]).then_inc(S["x_sumsq"], 1)
            act.wait_ge(S["x_rstd"], 1)
            act_(ST[:, 2:4], ST[:, 2:4], ACT.Sqrt).then_inc(S["x_rstd"], 1)
            act.wait_ge(S["x_rstd"], 3)
            act.wait_ge(S["x_sumsq"], NT)
            for t in range(NT):
                act_(h3[:, t, :], x3[:, t, :], ACT.Copy, scale=ST[:, 4 + t:5 + t]).then_inc(S["x_norm"], 1)
            for r in range(4):
                act.wait_ge(S["xT_ps"], r + 1)
                b = 2 * (r % 2)
                act_(HT[:, r * 1024:(r + 1) * 1024].rearrange("p (b n) -> p b n", b=2), PS[:, b:b + 2, :], ACT.Copy)\
                    .then_inc(S["xT_sb"], 1)
            for g in range(RG + 1):
                act.wait_ge(S["w_used"], 4 * (g + 1))
                w = 512 if g < RG else LASTW
                for t in range(NT):
                    act_(ptok[:, t, g * 512:g * 512 + w], PS[:, 2 * (g % 2) + t, 0:w], ACT.Copy).then_inc(S["w_evac"], 1)
            for r in range(7):
                act.wait_ge(S["pT_ps"], r + 1)
                for j in range(4 * r, min(4 * r + 4, NRT), 2):
                    b = 4 + 2 * (r % 2) + (j % 4) // 2
                    if j + 1 < NRT:
                        last = act_(pt3[:, j:j + 2, 1:SEQ + 1], PS[:, b, :].rearrange("p (j s) -> p j s", j=2), ACT.Copy)
                    else:
                        last = act_(pt3[0:32, j, 1:SEQ + 1], PS[0:32, b, 0:SEQ], ACT.Copy)
                last.then_inc(S["pT_sb"], 1)
            act.wait_ge(S["mix_lora"], 1)
            act_(m3[0:64, LORA0, :], m3[0:64, LORA0, :], ACT.Tanh).then_inc(S["lora_act"], 1)
            act_(m3[:, LORA0 + 1, :], m3[:, LORA0 + 1, :], ACT.Sigmoid).then_inc(S["lora_act"], 1)
            act_(m3[0:32, LORA0 + 2, :], m3[0:32, LORA0 + 2, :], ACT.Sigmoid).then_inc(S["lora_act"], 1)

            def gelu_evac(b, half):
                act.wait_ge(S["w_used"], 28 + 8 * b + 4 * (half + 1))
                for t in range(NT):
                    act_(h3[:, t, b * GW + half * 512:b * GW + (half + 1) * 512], PS[:, 2 * half + t, :], ACT.Gelu)\
                        .then_inc(S["w_evac"], 1)

            gelu_evac(0, 0)
            gelu_evac(0, 1)
            act.wait_ge(S["z_ps"], 1)
            for j in range(RT):
                act_(T1[:, j, :], PS[:, 4 + j // 2, (j % 2) * 256:(j % 2 + 1) * 256], ACT.Sigmoid,
                     bias=col("w0", j, j + 1)).then_inc(S["z_sb"], 1)
            act.wait_ge(S["a_ps"], 1)
            for j in range(RT):
                act_(a_ft[:, j, :], PS[:, 4 + j // 2, (j % 2) * 256:(j % 2 + 1) * 256], ACT.Sigmoid,
                     bias=col("a0", j, j + 1)).then_inc(S["a_sb"], 1)
            act.wait_ge(S["ss_ps"], 1)
            act_(PT[:, 4096:6144].rearrange("p (b n) -> p b n", b=4), PS[:, 4:8, :], ACT.Sqrt).then_inc(S["ss_sb"], 1)
            act.wait_ge(S["modT_ps"], 1)
            act_(MODT[:, :], PS[0:3 * KT, 3, 0:P], ACT.Copy).then_inc(S["modT_sb"], 1)
            act.wait_ge(S["modT_sb"], 1)
            act.dma_start(mod_dram[0:3 * KT, :], MODT[:, :]).then_inc(S["ada_stored"], 16)
            act.wait_ge(S["l_ready"], 1)
            act_(T3f, T3f, ACT.Exp).then_inc(S["l_exp"], 1)
            act_(T1f, T2f, ACT.Exp).then_inc(S["l_exp"], 1)
            act_(FC[:, :], FC[:, :], ACT.Exp).then_inc(S["l_exp"], 1)
            act.wait_ge(S["l_exp"], 2)
            act_(T2f, T2f, ACT.Exp, scale=-1.0).then_inc(S["l_exp"], 1)
            act.wait_ge(S["at_done"], 1)
            for j in range(RT):
                act_(T3[:, j, :], a_ft[:, j, :], ACT.Identity, scale=col("ka", j, j + 1), bias=OMK[:, j:j + 1])\
                    .then_inc(S["k_scale"], 1)
            gelu_evac(1, 0)
            act.wait_ge(S["vt_ps"], 1)
            act.wait_ge(S["k2_done"], 1)
            act_(T3f.rearrange("p (b n) -> p b n", b=4), PS[:, 4:8, :], ACT.Copy).then_inc(S["vt_sb"], 1)
            act.wait_ge(S["w_used"], 40)
            act_(Qf.rearrange("p (m t) -> p m t", t=P), ident.unsqueeze(1).broadcast_to([P, LEVELS * 8, P]),
                 ACT.Copy).then_inc(S["q_init"], 1)
            gelu_evac(1, 1)
            act.wait_ge(S["bon_ps"], 1)
            act_(BON[:, :, :].rearrange("p c h -> p (c h)"), PS[:, 4, 0:32], ACT.Copy).then_inc(S["bon_sb"], 1)

            def chain(n, step):
                hf, c = n // 2, n % 2
                if step == 0 and c == 0:
                    act.wait_ge(S["tok_ps"], hf + 1)
                    act_(BTok, PS[:, 6, :], ACT.Copy).then_inc(S["tok_sb"], 1)
                    act_(KTok, PS[:, 7, :], ACT.Copy).then_inc(S["tok_sb"], 1)
                if step == 1:
                    act.wait_ge(S["rhs_ps"], n + 1)
                    act_(RH.rearrange("p (b n) -> p b n", b=2), PS[:, 6:8, 0:256], ACT.Copy).then_inc(S["rhs_sb"], 1)
                if step == 2:
                    act.wait_ge(S["sa_ps"], n + 1)
                    act_(SA, PS[:, 6, :], ACT.Copy).then_inc(S["sa_sb"], 1)
                if step == 3:
                    for par in range(2):
                        act.wait_ge(S["y_ps"], 2 * n + par + 1)
                        dst = ytok[:, c, QUAD * hf * P:QUAD * (hf + 1) * P].rearrange("p (i d) -> p i d", i=QUAD)
                        act_(dst[:, :, HD * par:HD * (par + 1)],
                             PS[:, 6 + par, 0:256].rearrange("p (i d) -> p i d", i=QUAD), ACT.Copy).then_inc(S["y_sb"], 1)

            for n in range(4):
                for l in range(LEVELS):
                    if n == 0 and l == 1:
                        act.wait_ge(S["ln_var"], 1)
                        act_(ST[:, 12:14], ST[:, 12:14], ACT.Sqrt).then_inc(S["ln_std"], 1)
                    if n == 1 and l == 5:
                        act.wait_ge(S["zg_sb"], 2 * NT)
                        for t in range(NT):
                            act_(h3[:, t, GW:2 * GW], h3[:, t, 0:GW], ACT.Square, accum_out=ST[:, 16 + t:17 + t])\
                                .then_inc(S["ya_sumsq"], 1)
                    if n == 2 and l == 0:
                        act.wait_ge(S["ya_std"], 1)
                        act_(ST[:, 18:20], ST[:, 18:20], ACT.Sqrt).then_inc(S["ya_std"], 1)
                    if n == 3 and l == 3:
                        act.wait_ge(S["gn_var"], 1)
                        act_(GST[:, 1, 0:16], GST[:, 1, 0:16], ACT.Sqrt).then_inc(S["gn_std"], 1)
                    if n >= 1 and l < 4:
                        chain(n - 1, l)
                    if 1 <= l < LEVELS - 1:
                        for g in range(2):
                            act.wait_ge(S["inv_xy"], 14 * n + 2 * l + g + 1)
                            act_(Xi[:, 4 * g:4 * g + 4, :].rearrange("p h t -> p (h t)"), PS[:, 2 + g, :], ACT.Copy)\
                                .then_inc(S["inv_x"], 1)
                    act.wait_ge(S["inv_xy"], 14 * n + 2 * l + 2)
                    act_(Yi[n % 2][:, 4:8, :].rearrange("p h t -> p (h t)"), PS[:, 5, :], ACT.Copy).then_inc(S["inv_y1"], 1)
            def evac_t(r, at, bank, done_ps, done_sb):
                t, k0 = at(r)
                act.wait_ge(S[done_ps], r + 1)
                act_(ht3[:, k0:k0 + 4, t * P:(t + 1) * P], PS[:, bank, :].rearrange("p (j s) -> p j s", j=4), ACT.Copy)\
                    .then_inc(S[done_sb], 1)

            evac_t(0, y_round, 4, "yT_ps", "yT_sb")
            evac_t(1, y_round, 5, "yT_ps", "yT_sb")
            chain(3, 1)
            evac_t(2, y_round, 4, "yT_ps", "yT_sb")
            evac_t(3, y_round, 5, "yT_ps", "yT_sb")
            chain(3, 2)
            chain(3, 3)
            act.wait_ge(S["gn_var"], 2)
            act_(GST[:, 1, 16:32], GST[:, 1, 16:32], ACT.Sqrt).then_inc(S["gn_std"], 1)

            for r in range(4, 8):
                evac_t(r, y_round, 6 + r % 2, "yT_ps", "yT_sb")
            for g in range(4):
                act.wait_ge(S["x2_done"], 2 * (g + 1))
                for t in range(NT):
                    cs = slice(g * 512, (g + 1) * 512)
                    if 2 * g + t:
                        act.wait_ge(S["x2_sumsq"], 2 * g + t)
                    act_(junk, x3[:, t, cs], ACT.Square, accum_out=SSQ[:, t, g:g + 1]).then_inc(S["x2_sumsq"], 1)
            act.wait_ge(S["x2_std"], 1)
            act_(ST[:, 22:24], ST[:, 22:24], ACT.Sqrt).then_inc(S["x2_std"], 1)
            act.wait_ge(S["modT_ps"], 2)
            act.wait_ge(S["ada_stored"], 16)
            act_(MODT[0:KT, :], PS[0:KT, 0, 0:P], ACT.Copy).then_inc(S["modT_sb"], 1)
            act.wait_ge(S["modT_sb"], 2)
            act.dma_start(mod_dram[3 * KT:4 * KT, :], MODT[0:KT, :]).then_inc(S["ada_stored"], 16)
            for r in range(8):
                evac_t(r, h_round, 4 + r % 2, "h2T_ps", "h2T_sb")

            def query_out(g, t):
                act_(q3[:, t, g * 512:(g + 1) * 512], PS[:, 2 * (g % 2) + t, :], ACT.Copy).then_inc(S[f"q_done{t}"], 1)

            def query_t_out(g, t):
                act.wait_ge(S[f"qT_ps{t}"], g + 1)
                if g >= 2:
                    act.wait_ge(S[f"sc_ps{t}"], g - 1)
                act_(qt[:, g % 2, t, :, :].rearrange("p j s -> p (j s)"), PS[:, 4 + t, :], ACT.Copy)\
                    .then_inc(S[f"qT_sb{t}"], 1)

            for g in range(4):
                if g == 0:
                    act.wait_ge(S["q00_ps"], 1)
                    query_out(0, 0)
                    query_t_out(0, 0)
                    act.wait_ge(S["w_used"], 64)
                    query_out(0, 1)
                    query_t_out(0, 1)
                else:
                    act.wait_ge(S["w_used"], 60 + 4 * (g + 1))
                    for t in range(NT):
                        query_out(g, t)
                    for t in range(NT):
                        query_t_out(g, t)
                act.wait_ge(S["sc_ps1"], g + 1)
                act_(sc1[:, g * 512:(g + 1) * 512], PS[:, 7, :], ACT.Copy).then_inc(S["sc1_sb"], 1)

            def finish(t):
                for i in range(2):
                    cs = slice(i * GW, (i + 1) * GW)
                    act.wait_ge(S["x_out"], 2 * t + i + 1)
                    act_(h3[:, t, cs], x3[:, t, cs], ACT.Square, accum_out=ST[:, 28 + 2 * t + i:29 + 2 * t + i])\
                        .then_inc(S["out_sumsq"], 1)
                act.wait_ge(S["out_var"], t + 1)
                act_(ST[:, 60 + 2 * t:61 + 2 * t], ST[:, 60 + 2 * t:61 + 2 * t], ACT.Sqrt).then_inc(S["out_std"], 1)

            for t in range(NT):
                act.wait_ge(S["sm_in"], t + 1)
                act_(gate[:, t, :], gate[:, t, :], ACT.Exp).then_inc(S["sm_exp"], 1)
                if t == 1:
                    finish(0)
                act.wait_ge(S["dots_done"], t + 1)
                act_(dots[:, t, :], dots[:, t, :], ACT.Gelu).then_inc(S["act_ready"], 1)
            finish(1)

        @block.vector
        def _(dve):
            v = nc.vector
            own = Steps(dve, S["dve_own"])

            def bc(ap, n):
                return ap.unsqueeze(2).broadcast_to([P, ap.shape[1], n])

            def mean_eps(out_, in_, width, eps, sem_=None):
                own(v.tensor_scalar(out_, in_, 1.0 / width, eps, ALU.mult, ALU.add), sem_)

            dve.wait_ge(S["x_sumsq"], NT)
            mean_eps(ST[:, 2:4], ST[:, 0:2], D, 1e-6, S["x_rstd"])
            dve.wait_ge(S["x_rstd"], 2)
            v.reciprocal(ST[:, 4:6], ST[:, 2:4]).then_inc(S["x_rstd"], 1)
            dve.wait_ge(S["ld_const"], 48)

            def ada_units(b, a, k0, k1):
                for k in range(k0, k1):
                    n = b * KT + k
                    dve.wait_ge(a_slot[n % NA], 16 * (n // NA + 1))
                    w, ck = slot(NW + n % NA), col("c", k, k + 1)
                    if k == 0:
                        v.tensor_scalar(a, w, ck, None, ALU.mult).then_inc(S["ada_used"], 1)
                    else:
                        v.scalar_tensor_tensor(a, w, ck, a, ALU.mult, ALU.add).then_inc(S["ada_used"], 1)
                    dve.wait_ge(S["ada_used"], n + 1)

            def ada(b):
                if b >= 2:
                    dve.wait_ge(S["ada_cols"], b - 1)
                ada_units(b, acc[b % 2], 0, KT)
                dve.sem_inc(S["ada_acc"], 1)

            def mod_cols(b, bank=4):
                dve.wait_ge(S["ada_cols"], b + 1)
                own(v.tensor_tensor(MODR[:, (b - 2) * KT:(b - 1) * KT], PS[:, bank, (b % 2) * KT:(b % 2 + 1) * KT],
                                    col("adab", b * KT, (b + 1) * KT), ALU.add), S["mod_sb"])

            dve.wait_ge(S["silu_c"], 1)
            dve.wait_ge(S["ld_const"], 48)
            own(v.tensor_copy(MASK[:, :, :], mask32))
            v.memset(pt3[:, :, 0:1], 0.0).then_inc(S["pt_zero"], 1)
            ada(0)
            ada(1)
            dve.wait_ge(S["ada_cols"], 2)
            own(v.tensor_tensor(MODC[:, :], PS[:, 4, 0:32], col("adab", 0, 32), ALU.add), S["mod_sb"])
            own(v.scalar_tensor_tensor(MODC[:, 16:32], MODC[:, 16:32], 1.0, col("g1"), ALU.add, ALU.mult))
            dve.wait_ge(S["xT_sb"], 4)
            for k in range(KT):
                own.post(v.tensor_scalar(ht3[:, k, :], ht3[:, k, :], MODC[:, 16 + k:17 + k], MODC[:, k:k + 1], ALU.mult, ALU.add),
                    S["h1_ready"])
            ada(2)
            ada(3)
            mod_cols(2)
            ada_units(4, acc[0], 0, 4)

            dve.wait_ge(S["pt_zero"], 1)
            dve.wait_ge(S["pT_sb"], 7)

            def mix(j0, j1, parts=P, sem_=None, ada4=0, n=0):
                m, cur, prev = m3[0:parts, j0:j1, :], pt3[0:parts, j0:j1, 1:SEQ + 1], pt3[0:parts, j0:j1, 0:SEQ]
                own(v.tensor_tensor(m, prev, cur, ALU.subtract))
                ada_units(4, acc[0], ada4, ada4 + n)
                mu = COL[0:parts, COLS["mu"][0] + j0:COLS["mu"][0] + j1].unsqueeze(2).broadcast_to([parts, j1 - j0, SEQ])
                own(v.tensor_tensor(m, m, mu, ALU.mult))
                ada_units(4, acc[0], ada4 + n, ada4 + 2 * n)
                own(v.tensor_tensor(m, m, cur, ALU.add), sem_)
                ada_units(4, acc[0], ada4 + 2 * n, ada4 + 3 * n)

            mix(NRT - 1, NRT, 32)
            mix(LORA0, NRT - 1, P, S["mix_lora"], 4, 1)
            mix(RT, 2 * RT, P, None, 7, 3)
            dve.sem_inc(S["ada_acc"], 1)
            mod_cols(3)
            own(v.tensor_tensor(kk_ft, mk, bc(col("kk"), SEQ), ALU.mult))
            mix(0, RT)
            mix(2 * RT, 3 * RT)
            own(v.tensor_tensor(bt, kk_ft, kk_ft, ALU.mult), S["mix_kk"])
            mod_cols(4, 2)
            own(v.tensor_scalar(OMK[:, :], col("ka"), -1.0, 1.0, ALU.mult, ALU.add))
            dve.wait_ge(S["z_sb"], RT)
            own(v.tensor_scalar(T1f, T1f, DECAY, None, ALU.mult))
            for j in range(RT):
                for c in range(NT):
                    own.post(v.tensor_tensor_scan(T2[:, j, c * P:(c + 1) * P], ones, T1[:, j, c * P:(c + 1) * P], 0.0,
                                                  ALU.mult, ALU.add))
            own.wait()
            t2c = T2f.rearrange("p (m s) -> p m s", s=P)
            own(v.tensor_copy(MID[:, :, :].rearrange("p j c -> p (j c)"), t2c[:, :, P // 2 - 1]))
            own(v.tensor_tensor(t2c, t2c, bc(MID[:, :, :].rearrange("p j c -> p (j c)"), P), ALU.subtract))
            own(v.tensor_tensor(FC[:, :], T2[:, :, P - 1], MID[:, :, 1], ALU.add))
            own(v.tensor_tensor(T3f, T2f, T1f, ALU.subtract), S["l_ready"])
            dve.wait_ge(S["ss_sb"], 1)
            own(v.tensor_scalar(bt, bt, 1e-12, None, ALU.max))
            own(v.reciprocal(bt, bt))
            own(v.tensor_tensor(kk_ft, kk_ft, bt, ALU.mult))
            dve.wait_ge(S["l_exp"], 1)
            own(v.scalar_tensor_tensor(ar[:, :, 0, :], kk_ft, -1.0, T3, ALU.mult, ALU.mult),
                S["at_done"])
            dve.wait_ge(S["l_exp"], 2)
            own(v.tensor_tensor(ar[:, :, 1, :], mr, T1, ALU.mult))
            dve.wait_ge(S["a_sb"], RT)
            dve.wait_ge(S["k_scale"], RT)
            own(v.tensor_tensor(mk, mk, T3, ALU.mult), S["k2_done"])
            dve.wait_ge(S["l_exp"], 4)
            own(v.tensor_tensor(T1, mr, mk, ALU.mult))
            own(v.tensor_tensor(T1, T1, bc(col("rk"), SEQ), ALU.mult), S["bon_in"])
            own(v.tensor_tensor(a_ft, a_ft, kk_ft, ALU.mult))
            own(v.tensor_tensor(bt, a_ft, T2, ALU.mult))
            own(v.tensor_tensor(mk, mk, T2, ALU.mult), S["wkv_in"])

            def gt2_unit(k):
                dve.wait_ge(S[f"ld_gt2_{GT2_SLOT[k]}"], 16 * GT2_SLOT[:k + 1].count(GT2_SLOT[k]))
                unit_ = slot(8 + GT2_SLOT[k])
                ck = col("c", k, k + 1)
                if k == 0:
                    v.tensor_scalar(gt2acc, unit_, ck, None, ALU.mult).then_inc(S["ada_used"], 1)
                else:
                    v.scalar_tensor_tensor(gt2acc, unit_, ck, gt2acc, ALU.mult, ALU.add).then_inc(S["ada_used"], 1)
                dve.wait_ge(S["ada_used"], (NB - 1) * KT + k + 1)
                if k == KT - 1:
                    dve.sem_inc(S["ada_acc"], 1)

            def gt2_cols():
                dve.wait_ge(S["ada_cols"], NB)
                own(v.tensor_tensor(MODR[:, 3 * KT:4 * KT], PS[:, 7, 256:256 + KT], col("adab", 5 * KT, 6 * KT), ALU.add),
                    S["mod_sb"])

            def gmlp_stats():
                dve.wait_ge(S["ld_small"], 80)
                own(v.memset(wst[64:P, :, 0:64], 0.0))
                dve.wait_ge(S["w_evac"], 22)
                for t in range(NT):
                    for i in range(2):
                        own(v.bn_stats(ST[:, 32 + 6 * i:38 + 6 * i], h3[:, t, GW + 512 * i:GW + 512 * (i + 1)]))
                    own(v.bn_aggr(ST[:, 8 + 2 * t:10 + 2 * t], ST[:, 32:44]))
                    own(v.tensor_scalar(ST[:, 12 + t:13 + t], ST[:, 9 + 2 * t:10 + 2 * t], 1e-5, None, ALU.add))
                dve.sem_inc(S["ln_var"], 1)

            def gmlp_norm(t):
                if t == 0:
                    dve.wait_ge(S["ln_std"], 1)
                    own(v.reciprocal(ST[:, 14:16], ST[:, 12:14]))
                    dve.wait_ge(S["ld_vrow"], 48)
                vv = h3[:, t, GW:2 * GW]
                own(v.tensor_scalar(vv, vv, ST[:, 8 + 2 * t:9 + 2 * t], ST[:, 14 + t:15 + t], ALU.subtract, ALU.mult))
                own(v.tensor_tensor(vv, vv, vgr, ALU.mult))
                own(v.tensor_tensor(vv, vv, vbr, ALU.add), S["vn_ready"])

            def gmlp_gate(i):
                t, hh = i // 2, i % 2
                dve.wait_ge(S["zg_ps"], i + 1)
                for h in range(4 * hh, 4 * hh + 4):
                    u_ = h3[:, t, h * P:(h + 1) * P]
                    last = v.scalar_tensor_tensor(u_, PS[:, 6 + i % 2, (h % 4) * P:(h % 4 + 1) * P],
                                                  col("bs", h, h + 1), u_, ALU.add, ALU.mult)
                    own.post(last, S["zg_sb"] if h % 4 == 3 else None)

            def gmlp_out(part):
                if part == 0:
                    dve.wait_ge(S["ya_sumsq"], NT)
                    mean_eps(ST[:, 18:20], ST[:, 16:18], GW, 1e-6, S["ya_std"])
                else:
                    dve.wait_ge(S["ya_std"], 2)
                    own(v.reciprocal(ST[:, 24:26], ST[:, 18:20]))
                    for t in range(NT):
                        ya = h3[:, t, 0:GW]
                        own(v.scalar_tensor_tensor(ya, ya, ST[:, 24 + t:25 + t], ogr, ALU.mult, ALU.mult), S["ya_done"])

            def group_norm(hf, part):
                fs = slice(hf * 512, (hf + 1) * 512)
                y3, s3 = ytok[:, :, fs], acc[0].rearrange("p (t f) -> p t f", t=NT)[:, :, fs]

                def per_head(ap):
                    return ap.rearrange("p t (h d) -> p t h d", d=HD)

                def stat(i):
                    return GST[:, i, hf * 16:(hf + 1) * 16].rearrange("p (t h) -> p t h", t=NT)

                def over_d(ap):
                    return ap.unsqueeze(3).broadcast_to([P, NT, 8, HD])

                if part == 0:
                    dve.wait_ge(S["y_sb"], 4 * (hf + 1))
                    own(v.tensor_reduce(stat(0), per_head(y3), AX.X, ALU.add))
                    own(v.tensor_scalar(stat(0), stat(0), 1.0 / HD, None, ALU.mult))
                    own(v.tensor_tensor(per_head(y3), per_head(y3), over_d(stat(0)), ALU.subtract))
                if part == 1:
                    own(v.tensor_tensor(s3, y3, y3, ALU.mult))
                    own(v.tensor_reduce(stat(1), per_head(s3), AX.X, ALU.add))
                    mean_eps(stat(1), stat(1), HD, 64e-5, S["gn_var"])
                if part == 2:
                    own(v.tensor_tensor(per_head(s3), per_head(vtok[:, :, fs]),
                                        over_d(BON[:, :, 8 * hf:8 * hf + 8]), ALU.mult))
                    dve.wait_ge(S["gn_std"], hf + 1)
                    own(v.reciprocal(stat(2), stat(1)))
                if part == 3:
                    own(v.tensor_tensor(per_head(y3), per_head(y3), over_d(stat(2)), ALU.mult))
                    dve.wait_ge(S["ld_lnrow"], 32)
                    own(v.tensor_tensor(y3, y3, lngr[:, fs].unsqueeze(1).broadcast_to([P, NT, 512]), ALU.mult))
                if part == 4:
                    own(v.tensor_tensor(y3, y3, lnbr[:, fs].unsqueeze(1).broadcast_to([P, NT, 512]), ALU.add))
                    own(v.tensor_tensor(y3, y3, s3, ALU.add))
                if part == 5:
                    dve.wait_ge(S["gate_ps"], hf + 1)
                    for t in range(NT):
                        own(v.tensor_tensor(h3[:, t, GW + hf * 512:GW + (hf + 1) * 512], y3[:, t, :], PS[:, 6 + t, :],
                                            ALU.mult))
                    dve.sem_inc(S["gate_used"], 1)
                    dve.sem_inc(S["yb_done"], 1)

            fill = {(0, 0): [gmlp_stats], (0, 1): [lambda: gmlp_norm(0)], (0, 2): [lambda: gmlp_norm(1)],
                    (2, 0): [lambda: gmlp_out(1)],
                    (3, 0): [lambda: group_norm(0, 0)], (3, 1): [lambda: group_norm(0, 1)],
                    (3, 3): [lambda: group_norm(0, 2)], (3, 4): [lambda: group_norm(0, 3)],
                    (3, 5): [gt2_cols, lambda: group_norm(0, 4)], (3, 6): [lambda: group_norm(0, 5)]}
            gt2_at = [(0, l) for l in range(3, 7)] + [(n, l) for n in (1, 2) for l in range(1, 6)] + [(3, 1), (3, 2)]
            dve.wait_ge(S["w_used"], 44)
            own.post(v.memset(slot(0), 0.0))
            own.post(v.memset(slot(3), 0.0))
            own.wait()
            strict_incl = MASK[:, LEVELS:LEVELS + 2, :].rearrange("p w t -> p (w t)")
            for n in range(4):
                hf, c = n // 2, n % 2
                for i in range(8):
                    dve.wait_ge(S["score_ps"], 8 * n + i + 1)
                    if n < 2 and i == 4:
                        dve.wait_ge(S["kar_zero"], n + 1)
                    dst = (BAR, KAR)[i // 4][n % 2][:, 2 * (i % 4):2 * (i % 4) + 2, :, :].rearrange("p h w t -> p h (w t)")
                    own.post(v.copy_predicated(dst, strict_incl.unsqueeze(1).broadcast_to([P, 2, 2 * P]),
                                          PS[:, i % 6, :].rearrange("p (h t) -> p h t", h=2)), S["score_sb"])
                if n == 0:
                    dve.wait_ge(S["q_init"], 1)
                for l in range(LEVELS):
                    mask = MASK[:, l, :].unsqueeze(1).broadcast_to([P, 4, P])
                    for g in range(2):
                        dve.wait_ge(S["inv_p"], 14 * n + 2 * l + g + 1)
                        own.post(v.copy_predicated(Q[:, l, 4 * g:4 * g + 4, :], mask,
                                              PS[:, g, :].rearrange("p (h t) -> p h t", h=4)), S["inv_q"])
                    if n == 0 and l >= 3:
                        gmlp_gate(l - 3)
                    if n == 1 and l == 6:
                        gmlp_out(0)
                    if n in (1, 3) and l == 4:
                        dve.wait_ge(S["st_ps"], hf + 1)
                        for par in range(2):
                            pr = slice(HD * par, HD * (par + 1))
                            fc = FC[pr, QUAD * hf:QUAD * (hf + 1)].unsqueeze(2).broadcast_to([HD, QUAD, HD])
                            own.post(v.tensor_tensor(SPR[pr, :, :],
                                                PS[pr, 6, :].rearrange("p (i v) -> p i v", i=QUAD)[:, :, pr], fc, ALU.mult),
                                S["st_sb"])
                    dve.wait_ge(S["inv_xy"], 14 * n + 2 * l + 1)
                    own.post(v.tensor_copy(Yi[n % 2][:, 0:4, :].rearrange("p h t -> p (h t)"), PS[:, 4, :]), S["inv_y0"])
                    if (n, l) in gt2_at:
                        gt2_unit(gt2_at.index((n, l)))
                    for piece in fill.get((n, l), ()):
                        piece()
            for part in range(6):
                group_norm(1, part)

            dve.wait_ge(S["ld_x2"], 16)
            dve.wait_ge(S["ld_rows"], 64)
            own(v.scalar_tensor_tensor(a2b, a2b, 1.0, n2gr, ALU.add, ALU.mult))
            for g in range(4):
                cs = slice(g * 512, (g + 1) * 512)
                dve.wait_ge(S["w_used"], OUT_DONE[g])
                for t in range(NT):
                    own(v.tensor_tensor(xtmp, PS[:, 2 * g + t, :], gt1b[:, cs], ALU.mult))
                    own(v.tensor_tensor(x3[:, t, cs], x3[:, t, cs], xtmp, ALU.add), S["x2_done"])
                if g == 0:
                    dve.wait_ge(S["yT_sb"], 8)
                for t in range(NT):
                    own(v.tensor_tensor(h3[:, t, cs], x3[:, t, cs], a2b[:, cs], ALU.mult))
            dve.wait_ge(S["x2_sumsq"], 8)
            own(v.tensor_reduce(ST[:, 20:22], SSQ[:, :, :], AX.X, ALU.add))
            mean_eps(ST[:, 22:24], ST[:, 20:22], D, 1e-6, S["x2_std"])
            dve.wait_ge(S["x2_std"], 2)
            own(v.reciprocal(ST[:, 26:28], ST[:, 22:24]))
            for t in range(NT):
                for i in range(2):
                    cs = slice(i * GW, (i + 1) * GW)
                    own.post(v.scalar_tensor_tensor(h3[:, t, cs], h3[:, t, cs], ST[:, 26 + t:27 + t], sh2b[:, cs],
                                               ALU.mult, ALU.add), S["h2_done"])

            def top16(rows):
                for values, val, idx, work in rows:
                    own.post(v.max(val[:, 0:8], values))
                own.wait()
                for values, val, idx, work in rows:
                    own.post(v.max_index(idx[:, 0:8], val[:, 0:8], values))
                    own.post(v.match_replace(work, val[:, 0:8], values, BIG))
                own.wait()
                for values, val, idx, work in rows:
                    own.post(v.max(val[:, 8:16], work))
                own.wait()
                for values, val, idx, work in rows:
                    own.post(v.max_index(idx[:, 8:16], val[:, 8:16], work))
                own.wait()

            iota = col("iota").unsqueeze(1).broadcast_to([P, GS, TOPK])

            def select(g, t):
                src = PS[:, 6, :] if t == 0 else sc1[:, g * 512:(g + 1) * 512]
                top16([(src[:, j * P:(j + 1) * P], tops[:, j, :], topi[:, j, :], onehot[0][:, j * P:(j + 1) * P])
                       for j in range(4)])
                if t == 0:
                    dve.sem_inc(S["sc_used"], 1)
                tp = tops.rearrange("p (h w) k -> p h w k", w=2)
                own.post(v.tensor_copy(topf, topi.rearrange("p g k -> p (g k)")))
                tf = topf.rearrange("p (h w k) -> p h w k", h=2, w=2)
                own(v.tensor_tensor(cand, tp[:, :, 0, :].unsqueeze(3).broadcast_to([P, 2, TOPK, TOPK]),
                                    tp[:, :, 1, :].unsqueeze(2).broadcast_to([P, 2, TOPK, TOPK]), ALU.add))
                top16([(cand[:, h, :, :].rearrange("p a b -> p (a b)"), sfin[:, t, g * GS + h * TOPK:g * GS + (h + 1) * TOPK],
                        pos[:, h * TOPK:(h + 1) * TOPK], onehot[0][:, h * 256:(h + 1) * 256]) for h in range(2)])
                own.post(v.tensor_scalar(posp[:, 0, :], pos, 4, None, ALU.logical_shift_right))
                own(v.tensor_scalar(posp[:, 1, :], pos, 15, None, ALU.bitwise_and))
                own(v.tensor_copy(posf, posp))
                for w in range(2):
                    own.post(v.tensor_tensor(onehot[w].rearrange("p (s b) -> p s b", b=TOPK), iota, bc(posf[:, w, :], TOPK),
                                             ALU.is_equal))
                own.wait()
                for w in range(2):
                    oh = onehot[w].rearrange("p (h a b) -> p h a b", h=2, a=TOPK)
                    own.post(v.tensor_tensor(oh, oh, tf[:, :, w, :].unsqueeze(2).broadcast_to([P, 2, TOPK, TOPK]), ALU.mult))
                own.wait()
                for w in range(2):
                    own.post(v.tensor_reduce(isel[:, w, :], onehot[w].rearrange("p (s b) -> p s b", b=TOPK), AX.X, ALU.add))
                own.wait()
                own(v.scalar_tensor_tensor(isel[:, 0, :], isel[:, 0, :], float(NK), isel[:, 1, :], ALU.mult, ALU.add))
                own(v.tensor_copy(eidx[:, t, g * GS:(g + 1) * GS], isel[:, 0, :]))
                dve.sem_inc(S[f"idx{t}_ready"], 2)

            def softmax_in(t):
                sh = sfin[:, t, :].rearrange("p (h k) -> p h k", h=NH)
                gt = gate[:, t, :].rearrange("p (h k) -> p h k", h=NH)
                own(v.tensor_tensor(gt, sh, bc(sh[:, :, 0], TOPK), ALU.subtract), S["sm_in"])

            def softmax_out(t):
                gt = gate[:, t, :].rearrange("p (h k) -> p h k", h=NH)
                dve.wait_ge(S["sm_exp"], t + 1)
                own(v.tensor_reduce(ST[:, 44:52], gt, AX.X, ALU.add))
                own(v.reciprocal(ST[:, 52:60], ST[:, 44:52]))
                own(v.tensor_tensor(gt, gt, bc(ST[:, 52:60], TOPK), ALU.mult))

            def experts(ps, i0, i1):
                t = ps // 2
                with dve.Fori(i0, i1) as i:
                    for s in range(NW):
                        dve.wait_ge(g_slot[s], i * 16 + 16 * (16 * ps + 1))
                        if ps % 2 == 0:
                            v.scalar_tensor_tensor(gslot[s], gslot[s], 1.0, h3[:, t, :], ALU.mult, ALU.mult,
                                                   accum_out=dots[:, t, ds(i * NW + s, 1)]).then_inc(S["used"], 1)
                        else:
                            v.scalar_tensor_tensor(acc[t], gslot[s], dots[:, t, ds(i * NW + s, 1)], acc[t],
                                                   ALU.mult, ALU.add).then_inc(S["used"], 1)
                            dve.wait_ge(S["used"], i * NW + (NW + 128 * ps + s + 1))

            def weights(t):
                dve.wait_ge(S["used"], NW + NSEL * (2 * t + 1))
                dve.sem_inc(S["dots_done"], 1)
                dve.wait_ge(S["act_ready"], t + 1)
                own(v.tensor_tensor(dots[:, t, :], dots[:, t, :], gate[:, t, :], ALU.mult))
                own(v.memset(acc[t], 0.0))

            def finish(t):
                dve.wait_ge(S["ld_fin"], 32)
                for i in range(2):
                    cs = slice(i * GW, (i + 1) * GW)
                    own(v.tensor_tensor(acc[t][:, cs], acc[t][:, cs], gt2b[:, cs], ALU.mult))
                    own(v.tensor_tensor(x3[:, t, cs], x3[:, t, cs], acc[t][:, cs], ALU.add), S["x_out"])
                dve.wait_ge(S["out_sumsq"], 2 * (t + 1))
                var, rstd = ST[:, 60 + 2 * t:61 + 2 * t], ST[:, 61 + 2 * t:62 + 2 * t]
                own(v.tensor_tensor(var, ST[:, 28 + 2 * t:29 + 2 * t], ST[:, 29 + 2 * t:30 + 2 * t], ALU.add))
                mean_eps(var, var, D, 1e-6, S["out_var"])
                dve.wait_ge(S["out_std"], t + 1)
                own(v.reciprocal(rstd, var))
                for i in range(2):
                    cs = slice(i * GW, (i + 1) * GW)
                    own.post(v.scalar_tensor_tensor(h3[:, t, cs], x3[:, t, cs], rstd, fgr[:, cs], ALU.mult, ALU.mult),
                        S["out_ready"])

            dve.wait_ge(S["sc_ps0"], 1)
            select(0, 0)
            dve.wait_ge(S["w_used"], 64)
            dve.sem_inc(S["used"], NW)
            experts(0, 0, 1)
            dve.wait_ge(S["sc_ps0"], 2)
            select(1, 0)
            experts(0, 1, 2)
            dve.wait_ge(S["sc_ps0"], 3)
            select(2, 0)
            experts(0, 2, 5)
            dve.wait_ge(S["sc_ps0"], 4)
            select(3, 0)
            softmax_in(0)
            experts(0, 5, 6)
            softmax_out(0)
            experts(0, 6, 10)
            dve.wait_ge(S["sc1_sb"], 4)
            select(0, 1)
            experts(0, 10, 15)
            select(1, 1)
            experts(0, 15, 16)
            weights(0)
            experts(1, 0, 5)
            select(2, 1)
            experts(1, 5, 10)
            select(3, 1)
            softmax_in(1)
            experts(1, 10, 16)
            experts(2, 0, 8)
            finish(0)
            experts(2, 8, 16)
            softmax_out(1)
            weights(1)
            experts(3, 0, 16)
            finish(1)


_COLS = [("c", 16), ("ada_b", 96), ("norm1_g", 16), ("rwkv_mu", 27), ("rwkv_w0", 8), ("rwkv_a0", 8),
         ("rwkv_kk", 8), ("rwkv_ka", 8), ("rwkv_rk", 8), ("gmlp_bs", 8)]


def kernel(**inputs):
    import concourse.bacc as _bacc
    from concourse.bass_utils import run_bass_kernel_spmd as _run

    a = {k: np.asarray(val) for k, val in inputs.items()}
    f = np.float32

    parts = []
    for name, w in _COLS:
        flat = a[name].reshape(-1)[:w * P]
        pad = np.zeros(w * P - flat.size, f)
        parts.append(np.concatenate([flat, pad]).reshape(w, P).T)
    parts.append(np.tile(np.arange(16, dtype=f), (P, 1)))
    i, l = np.arange(P)[:, None], np.arange(P)[None, :]
    mats = np.stack([(i == l), np.ones((P, P), bool), (i // HD == l // HD)], 1).astype(f)
    masks = [((i // (2 * m) == l // (2 * m)) & (i % (2 * m) >= m) & (l % (2 * m) < m)) for m in (1, 2, 4, 8, 16, 32, 64)]
    masks = np.stack(masks + [i < l, i <= l], 1).astype(np.uint32)

    data = {
        "x": a["x"][0], "ada_w": a["ada_w"][0],
        "w_in": a["w_in"][0], "ws_t": a["gmlp_ws"][0].transpose(2, 0, 1), "w2": a["rwkv_w2"][0],
        "a2": a["rwkv_a2"][0], "g2": a["rwkv_g2"][0], "w_out": a["w_out"][0], "wq": a["peer_wq"][0],
        "keys_t": a["peer_keys"][0].reshape(2 * NH, NK, P).transpose(2, 0, 1), "peer_u": a["peer_u"][0],
        "peer_v": a["peer_v"][0], "cols": np.concatenate(parts, 1), "mats": mats, "masks": masks,
        "vg": a["gmlp_v_g"][0], "vb": a["gmlp_v_b"][0], "og": a["gmlp_out_g"][0], "lng": a["rwkv_ln_g"][0],
        "lnb": a["rwkv_ln_b"][0], "n2g": a["norm2_g"][0], "fg": a["final_g"],
    }
    nc = _bacc.Bacc("TRN2", target_bir_lowering=False, num_devices=1, dynamic_dma_scratch_size=8192)
    arrays, args = {}, []
    for name, arr in data.items():
        arr = np.ascontiguousarray(arr)
        arrays[f"in_{name}"] = arr
        args.append(nc.dram_tensor(f"in_{name}", arr.shape, mybir.dt.from_np(arr.dtype), kind="ExternalInput").ap())
    args.append(nc.dram_tensor("out", (SEQ, D), mybir.dt.float32, kind="ExternalOutput").ap())
    build(nc, *args)
    r = _run(nc, [arrays], core_ids=[0])
    return r.results[0]["out"].reshape(1, SEQ, D)
```
